# Optimizing a Trainium2 kernel written in Bass

```python
import math
import jax, jax.numpy as jnp
from jax import lax
import numpy as np
import jax
import jax.numpy as jnp

D_MODEL = 1024
BATCH = 1
SEQ = 256
DEPTH = 2

N_MIXERS = 3
MEM_LEN = 256
DA_HEADS = 8
DA_HEAD_DIM = 64
DA_QBLOCK = 128
ROPE_THETA = 10000.0
POOL_WINDOWS = (2, 4, 8, 16)
POOL_GROUPS = len(POOL_WINDOWS)
POOL_GROUP_DIM = D_MODEL // POOL_GROUPS
RET_HEADS = 4
RET_QK_DIM = D_MODEL // RET_HEADS
RET_V_DIM = 2 * RET_QK_DIM
RET_CHUNK = 128
XA_HEADS = 4
XA_HEAD_DIM = D_MODEL // XA_HEADS
D_FF = 2816
DEEPNORM_ALPHA = (2 * DEPTH) ** 0.25
DEEPNORM_BETA = (8 * DEPTH) ** -0.25
LN_EPS = 1e-5

N_DA = len(range(0, DEPTH, N_MIXERS))
N_POOL = len(range(1, DEPTH, N_MIXERS))
N_RET = len(range(2, DEPTH, N_MIXERS))


def layer_norm(x, g, b):
    xf = x.astype(jnp.float32)
    mu = jnp.mean(xf, axis=-1, keepdims=True)
    var = jnp.mean(jnp.square(xf - mu), axis=-1, keepdims=True)
    y = (xf - mu) * lax.rsqrt(var + LN_EPS) * g.astype(jnp.float32) + b.astype(jnp.float32)
    return y.astype(x.dtype)

def rope(x, cos, sin):
    half = x.shape[-1] // 2
    xf = x.astype(jnp.float32)
    x1, x2 = xf[..., :half], xf[..., half:]
    return jnp.concatenate([x1 * cos - x2 * sin, x2 * cos + x1 * sin], axis=-1).astype(x.dtype)

def swiglu_ffn(x, w_in, w_out):
    h = x @ w_in
    g, u = jnp.split(h, 2, axis=-1)
    return (jax.nn.silu(g) * u) @ w_out

def diff_attention(x, w_qkv, w_o, lam_q, lam_k, subln_g, cos, sin, lam_init):
    B, S, _ = x.shape
    H, dk = DA_HEADS, DA_HEAD_DIM
    q, k, v = jnp.split(x @ w_qkv, 3, axis=-1)
    q = q.reshape(B, S, H, 2, dk)
    k = k.reshape(B, S, H, 2, dk)
    v = v.reshape(B, S, H, 2 * dk)
    c5, s5 = cos[:, :, None, None, :], sin[:, :, None, None, :]
    q = rope(q, c5, s5)
    k = rope(k, c5, s5)
    lq = lam_q.astype(jnp.float32)
    lk = lam_k.astype(jnp.float32)
    lam = jnp.exp(jnp.sum(lq[0] * lk[0])) - jnp.exp(jnp.sum(lq[1] * lk[1])) + lam_init
    scale = dk ** -0.5
    nb = S // DA_QBLOCK
    qb = q.reshape(B, nb, DA_QBLOCK, H, 2, dk).transpose(1, 0, 2, 3, 4, 5)
    kpos = jnp.arange(S)

    def block(args):
        qblk, i = args
        s = jnp.einsum('bqhcd,bkhcd->bhcqk', qblk, k).astype(jnp.float32) * scale
        qpos = i * DA_QBLOCK + jnp.arange(DA_QBLOCK)
        mask = kpos[None, :] <= qpos[:, None]
        s = jnp.where(mask, s, jnp.finfo(jnp.float32).min)
        p = jax.nn.softmax(s, axis=-1)
        a = p[:, :, 0] - lam * p[:, :, 1]
        return jnp.einsum('bhqk,bkhe->bqhe', a.astype(v.dtype), v)

    o = lax.map(block, (qb, jnp.arange(nb)))
    o = o.transpose(1, 0, 2, 3, 4).reshape(B, S, H, 2 * dk).astype(jnp.float32)
    o = o * lax.rsqrt(jnp.mean(jnp.square(o), axis=-1, keepdims=True) + LN_EPS)
    o = o * subln_g.astype(jnp.float32) * (1.0 - lam_init)
    return o.reshape(B, S, H * 2 * dk).astype(x.dtype) @ w_o

def pool_mixer(x, w_grp, b_grp, scale):
    B, S, D = x.shape
    xg = x.reshape(B, S, POOL_GROUPS, POOL_GROUP_DIM).astype(jnp.float32)
    cs = jnp.cumsum(xg, axis=1)
    t = jnp.arange(S)
    pooled = []
    for g, w in enumerate(POOL_WINDOWS):
        c = cs[:, :, g]
        prev = jnp.pad(c, ((0, 0), (w, 0), (0, 0)))[:, :S]
        cnt = jnp.minimum(t + 1, w).astype(jnp.float32)[None, :, None]
        pooled.append((c - prev) / cnt)
    pooled = jnp.stack(pooled, axis=2) - xg
    y = jnp.einsum('bsgc,gcd->bsgd', pooled.astype(x.dtype), w_grp) + b_grp
    return y.reshape(B, S, D) * scale

def retention(x, w_qkvg, w_o, cos, sin):
    B, S, _ = x.shape
    H, dk, dv, C = RET_HEADS, RET_QK_DIM, RET_V_DIM, RET_CHUNK
    proj = x @ w_qkvg
    q, k, v, g = jnp.split(proj, [H * dk, 2 * H * dk, 2 * H * dk + H * dv], axis=-1)
    c4, s4 = cos[:, :, None, :], sin[:, :, None, :]
    q = rope(q.reshape(B, S, H, dk), c4, s4).astype(jnp.float32)
    k = rope(k.reshape(B, S, H, dk), c4, s4).astype(jnp.float32) * (dk ** -0.5)
    v = v.reshape(B, S, H, dv).astype(jnp.float32)
    log_gamma = jnp.log(1.0 - jnp.exp2(-5.0 - jnp.arange(H, dtype=jnp.float32)))
    idx = jnp.arange(C, dtype=jnp.float32)
    rel = idx[:, None] - idx[None, :]
    d_intra = jnp.where(rel[None] >= 0,
                        jnp.exp(jnp.maximum(rel, 0.0)[None] * log_gamma[:, None, None]), 0.0)
    q_decay = jnp.exp((idx[:, None] + 1.0) * log_gamma[None, :])
    k_decay = jnp.exp((C - 1.0 - idx[:, None]) * log_gamma[None, :])
    chunk_decay = jnp.exp(C * log_gamma)
    nc = S // C

    def to_chunks(a):
        return a.reshape(B, nc, C, H, a.shape[-1]).transpose(1, 0, 2, 3, 4)

    def step(R, inp):
        qc, kc, vc = inp
        att = jnp.einsum('bihd,bjhd->bhij', qc, kc) * d_intra[None]
        inner = jnp.einsum('bhij,bjhe->bihe', att, vc)
        cross = jnp.einsum('bihd,bhde->bihe', qc, R) * q_decay[None, :, :, None]
        R = R * chunk_decay[None, :, None, None] + jnp.einsum(
            'bjhd,bjhe->bhde', kc * k_decay[None, :, :, None], vc)
        return R, inner + cross

    R0 = jnp.zeros((B, H, dk, dv), jnp.float32)
    _, o = lax.scan(step, R0, (to_chunks(q), to_chunks(k), to_chunks(v)))
    o = o.transpose(1, 0, 2, 3, 4).reshape(B, S, H, dv)
    mu = jnp.mean(o, axis=-1, keepdims=True)
    var = jnp.mean(jnp.square(o - mu), axis=-1, keepdims=True)
    o = ((o - mu) * lax.rsqrt(var + LN_EPS)).reshape(B, S, H * dv).astype(x.dtype)
    return (jax.nn.silu(g) * o) @ w_o

def memory_cross_attention(x, mem, wq, wkv, wo):
    B, S, _ = x.shape
    M = mem.shape[1]
    q = (x @ wq).reshape(B, S, XA_HEADS, XA_HEAD_DIM)
    k, v = jnp.split(mem @ wkv, 2, axis=-1)
    k = k.reshape(B, M, XA_HEADS, XA_HEAD_DIM)
    v = v.reshape(B, M, XA_HEADS, XA_HEAD_DIM)
    s = jnp.einsum('bshd,bmhd->bhsm', q, k).astype(jnp.float32) * (XA_HEAD_DIM ** -0.5)
    p = jax.nn.softmax(s, axis=-1).astype(v.dtype)
    o = jnp.einsum('bhsm,bmhd->bshd', p, v).reshape(B, S, D_MODEL)
    return o @ wo

def first_inputs(seed: int = 0) -> dict:
    key = jax.random.key(seed)
    ks = jax.random.split(key, 24)
    f32 = jnp.float32
    D, F = D_MODEL, D_FF
    nrm = lambda k, shape, std: jax.random.normal(k, shape, f32) * std
    x = nrm(ks[0], (BATCH, SEQ, D), 1.0)
    mem = nrm(ks[1], (BATCH, MEM_LEN, D), 1.0)
    offset = jax.random.randint(ks[2], (BATCH, 1), 0, 4096, dtype=jnp.int32)
    positions = (jnp.arange(SEQ, dtype=jnp.int32)[None, :] + offset).astype(jnp.int32)
    ffn_w_in = nrm(ks[3], (DEPTH, 2, D, 2 * F), D ** -0.5)
    ffn_w_out = nrm(ks[4], (DEPTH, 2, F, D), F ** -0.5 * DEEPNORM_BETA)
    ln_g = 1.0 + nrm(ks[5], (DEPTH, 4, D), 0.02)
    ln_b = nrm(ks[6], (DEPTH, 4, D), 0.02)
    da_w_qkv = nrm(ks[7], (N_DA, D, 3 * DA_HEADS * 2 * DA_HEAD_DIM), D ** -0.5)
    da_w_o = nrm(ks[8], (N_DA, DA_HEADS * 2 * DA_HEAD_DIM, D),
                 (DA_HEADS * 2 * DA_HEAD_DIM) ** -0.5 * DEEPNORM_BETA)
    da_lam_q = nrm(ks[9], (N_DA, 2, DA_HEAD_DIM), 0.1)
    da_lam_k = nrm(ks[10], (N_DA, 2, DA_HEAD_DIM), 0.1)
    da_subln_g = 1.0 + nrm(ks[11], (N_DA, 2 * DA_HEAD_DIM), 0.02)
    pool_w = nrm(ks[12], (N_POOL, POOL_GROUPS, POOL_GROUP_DIM, POOL_GROUP_DIM),
                 POOL_GROUP_DIM ** -0.5 * DEEPNORM_BETA)
    pool_b = nrm(ks[13], (N_POOL, POOL_GROUPS, POOL_GROUP_DIM), 0.02)
    pool_scale = 1.0 + nrm(ks[14], (N_POOL, D), 0.02)
    ret_w_qkvg = nrm(ks[15], (N_RET, D, 2 * RET_HEADS * RET_QK_DIM + 2 * RET_HEADS * RET_V_DIM),
                     D ** -0.5)
    ret_w_o = nrm(ks[16], (N_RET, RET_HEADS * RET_V_DIM, D),
                  (RET_HEADS * RET_V_DIM) ** -0.5 * DEEPNORM_BETA)
    xa_wq = nrm(ks[17], (DEPTH, D, D), D ** -0.5)
    xa_wkv = nrm(ks[18], (DEPTH, D, 2 * D), D ** -0.5)
    xa_wo = nrm(ks[19], (DEPTH, D, D), D ** -0.5 * DEEPNORM_BETA)
    return {"x": x, "mem": mem, "positions": positions,
            "ffn_w_in": ffn_w_in, "ffn_w_out": ffn_w_out, "ln_g": ln_g, "ln_b": ln_b,
            "da_w_qkv": da_w_qkv, "da_w_o": da_w_o, "da_lam_q": da_lam_q,
            "da_lam_k": da_lam_k, "da_subln_g": da_subln_g,
            "pool_w": pool_w, "pool_b": pool_b, "pool_scale": pool_scale,
            "ret_w_qkvg": ret_w_qkvg, "ret_w_o": ret_w_o,
            "xa_wq": xa_wq, "xa_wkv": xa_wkv, "xa_wo": xa_wo}

def first_block(x, mem, positions, ffn_w_in, ffn_w_out, ln_g, ln_b,
              da_w_qkv, da_w_o, da_lam_q, da_lam_k, da_subln_g,
              pool_w, pool_b, pool_scale, ret_w_qkvg, ret_w_o,
              xa_wq, xa_wkv, xa_wo):
    pos = positions.astype(jnp.float32)[..., None]
    da_inv = 1.0 / (ROPE_THETA ** (jnp.arange(0, DA_HEAD_DIM, 2, dtype=jnp.float32) / DA_HEAD_DIM))
    da_ang = pos * da_inv[None, None, :]
    da_cos, da_sin = jnp.cos(da_ang), jnp.sin(da_ang)
    ret_inv = 1.0 / (ROPE_THETA ** jnp.linspace(0.0, 1.0, RET_QK_DIM // 2, dtype=jnp.float32))
    ret_ang = pos * ret_inv[None, None, :]
    ret_cos, ret_sin = jnp.cos(ret_ang), jnp.sin(ret_ang)
    a = DEEPNORM_ALPHA
    for i in range(DEPTH):
        m, j = i % N_MIXERS, i // N_MIXERS
        x = layer_norm(a * x + 0.5 * swiglu_ffn(x, ffn_w_in[i, 0], ffn_w_out[i, 0]),
                       ln_g[i, 0], ln_b[i, 0])
        if m == 0:
            lam_init = 0.8 - 0.6 * math.exp(-0.3 * i)
            h = diff_attention(x, da_w_qkv[j], da_w_o[j], da_lam_q[j], da_lam_k[j],
                               da_subln_g[j], da_cos, da_sin, lam_init)
        elif m == 1:
            h = pool_mixer(x, pool_w[j], pool_b[j], pool_scale[j])
        else:
            h = retention(x, ret_w_qkvg[j], ret_w_o[j], ret_cos, ret_sin)
        x = layer_norm(a * x + h, ln_g[i, 1], ln_b[i, 1])
        x = layer_norm(a * x + memory_cross_attention(x, mem, xa_wq[i], xa_wkv[i], xa_wo[i]),
                       ln_g[i, 2], ln_b[i, 2])
        x = layer_norm(a * x + 0.5 * swiglu_ffn(x, ffn_w_in[i, 1], ffn_w_out[i, 1]),
                       ln_g[i, 3], ln_b[i, 3])
    return x


GRID_W = 64
CTX_LEN = 256
N_MIXERS_2 = 4
EPS = 1e-6
NEG_INF = -1e30
F32 = jnp.float32

HY_ORDER = 2
HY_SHORT = 3
HY_EMB = 33
HY_FFN = 64
HY_FAST_DECAY = 0.3
HY_SLOW_DECAY = 1.5
HY_TARGET = 1e-2
HY_SHIFT = 0.05

SW_HQ = 16
SW_HKV = 4
SW_REP = SW_HQ // SW_HKV
SW_HD = 64
SW_WINDOW = 128
SW_BLOCK = SW_WINDOW
ROPE_BASE = 10000.0

GD_H = 8
GD_DK = 128
GD_DV = 128
GD_QK = GD_H * GD_DK
GD_V = GD_H * GD_DV
GD_CONV = 3
GD_CHUNK = 64

HG_DK = 128
HG_H = D_MODEL // HG_DK
HG_DV = D_MODEL // HG_H
HG_CHUNK = 64

N_EXPERTS = 16
EXPERT_FF = 1024
EC_CAPACITY = 2


def rms_norm(x, w):
    xf = x.astype(F32)
    y = xf * lax.rsqrt(jnp.mean(xf * xf, axis=-1, keepdims=True) + EPS)
    return (y * w.astype(F32)).astype(x.dtype)

def l2_normalize(x):
    xf = x.astype(F32)
    return xf * lax.rsqrt(jnp.sum(xf * xf, axis=-1, keepdims=True) + EPS)

def orient(t, direction):
    return jnp.flip(t, axis=1) if direction == 1 else t

def centred_depthwise_conv(x, w, b=None):
    K, C = w.shape
    y = lax.conv_general_dilated(x, w[:, None, :].astype(x.dtype), window_strides=(1,),
                                 padding=[(K // 2, K // 2)],
                                 dimension_numbers=('NWC', 'WIO', 'NWC'), feature_group_count=C)
    return y if b is None else y + b

def hyena_positional_features(L):
    t = jnp.linspace(0.0, 1.0, L, dtype=F32)[:, None]
    bands = (HY_EMB - 1) // 2
    w = 2.0 * math.pi * jnp.arange(L, dtype=F32)[:, None] / L
    f = jnp.linspace(1e-4, bands - 1, bands, dtype=F32)[None, :]
    z = jnp.concatenate([t, jnp.cos(f * w), -jnp.sin(f * w)], axis=-1)
    return t, z

def hyena_filters(L, w1, b1, w2, b2, w3, freq):
    t, z = hyena_positional_features(L)
    h = jnp.sin(freq[0].astype(F32) * (z @ w1.astype(F32) + b1.astype(F32)))
    h = jnp.sin(freq[1].astype(F32) * (h @ w2.astype(F32) + b2.astype(F32)))
    h = (h @ w3.astype(F32)).reshape(L, HY_ORDER, 2, D_MODEL)
    max_decay = math.log(HY_TARGET) / HY_FAST_DECAY
    min_decay = math.log(HY_TARGET) / HY_SLOW_DECAY
    deltas = jnp.abs(jnp.linspace(min_decay, max_decay, D_MODEL, dtype=F32))
    window = jnp.exp(-t * deltas) + HY_SHIFT
    return h * window[:, None, None, :]

def two_sided_fft_conv(u, h_fwd, h_bwd, bias):
    L = u.shape[1]
    kern = jnp.concatenate([h_fwd, jnp.zeros((1, h_fwd.shape[1]), F32), h_bwd[:0:-1]], axis=0)
    uf = u.astype(F32)
    spec = jnp.fft.rfft(uf, n=2 * L, axis=1) * jnp.fft.rfft(kern, n=2 * L, axis=0)[None]
    y = jnp.fft.irfft(spec, n=2 * L, axis=1)[:, :L]
    return (y + uf * bias.astype(F32)).astype(u.dtype)

def hyena_mixer(h, w_in, b_in, short_w, short_b, w1, b1, w2, b2, w3, freq, filt_bias, w_out, b_out):
    L = h.shape[1]
    u = centred_depthwise_conv(h @ w_in + b_in, short_w, short_b)
    v, x1, x2 = jnp.split(u, 3, axis=-1)
    filt = hyena_filters(L, w1, b1, w2, b2, w3, freq)
    z = x1 * two_sided_fft_conv(v, filt[:, 0, 0], filt[:, 0, 1], filt_bias[0])
    z = x2 * two_sided_fft_conv(z, filt[:, 1, 0], filt[:, 1, 1], filt_bias[1])
    return z @ w_out + b_out

def axial_rope_tables(L):
    rows = L // GRID_W
    row = jnp.repeat(jnp.arange(rows, dtype=F32), GRID_W)
    col = jnp.tile(jnp.arange(GRID_W, dtype=F32), rows)
    nf = SW_HD // 4
    inv = ROPE_BASE ** (-jnp.arange(nf, dtype=F32) / nf)
    ang = jnp.concatenate([row[:, None] * inv, col[:, None] * inv], axis=-1)
    return jnp.cos(ang), jnp.sin(ang)

def apply_rope(x, cos, sin):
    shape = (1, cos.shape[0]) + (1,) * (x.ndim - 3) + (cos.shape[1],)
    cos = cos.reshape(shape).astype(x.dtype)
    sin = sin.reshape(shape).astype(x.dtype)
    x1, x2 = jnp.split(x, 2, axis=-1)
    return jnp.concatenate([x1 * cos - x2 * sin, x2 * cos + x1 * sin], axis=-1)

def sink_softmax(s, sink):
    sk = jnp.broadcast_to(sink.astype(F32).reshape(SW_HKV, SW_REP, 1, 1), s.shape[:-1] + (1,))
    return jax.nn.softmax(jnp.concatenate([s, sk], axis=-1), axis=-1)[..., :-1]

def swa_mixer(h_ctx, h_lat, w_in, sink, w_out, with_ctx_out):
    B, L, _ = h_lat.shape
    scale = SW_HD ** -0.5

    def project(h):
        n = h.shape[1]
        u = h @ w_in
        q = u[..., :SW_HQ * SW_HD].reshape(B, n, SW_HKV, SW_REP, SW_HD)
        k = u[..., SW_HQ * SW_HD:(SW_HQ + SW_HKV) * SW_HD].reshape(B, n, SW_HKV, SW_HD)
        v = u[..., (SW_HQ + SW_HKV) * SW_HD:].reshape(B, n, SW_HKV, SW_HD)
        return q, k, v

    q_c, k_c, v_c = project(h_ctx)
    q_l, k_l, v_l = project(h_lat)
    cos, sin = axial_rope_tables(L)
    q_l = apply_rope(q_l, cos, sin)
    k_l = apply_rope(k_l, cos, sin)
    n_ctx = k_c.shape[1]
    nb = L // SW_BLOCK

    def band(t):
        tp = jnp.pad(t, ((0, 0), (SW_BLOCK, SW_BLOCK), (0, 0), (0, 0)))
        tp = tp.reshape(B, nb + 2, SW_BLOCK, SW_HKV, SW_HD)
        return jnp.concatenate([tp[:, :-2], tp[:, 1:-1], tp[:, 2:]], axis=2).swapaxes(0, 1)

    blk = jnp.arange(nb)[:, None, None]
    qpos = blk * SW_BLOCK + jnp.arange(SW_BLOCK)[None, :, None]
    kpos = (blk - 1) * SW_BLOCK + jnp.arange(3 * SW_BLOCK)[None, None, :]
    band_mask = (jnp.abs(qpos - kpos) <= SW_WINDOW) & (kpos >= 0) & (kpos < L)
    q_blocks = q_l.reshape(B, nb, SW_BLOCK, SW_HKV, SW_REP, SW_HD).swapaxes(0, 1)

    def block_attention(xs):
        q_b, k_b, v_b, m_b = xs
        s_ctx = jnp.einsum('bqgrd,bkgd->bgrqk', q_b, k_c).astype(F32) * scale
        s_loc = jnp.einsum('bqgrd,bkgd->bgrqk', q_b, k_b).astype(F32) * scale
        s_loc = jnp.where(m_b, s_loc, NEG_INF)
        p = sink_softmax(jnp.concatenate([s_ctx, s_loc], axis=-1), sink).astype(v_b.dtype)
        return (jnp.einsum('bgrqk,bkgd->bqgrd', p[..., :n_ctx], v_c)
                + jnp.einsum('bgrqk,bkgd->bqgrd', p[..., n_ctx:], v_b))

    o_l = lax.map(block_attention, (q_blocks, band(k_l), band(v_l), band_mask))
    y_lat = o_l.swapaxes(0, 1).reshape(B, L, SW_HQ * SW_HD) @ w_out
    y_ctx = None
    if with_ctx_out:
        s = jnp.einsum('bqgrd,bkgd->bgrqk', q_c, k_c).astype(F32) * scale
        p = sink_softmax(s, sink).astype(v_c.dtype)
        y_ctx = jnp.einsum('bgrqk,bkgd->bqgrd', p, v_c).reshape(B, n_ctx, SW_HQ * SW_HD) @ w_out
    return y_ctx, y_lat

def to_chunks(t, size):
    B, L, H = t.shape[:3]
    t = t.reshape((B, L // size, size, H) + t.shape[3:])
    return jnp.moveaxis(t, (1, 3), (0, 2))

def from_chunks(t):
    t = jnp.moveaxis(t, (0, 2), (1, 3))
    return t.reshape((t.shape[0], t.shape[1] * t.shape[2]) + t.shape[3:])

def chunk_gated_delta(q, k, v, g, beta, S0):
    dv = v.shape[-1]
    C = GD_CHUNK
    qc, kc, vc = to_chunks(q, C), to_chunks(k, C), to_chunks(v, C)
    gc, bc = to_chunks(g, C), to_chunks(beta, C)
    G = jnp.cumsum(gc, axis=-1)
    incl = jnp.tril(jnp.ones((C, C), bool))
    strict = jnp.tril(jnp.ones((C, C), bool), -1)
    decay = jnp.exp(jnp.where(incl, G[..., :, None] - G[..., None, :], -jnp.inf))
    kb = kc * bc[..., None]
    A = jnp.where(strict, jnp.einsum('nbhid,nbhjd->nbhij', kb, kc) * decay, 0.0)
    rhs = jnp.concatenate([vc * bc[..., None], kb * jnp.exp(G)[..., None]], axis=-1)
    uw = lax.linalg.triangular_solve(jnp.eye(C, dtype=F32) + A, rhs, left_side=True, lower=True,
                                     unit_diagonal=True)
    u, w = uw[..., :dv], uw[..., dv:]

    def step(S, xs):
        q_i, k_i, u_i, w_i, G_i, dec_i = xs
        v_new = u_i - jnp.einsum('bhck,bhkv->bhcv', w_i, S)
        attn = jnp.einsum('bhik,bhjk->bhij', q_i, k_i) * dec_i
        o = (jnp.einsum('bhck,bhkv->bhcv', q_i * jnp.exp(G_i)[..., None], S)
             + jnp.einsum('bhij,bhjv->bhiv', attn, v_new))
        g_last = G_i[..., -1:]
        S = (S * jnp.exp(g_last)[..., None]
             + jnp.einsum('bhck,bhcv->bhkv', k_i * jnp.exp(g_last - G_i)[..., None], v_new))
        return S, o

    S, o = lax.scan(step, S0, (qc, kc, u, w, G, decay))
    return from_chunks(o), S

def chunk_gla(q, k, v, logf, S0):
    C = HG_CHUNK
    qc, kc, vc, gc = to_chunks(q, C), to_chunks(k, C), to_chunks(v, C), to_chunks(logf, C)
    G = jnp.cumsum(gc, axis=-2)
    incl = jnp.tril(jnp.ones((C, C), bool))[:, :, None]

    def step(S, xs):
        q_i, k_i, v_i, G_i = xs
        dec = jnp.exp(jnp.where(incl, G_i[:, :, :, None, :] - G_i[:, :, None, :, :], -jnp.inf))
        attn = jnp.einsum('bhtk,bhtsk->bhts', q_i, dec * k_i[:, :, None, :, :])
        o = (jnp.einsum('bhtk,bhkv->bhtv', q_i * jnp.exp(G_i), S)
             + jnp.einsum('bhts,bhsv->bhtv', attn, v_i))
        g_last = G_i[:, :, -1:, :]
        S = (S * jnp.exp(g_last[:, :, 0, :])[..., None]
             + jnp.einsum('bhsk,bhsv->bhkv', k_i * jnp.exp(g_last - G_i), v_i))
        return S, o

    S, o = lax.scan(step, S0, (qc, kc, vc, G))
    return from_chunks(o), S

def gdn_mixer(h_ctx, h_lat, w_in, conv_w, a_log, dt_bias, norm_w, w_out, with_ctx_out):
    n_qkv = 2 * GD_QK + GD_V

    def project(h):
        B, n, _ = h.shape
        u = h @ w_in
        qkv = jax.nn.silu(centred_depthwise_conv(u[..., :n_qkv], conv_w))
        q = l2_normalize(qkv[..., :GD_QK].reshape(B, n, GD_H, GD_DK)) * GD_DK ** -0.5
        k = l2_normalize(qkv[..., GD_QK:2 * GD_QK].reshape(B, n, GD_H, GD_DK))
        v = qkv[..., 2 * GD_QK:].astype(F32).reshape(B, n, GD_H, GD_DV)
        z = u[..., n_qkv:n_qkv + GD_V]
        ba = u[..., n_qkv + GD_V:].astype(F32).reshape(B, n, 2, 2, GD_H)
        beta = jax.nn.sigmoid(ba[:, :, 0])
        g = -jnp.exp(a_log.astype(F32)) * jax.nn.softplus(ba[:, :, 1] + dt_bias.astype(F32))
        return q, k, v, z, beta, g

    qc, kc, vc, zc, bc, gc = project(h_ctx)
    ql, kl, vl, zl, bl, gl = project(h_lat)
    S0 = jnp.zeros((h_lat.shape[0], GD_H, GD_DK, GD_DV), F32)
    o_c = 0.0
    o_l = 0.0
    for d in range(2):
        oc_d, S_c = chunk_gated_delta(orient(qc, d), orient(kc, d), orient(vc, d),
                                      orient(gc[:, :, d], d), orient(bc[:, :, d], d), S0)
        ol_d, _ = chunk_gated_delta(orient(ql, d), orient(kl, d), orient(vl, d),
                                    orient(gl[:, :, d], d), orient(bl[:, :, d], d), S_c)
        o_c = o_c + orient(oc_d, d)
        o_l = o_l + orient(ol_d, d)

    def readout(o, z):
        B, n = o.shape[:2]
        y = rms_norm(o, norm_w) * jax.nn.silu(z.astype(F32)).reshape(B, n, GD_H, GD_DV)
        return y.reshape(B, n, GD_V).astype(z.dtype) @ w_out

    y_ctx = readout(o_c, zc) if with_ctx_out else None
    return y_ctx, readout(o_l, zl)

def hgrn2_mixer(h_ctx, h_lat, w_in, lb, norm_w, w_out, with_ctx_out):
    lbh = lb.reshape(HG_H, HG_DK)

    def project(h):
        B, n, _ = h.shape
        q, f_fw, f_bw, i, g = jnp.split(h @ w_in, 5, axis=-1)
        q = jax.nn.silu(q).astype(F32).reshape(B, n, HG_H, HG_DK)
        f = jnp.stack([f_fw, f_bw], axis=2).astype(F32).reshape(B, n, 2, HG_H, HG_DK)
        logf = jnp.log(lbh + (1.0 - lbh) * jax.nn.sigmoid(f))
        k = (1.0 - lbh) * jax.nn.sigmoid(-f)
        v = i.astype(F32).reshape(B, n, HG_H, HG_DV)
        return q, k, v, logf, g

    qc, kc, vc, fc, gc = project(h_ctx)
    ql, kl, vl, fl, gl = project(h_lat)
    S0 = jnp.zeros((h_lat.shape[0], HG_H, HG_DK, HG_DV), F32)
    o_c = 0.0
    o_l = 0.0
    for d in range(2):
        oc_d, S_c = chunk_gla(orient(qc, d), orient(kc[:, :, d], d), orient(vc, d),
                              orient(fc[:, :, d], d), S0)
        ol_d, _ = chunk_gla(orient(ql, d), orient(kl[:, :, d], d), orient(vl, d),
                            orient(fl[:, :, d], d), S_c)
        o_c = o_c + orient(oc_d, d)
        o_l = o_l + orient(ol_d, d)

    def readout(o, g):
        B, n = o.shape[:2]
        y = rms_norm(o, norm_w) * jax.nn.silu(g.astype(F32)).reshape(B, n, HG_H, HG_DV)
        return y.reshape(B, n, D_MODEL).astype(g.dtype) @ w_out

    y_ctx = readout(o_c, gc) if with_ctx_out else None
    return y_ctx, readout(o_l, gl)

def expert_choice_ffn(h, router_w, w_gate, w_up, w_down):
    B, n, D = h.shape
    cap = EC_CAPACITY * n // N_EXPERTS
    aff = jax.nn.softmax((h @ router_w).astype(F32), axis=-1)
    gate, idx = lax.top_k(jnp.swapaxes(aff, 1, 2), cap)
    xe = jax.vmap(lambda hb, ib: hb[ib])(h, idx)
    a = jnp.einsum('becd,edf->becf', xe, w_gate)
    u = jnp.einsum('becd,edf->becf', xe, w_up)
    ye = jnp.einsum('becf,efd->becd', jax.nn.silu(a) * u, w_down) * gate[..., None].astype(h.dtype)
    return jax.vmap(lambda ib, yb: jnp.zeros((n, D), h.dtype).at[ib.reshape(-1)].add(yb.reshape(-1, D)))(idx, ye)

def second_inputs(seed: int = 0) -> dict:
    key = jax.random.key(seed)
    keys = iter(jax.random.split(key, 48))

    def nrm(shape, std):
        return std * jax.random.normal(next(keys), shape, F32)

    def gain(shape):
        return 1.0 + nrm(shape, 0.02)

    D = D_MODEL
    gd_cols = 2 * GD_QK + 2 * GD_V + 4 * GD_H
    gd_a_log = jnp.log(jax.random.uniform(next(keys), (2, GD_H), F32, 1.0, 16.0))
    dt = jnp.exp(jax.random.uniform(next(keys), (2, GD_H), F32, math.log(1e-3), math.log(1e-1)))
    gd_dt_bias = jnp.log(jnp.expm1(dt))
    return {
        'x': nrm((BATCH, SEQ, D), 1.0),
        'c': nrm((BATCH, D), 1.0),
        'ctx': nrm((BATCH, CTX_LEN, D), 1.0),
        'c_ctx': nrm((D,), 1.0),
        'ada_w': nrm((DEPTH, D, 6 * D), 0.5 * D ** -0.5),
        'ada_b': nrm((DEPTH, 6 * D), 0.02),
        'norm1_w': gain((DEPTH, D)),
        'norm2_w': gain((DEPTH, D)),
        'final_norm_w': gain((D,)),
        'hy_w_in': nrm((D, 3 * D), D ** -0.5),
        'hy_b_in': nrm((3 * D,), 0.02),
        'hy_short_w': nrm((HY_SHORT, 3 * D), HY_SHORT ** -0.5),
        'hy_short_b': nrm((3 * D,), 0.02),
        'hy_ffn_w1': nrm((HY_EMB, HY_FFN), HY_EMB ** -0.5),
        'hy_ffn_b1': nrm((HY_FFN,), 0.02),
        'hy_ffn_w2': nrm((HY_FFN, HY_FFN), HY_FFN ** -0.5),
        'hy_ffn_b2': nrm((HY_FFN,), 0.02),
        'hy_ffn_w3': nrm((HY_FFN, HY_ORDER * 2 * D), 0.01),
        'hy_sin_freq': gain((2, HY_FFN)),
        'hy_filter_bias': nrm((HY_ORDER, D), 0.5),
        'hy_w_out': nrm((D, D), D ** -0.5),
        'hy_b_out': nrm((D,), 0.02),
        'sw_w_in': nrm((D, (SW_HQ + 2 * SW_HKV) * SW_HD), D ** -0.5),
        'sw_sink': nrm((SW_HQ,), 0.5),
        'sw_w_out': nrm((SW_HQ * SW_HD, D), (SW_HQ * SW_HD) ** -0.5),
        'gd_w_in': nrm((D, gd_cols), D ** -0.5),
        'gd_conv_w': nrm((GD_CONV, 2 * GD_QK + GD_V), GD_CONV ** -0.5),
        'gd_a_log': gd_a_log,
        'gd_dt_bias': gd_dt_bias,
        'gd_norm_w': gain((GD_DV,)),
        'gd_w_out': nrm((GD_V, D), GD_V ** -0.5),
        'hg_w_in': nrm((D, 5 * D), D ** -0.5),
        'hg_lb': nrm((DEPTH, D), 1.0),
        'hg_norm_w': gain((HG_DV,)),
        'hg_w_out': nrm((D, D), D ** -0.5),
        'moe_router': nrm((DEPTH, D, N_EXPERTS), D ** -0.5),
        'moe_w_gate': nrm((DEPTH, N_EXPERTS, D, EXPERT_FF), D ** -0.5),
        'moe_w_up': nrm((DEPTH, N_EXPERTS, D, EXPERT_FF), D ** -0.5),
        'moe_w_down': nrm((DEPTH, N_EXPERTS, EXPERT_FF, D), EXPERT_FF ** -0.5),
    }

def second_block(x, c, ctx, c_ctx, ada_w, ada_b, norm1_w, norm2_w, final_norm_w,
              hy_w_in, hy_b_in, hy_short_w, hy_short_b, hy_ffn_w1, hy_ffn_b1, hy_ffn_w2, hy_ffn_b2,
              hy_ffn_w3, hy_sin_freq, hy_filter_bias, hy_w_out, hy_b_out,
              sw_w_in, sw_sink, sw_w_out,
              gd_w_in, gd_conv_w, gd_a_log, gd_dt_bias, gd_norm_w, gd_w_out,
              hg_w_in, hg_lb, hg_norm_w, hg_w_out,
              moe_router, moe_w_gate, moe_w_up, moe_w_down):
    lat, cx = x, ctx
    lb_all = jnp.cumsum(jax.nn.softmax(hg_lb.astype(F32), axis=0), axis=0)
    for layer in range(DEPTH):
        kind = layer % N_MIXERS_2
        keep_ctx = layer < DEPTH - 1
        mod_l = [m[:, None, :] for m in jnp.split(jax.nn.silu(c) @ ada_w[layer] + ada_b[layer], 6, axis=-1)]
        mod_c = jnp.split(jax.nn.silu(c_ctx) @ ada_w[layer] + ada_b[layer], 6, axis=-1)
        h_l = rms_norm(lat, norm1_w[layer]) * (1.0 + mod_l[1]) + mod_l[0]
        h_c = rms_norm(cx, norm1_w[layer]) * (1.0 + mod_c[1]) + mod_c[0]
        if kind == 0:
            hy_args = (hy_w_in, hy_b_in, hy_short_w, hy_short_b, hy_ffn_w1, hy_ffn_b1, hy_ffn_w2,
                       hy_ffn_b2, hy_ffn_w3, hy_sin_freq, hy_filter_bias, hy_w_out, hy_b_out)
            y_l = hyena_mixer(h_l, *hy_args)
            y_c = hyena_mixer(h_c, *hy_args) if keep_ctx else None
        elif kind == 1:
            y_c, y_l = swa_mixer(h_c, h_l, sw_w_in, sw_sink, sw_w_out, keep_ctx)
        elif kind == 2:
            y_c, y_l = gdn_mixer(h_c, h_l, gd_w_in, gd_conv_w, gd_a_log, gd_dt_bias, gd_norm_w,
                                 gd_w_out, keep_ctx)
        else:
            lb = lb_all[layer] - lb_all[0]
            y_c, y_l = hgrn2_mixer(h_c, h_l, hg_w_in, lb, hg_norm_w, hg_w_out, keep_ctx)
        lat = lat + mod_l[2] * y_l
        h_l = rms_norm(lat, norm2_w[layer]) * (1.0 + mod_l[4]) + mod_l[3]
        lat = lat + mod_l[5] * expert_choice_ffn(h_l, moe_router[layer], moe_w_gate[layer],
                                                 moe_w_up[layer], moe_w_down[layer])
        if keep_ctx:
            cx = cx + mod_c[2] * y_c
            h_c = rms_norm(cx, norm2_w[layer]) * (1.0 + mod_c[4]) + mod_c[3]
            cx = cx + mod_c[5] * expert_choice_ffn(h_c, moe_router[layer], moe_w_gate[layer],
                                                   moe_w_up[layer], moe_w_down[layer])
    return rms_norm(lat, final_norm_w)


def setup_inputs(seed=0):
    out = dict(first_inputs(seed))
    for name, value in second_inputs(seed + 1).items():
        if name != "x":
            out[name + "_2"] = value
    return out


def reference(
    x, mem, positions, ffn_w_in, ffn_w_out, ln_g, ln_b, da_w_qkv, da_w_o, da_lam_q, da_lam_k,
    da_subln_g, pool_w, pool_b, pool_scale, ret_w_qkvg, ret_w_o, xa_wq, xa_wkv, xa_wo, c_2,
    ctx_2, c_ctx_2, ada_w_2, ada_b_2, norm1_w_2, norm2_w_2, final_norm_w_2, hy_w_in_2,
    hy_b_in_2, hy_short_w_2, hy_short_b_2, hy_ffn_w1_2, hy_ffn_b1_2, hy_ffn_w2_2, hy_ffn_b2_2,
    hy_ffn_w3_2, hy_sin_freq_2, hy_filter_bias_2, hy_w_out_2, hy_b_out_2, sw_w_in_2, sw_sink_2,
    sw_w_out_2, gd_w_in_2, gd_conv_w_2, gd_a_log_2, gd_dt_bias_2, gd_norm_w_2, gd_w_out_2,
    hg_w_in_2, hg_lb_2, hg_norm_w_2, hg_w_out_2, moe_router_2, moe_w_gate_2, moe_w_up_2,
    moe_w_down_2,
):
    x = first_block(
        x, mem, positions, ffn_w_in, ffn_w_out, ln_g, ln_b, da_w_qkv, da_w_o, da_lam_q,
        da_lam_k, da_subln_g, pool_w, pool_b, pool_scale, ret_w_qkvg, ret_w_o, xa_wq, xa_wkv,
        xa_wo,
    )
    return second_block(
        x, c_2, ctx_2, c_ctx_2, ada_w_2, ada_b_2, norm1_w_2, norm2_w_2, final_norm_w_2,
        hy_w_in_2, hy_b_in_2, hy_short_w_2, hy_short_b_2, hy_ffn_w1_2, hy_ffn_b1_2, hy_ffn_w2_2,
        hy_ffn_b2_2, hy_ffn_w3_2, hy_sin_freq_2, hy_filter_bias_2, hy_w_out_2, hy_b_out_2,
        sw_w_in_2, sw_sink_2, sw_w_out_2, gd_w_in_2, gd_conv_w_2, gd_a_log_2, gd_dt_bias_2,
        gd_norm_w_2, gd_w_out_2, hg_w_in_2, hg_lb_2, hg_norm_w_2, hg_w_out_2, moe_router_2,
        moe_w_gate_2, moe_w_up_2, moe_w_down_2,
    )


_drawn_inputs = setup_inputs


def setup_inputs(seed=0):
    import zlib

    import numpy as np

    out = dict(_drawn_inputs(seed))
    spreads = {}
    factors = {'da_lam_q': 8.0,
     'da_subln_g': 7.638,
     'pool_b': 3.687,
     'pool_scale': 7.936,
     'ada_b_2': 3.157,
     'norm1_w_2': 8.0,
     'norm2_w_2': 38.361,
     'final_norm_w_2': 8.647,
     'hy_b_in_2': 8.0,
     'hy_short_b_2': 8.0,
     'hy_ffn_b1_2': 8.0,
     'hy_ffn_b2_2': 5.717,
     'hy_sin_freq_2': 8.0,
     'hy_b_out_2': 64.0,
     'sw_sink_2': 8.0}
    for name, (base, spread) in spreads.items():
        noise = np.random.default_rng([zlib.crc32(name.encode()), seed]).standard_normal(out[name].shape)
        drawn = base * np.exp(spread * noise) if base else spread * noise
        out[name] = jnp.asarray(drawn.astype(out[name].dtype))
    for name, factor in factors.items():
        out[name] = (out[name] * factor).astype(out[name].dtype)
    return out
```

```python
from collections import namedtuple
from contextlib import ExitStack
import math

import numpy as np

import concourse.bass as bass
from concourse import mybir

F32 = mybir.dt.float32
I32 = mybir.dt.int32
ACT = mybir.ActivationFunctionType
ALU = mybir.AluOpType
AX_X = mybir.AxisListType.X

P = 128
S = 256
D = 1024
KB = D // P
NT = S // P
DEPTH = 2
FF = 2816
FB = 256
FSTEPS = FF // FB
ALPHA = (2 * DEPTH) ** 0.25
LN_EPS = 1e-5
EPS = 1e-6
NEG = -1e30
DA_H, DA_DK = 8, 64
LAM_INIT = 0.8 - 0.6 * math.exp(0.0)
XA_H = 4
XA_DK = D // XA_H
POOL_WINDOWS = (2, 4, 8, 16)
NMOD = 6
HY_LFFT = 2 * S - 1
HY_EMB, HY_FFN = 33, 64
HC = 256
SW_HQ, SW_HKV, SW_HD, SW_WINDOW = 16, 4, 64, 128
E_N, E_FF, CAP = 16, 1024, 2 * S // 16

RING = 12
SLOT = 2048
PR_RING = 4
SCRATCH = 9216

TWO_PI = 2.0 * math.pi
PI_BELOW = 3.1415925
MAGIC = 12582912.0


def two_pi_parts():
    c1 = float(np.float32(6.28125))
    c2 = float(np.float32(int((TWO_PI - c1) * 2 ** 21) / 2 ** 21))
    return c1, c2, float(np.float32(TWO_PI - c1 - c2))


def const_pack():
    p = np.arange(P)
    tok = np.arange(NT)[:, None] * P + p[None, :]
    parts = {}
    parts["ident"] = np.eye(P)
    parts["lanes4"] = (p[:, None] % 32 == p[None, :] % 32)
    parts["lanes2"] = (p[:, None] % 64 == p[None, :] % 64)
    parts["iota"] = np.broadcast_to(np.arange(1, CAP + 1), (P, CAP))
    inv = (1.0 / (np.float32(10000.0) ** (np.arange(0, DA_DK, 2, dtype=np.float32) / np.float32(DA_DK)))).astype(np.float32)
    parts["da_inv"] = np.broadcast_to(inv, (P, DA_DK // 2))
    nf = SW_HD // 4
    sinv = (np.float32(10000.0) ** (-np.arange(nf, dtype=np.float32) / np.float32(nf))).astype(np.float32)
    row, col = (tok // 64).astype(np.float32), (tok % 64).astype(np.float32)
    ang = np.concatenate([row[..., None] * sinv, col[..., None] * sinv], -1).astype(np.float64)
    parts["sw_cos"] = np.cos(ang).transpose(1, 0, 2).reshape(P, -1)
    parts["sw_sin"] = np.sin(ang).transpose(1, 0, 2).reshape(P, -1)
    parts["not_first"] = (tok.T > 0)
    where, at, cols = {}, 0, []
    for name, a in parts.items():
        a = np.asarray(a, np.float32).reshape(P, -1)
        where[name] = (at, a.shape[1])
        at += a.shape[1]
        cols.append(a)
    return np.ascontiguousarray(np.concatenate(cols, 1)), where


def mask_tables():
    q = (np.arange(NT)[:, None] * P + np.arange(P)[None, :]).T[..., None]
    k = np.arange(S)[None, None, :]
    causal = np.where(k <= q, 0.0, NEG)
    band = np.where(np.abs(q - k) <= SW_WINDOW, 0.0, NEG)
    return np.stack([causal, band]).reshape(2, P, NT * S).astype(np.float32)


def pool_tables():
    out = np.zeros((S, len(POOL_WINDOWS), S))
    for g, w in enumerate(POOL_WINDOWS):
        for t in range(S):
            out[max(0, t - w + 1):t + 1, g, t] = 1.0 / min(t + 1, w)
            out[t, g, t] -= 1.0
    return np.ascontiguousarray(out.reshape(NT, P, -1).transpose(1, 0, 2).reshape(P, -1)).astype(np.float32)


def dft_tables():
    a = np.arange(S)
    ang = 2 * np.pi * ((a[:, None] * a[None, :]) % HY_LFFT) / HY_LFFT
    c = np.where(a == 0, 1.0, 2.0)[:, None] / HY_LFFT
    tabs = np.stack([np.cos(ang), np.sin(ang), c * np.cos(ang), c * np.sin(ang)])
    return np.ascontiguousarray(tabs.reshape(4, NT, P, S).transpose(2, 0, 1, 3).reshape(P, -1)).astype(np.float32)


def position_features():
    t = np.linspace(0.0, 1.0, S)
    w = 2.0 * np.pi * np.arange(S) / S
    f = np.linspace(1e-4, (HY_EMB - 1) // 2 - 1, (HY_EMB - 1) // 2)
    z = np.concatenate([t[:, None], np.cos(f * w[:, None]), -np.sin(f * w[:, None])], -1)
    return np.ascontiguousarray(z.T).astype(np.float32)


def window_table():
    lo, hi = math.log(1e-2) / 1.5, math.log(1e-2) / 0.3
    deltas = np.abs(np.linspace(lo, hi, D))
    w = np.exp(-np.linspace(0.0, 1.0, S)[:, None] * deltas) + 0.05
    return np.ascontiguousarray(w.reshape(NT, P, D).transpose(1, 0, 2)).astype(np.float32)


CONSTS, CONST_AT = const_pack()

SUMS_BEFORE_IN = ((), (), (), (4, 5))
SUMS_AFTER_IN = ((), (0, 1), (2, 3), ())
PARTS_AFTER_OUT = ((0, 1), (2, 3), (4, 5), ())
ADA_PER_BODY = 6


def ffn_events(steps, ada):
    out, tile, load, before, parts = [], 0, 0, -2, {}

    def sums(cs):
        nonlocal tile
        for c in cs:
            out.append(("sum", c, tile, parts[c]))
            tile += 1

    for n, u in enumerate(steps):
        if ada:
            sums(SUMS_BEFORE_IN[n])
        mine = tile
        for half in range(2):
            out.append(("in", (u, half), tile, load))
            tile += 1
        load += 2
        if ada:
            sums(SUMS_AFTER_IN[n])
        if u > 0:
            out.append(("out", u - 1, before, load))
            load += 1
        before = mine
        if ada:
            for c in PARTS_AFTER_OUT[n]:
                out.append(("part", c, tile, load))
                parts[c] = tile
                tile += 1
                load += 2
    assert before == tile - 2
    return out, tile, load


FFN_BODY = 4
FFN_HEAD = (FSTEPS - 1) % FFN_BODY + 1
FFN_LOOPS = (FSTEPS - FFN_HEAD) // FFN_BODY


def attention_order(units):
    at, order = 0, {}
    for v in range(units + 2):
        for kind, u in (("s", v), ("t", v - 1), ("o", v - 2)):
            if 0 <= u < units:
                order[kind, u] = at
                at += 1
    return order


class Plan:

    FIELDS = ("loads", "tiles", "acc", "rows", "norms", "silu", "units", "convs", "lags",
              "spectra", "experts")

    At = namedtuple("At", FIELDS)

    def __init__(self):
        self.now = dict.fromkeys(self.FIELDS, 0)
        self.stages = {}

    def add(self, stage, **n):
        self.stages[stage] = self.At(**self.now)
        for f, more in n.items():
            self.now[f] += more

    def __getitem__(self, stage):
        return self.stages[stage]


def ffn_totals(ada):
    _, t0, l0 = ffn_events(range(FFN_HEAD), False)
    _, t1, l1 = ffn_events(range(FFN_HEAD, FFN_HEAD + FFN_BODY), ada)
    assert t1 % 4 == 0 and l1 % RING == 0
    return t0, l0, t1, l1


def make_plan():
    plan = Plan()
    plan.add("mem_cols", tiles=4)
    plan.add("x_cols", tiles=4)
    plan.add("hy_mlp1", tiles=1)
    for i in range(DEPTH):
        for j in (0, 1):
            if j:
                if i == 0:
                    plan.add("hy_mlp2", tiles=1)
                    plan.add("da_qkv", loads=12, tiles=12)
                    plan.add("da_turn", tiles=8)
                    plan.add("da_att", tiles=3 * NT * DA_H, units=NT * DA_H)
                    plan.add("da_cols", tiles=4, norms=1)
                    plan.add("da_out", loads=4, acc=1)
                else:
                    plan.add("pool_mix", loads=1, tiles=4)
                    plan.add("pool_out", loads=1, acc=1)
                plan.add(f"xa_kv{i}", loads=8, tiles=8)
                plan.add(f"mix_norm{i}", tiles=4, rows=NT, norms=1)
                plan.add(f"xa_q{i}", loads=4, tiles=4)
                plan.add(f"xa_att{i}", tiles=3 * NT * XA_H, units=NT * XA_H)
                plan.add(f"xa_cols{i}", tiles=4)
                plan.add(f"xa_out{i}", loads=4, acc=1)
                plan.add(f"xa_norm{i}", tiles=4, rows=NT, norms=1)
            n = 2 * i + j
            t0, l0, t1, l1 = ffn_totals(n < DEPTH)
            plan.add(f"ffn{n}", loads=l0 + FFN_LOOPS * l1 + 1, tiles=t0 + FFN_LOOPS * t1, acc=1,
                     silu=2 * FSTEPS)
            plan.add(f"ffn_norm{n}", tiles=4 * int(n != 2), rows=NT, norms=1)
    plan.add("mod_norm0", tiles=4 * NT, rows=2 * NT, norms=1)
    for c in range(D // HC):
        plan.add(f"hy_u{c}", loads=3, tiles=10, convs=6)
        for o in range(2):
            plan.add(f"hy_k{c}{o}", loads=2 * int(o == 0), tiles=4, lags=NT)
            plan.add(f"hy_v{c}{o}", tiles=4, spectra=2)
            plan.add(f"hy_y{c}{o}", tiles=2)
    plan.add("hy_out0", loads=4, acc=1)
    plan.add("hy_out1", acc=1)
    plan.add("moe_norm0", tiles=4 * NT, rows=2 * NT, norms=1)
    plan_moe(plan, 0)
    plan.add("mod_norm1", tiles=4 * NT, rows=2 * NT, norms=1)
    plan.add("sw_qkv", loads=6, tiles=8)
    plan.add("sw_turn", tiles=6)
    plan.add("sw_att", tiles=3 * NT * SW_HQ, units=NT * SW_HQ)
    plan.add("sw_cols", tiles=4)
    plan.add("sw_out", loads=4, acc=1)
    plan.add("moe_norm1", tiles=2 * NT, rows=NT, norms=1)
    plan_moe(plan, 1)
    plan.add("last_norm", rows=NT, norms=1)
    return plan


MOE_LOADS = 12


def moe_body_tiles(streams):
    return 12 + 4 * streams


def plan_moe(plan, layer):
    streams = 2 - layer
    plan.add(f"router{layer}", tiles=3)
    plan.add(f"gather{layer}", tiles=KB * streams)
    plan.add(f"experts{layer}", loads=MOE_LOADS * E_N, tiles=moe_body_tiles(streams) * E_N, experts=E_N)


class Steps:

    def __init__(self, eng, sem):
        self.eng, self.sem, self.n, self.more = eng, sem, 0, 0

    def __call__(self, ins):
        ins.then_inc(self.sem, 1)
        self.n += 1

    def settle(self):
        self.eng.wait_ge(self.sem, self.n + self.more)

    def loop_in(self, i, per):
        self.at, self.per, self.more = self.n, per, i * per

    def loop_out(self, times):
        assert self.n - self.at == self.per, (self.n - self.at, self.per)
        self.n, self.more = self.at + self.per * times, 0


def param_rows(io, mod_rows):
    rows = []

    def ln(i, j):
        rows.extend([io["ln_g"][i, j], io["ln_b"][i, j]])

    for i in range(DEPTH):
        ln(i, 0)
        if i == 1:
            rows.extend([io["pool_b"][0].rearrange("g c -> (g c)"), io["pool_scale"][0]])
        ln(i, 1)
        ln(i, 2)
        ln(i, 3)

    def mod(layer, stream, n):
        rows.append(mod_rows[layer, stream, n * D:(n + 1) * D])

    for layer in range(DEPTH):
        for s in range(2):
            rows.append(io["norm1_w"][layer])
            mod(layer, s, 1)
            mod(layer, s, 0)
        if layer == 0:
            rows.extend([io["hy_bias"][0], io["hy_bias"][1]])
            mod(0, 0, 2)
            rows.append(io["hy_b_out"])
            mod(0, 1, 2)
        else:
            mod(1, 0, 2)
        for s in range(2 - layer):
            rows.append(io["norm2_w"][layer])
            mod(layer, s, 4)
            mod(layer, s, 3)
        for s in range(2 - layer):
            mod(layer, s, 5)
    rows.append(io["final_w"])
    return rows


def build_program(nc, io, out, mod_rows):
    plan = make_plan()
    with ExitStack() as ctx:
        def sb(name, shape, dt=F32):
            return ctx.enter_context(nc.sbuf_tensor(name, shape, dt))

        sems = {}

        def sem(name):
            sems[name] = ctx.enter_context(nc.semaphore(name))
            return sems[name]

        ring = sb("ring", [P, RING, SLOT])
        rows_x = sb("rows_x", [P, 2 * NT, D])
        rows_h = sb("rows_h", [P, 2 * NT, D])
        cols_x = sb("cols_x", [P, KB, 2 * S])
        prow = sb("prow", [P, PR_RING, D])
        scratch = sb("scratch", [P, SCRATCH])
        consts = sb("consts", [P, CONSTS.shape[1]])
        mask = sb("mask", [P, NT, S])
        stats = sb("stats", [P, NT, 2, 6])
        mean_var = sb("mean_var", [P, 2 * NT, 2])
        spread = sb("spread", [P, 2 * NT])
        root = sb("root", [P, 2 * NT])
        rstd = sb("rstd", [P, 2 * NT])
        newton = sb("newton", [P, 2 * NT])
        pos_i = sb("pos_i", [P, NT], I32)
        pos_f = sb("pos_f", [P, NT])
        da_cs = sb("da_cs", [P, 2, NT, DA_DK // 2])
        subln = sb("subln", [P, 2 * DA_DK])
        lam = sb("lam", [P, 4])
        head_sq = sb("head_sq", [P, 3, NT * DA_H])
        peak = sb("peak", [P, 2, 2])
        low = sb("low", [P, 2, 2])
        mass = sb("mass", [P, 2, 2])
        share = sb("share", [P, 2, 2])
        head_tmp = sb("head_tmp", [P, NT * DA_H])
        hy_cols = sb("hy_cols", [P, 3 * KB, 5])
        hy_small = sb("hy_small", [HY_FFN, 2 * HY_FFN + 4])
        hy_h = sb("hy_h", [HY_FFN, 2, S])
        router_w = sb("router_w", [P, DEPTH, KB, E_N])
        sink = sb("sink", [P, SW_HQ])
        sink_exp = sb("sink_exp", [P, 2])
        gate = sb("gate", [P, 2 * NT, E_N])
        codes = sb("codes", [P, 2 * NT, E_N])
        top8 = sb("top8", [E_N, 8])
        act_in = sb("act_in", [P, KB, 2])
        act_col = sb("act_col", [P, KB, 32])

        def const(name, rows=P):
            at, n = CONST_AT[name]
            return consts[0:rows, at:at + n]

        ident = const("ident")

        def scr(at, n):
            return scratch[:, at:at + n]

        work = ctx.enter_context(nc.psum_tensor("work", [P, 4, 512], F32))
        acc = ctx.enter_context(nc.psum_tensor("acc", [P, 4, 512], F32))

        load_landed = [sem(f"load_landed{i}") for i in range(RING)]
        loads_used = sem("loads_used")
        tile_full = [sem(f"tile_full{i}") for i in range(4)]
        tile_read = [sem(f"tile_read{i}") for i in range(4)]
        acc_full = sem("acc_full")
        acc_read = sem("acc_read")
        row_landed = [sem(f"row_landed{i}") for i in range(PR_RING)]
        rows_used = sem("rows_used")
        rows_ready = sem("rows_ready")
        silu_ready = sem("silu_ready")
        var_ready = sem("var_ready")
        root_ready = sem("root_ready")
        x_landed = sem("x_landed")
        mem_landed = sem("mem_landed")
        consts_landed = sem("consts_landed")
        cond_landed = sem("cond_landed")
        small_landed = sem("small_landed")
        mask_landed = sem("mask_landed")
        ada_bias_landed = sem("ada_bias_landed")
        cond_zeroed = sem("cond_zeroed")
        cond_ready = sem("cond_ready")
        part_ready = sem("part_ready")
        mods_summed = sem("mods_summed")
        mods_stored = sem("mods_stored")
        angles_ready = sem("angles_ready")
        sines_ready = sem("sines_ready")
        lam_sums = sem("lam_sums")
        lam_exp = sem("lam_exp")
        padded = sem("padded")
        low_ready = sem("low_ready")
        exp_ready = sem("exp_ready")
        share_ready = sem("share_ready")
        heads_normed = sem("heads_normed")
        out_landed = sem("out_landed")
        hy_landed = sem("hy_landed")
        ctx_landed = sem("ctx_landed")
        window_landed = sem("window_landed")
        mlp_angles = sem("mlp_angles")
        mlp_sines = sem("mlp_sines")
        conv_ready = sem("conv_ready")
        lags_ready = sem("lags_ready")
        spectra_ready = sem("spectra_ready")
        sinks_ready = sem("sinks_ready")
        logits_low = sem("logits_low")
        logits_exp = sem("logits_exp")
        gates_ready = sem("gates_ready")
        codes_ready = sem("codes_ready")
        choice_ready = sem("choice_ready")
        taken_ready = sem("taken_ready")
        spread_ready = sem("spread_ready")
        filters_done = sem("filters_done")
        router_landed = sem("router_landed")
        vec_steps = sem("vec_steps")
        act_steps = sem("act_steps")

        def filled(eng, t, more=0):
            eng.wait_ge(tile_full[t % 4], t // 4 + 1 + more)

        def read_out(eng, t, more=0):
            eng.wait_ge(tile_read[t % 4], t // 4 + 1 + more)

        silu_buf = scr(0, 1024).rearrange("p (b t) -> p b t", b=4)
        gated = scr(1024, 1024).rearrange("p (b t) -> p b t", b=4)
        ada_part = scr(2048, 1024).rearrange("p (b c) -> p b c", b=2)
        mods = scr(3072, NMOD * D)
        mlp_turns = scratch[0:HY_FFN, 0:S]
        lam_in = rows_h[:, 0, 0:4 * DA_DK].rearrange("p (c d) -> p c d", c=2)
        angle = rows_h[:, 0, 256:384].rearrange("p (c j d) -> p c j d", c=2, j=NT)
        turns = rows_h[:, 0, 384:512].rearrange("p (c j d) -> p c j d", c=2, j=NT)
        hy_z_in = rows_h[0:HY_EMB, 1, 0:S]
        q_lo = scr(0, 2048).rearrange("p (h t) -> p h t", h=8)
        q_hi = scr(2048, 2048).rearrange("p (h t) -> p h t", h=8)
        k_cols = scr(4096, 2048).rearrange("p (h t) -> p h t", h=8)
        v_rows = scr(6144, 2048).rearrange("p (j c) -> p j c", j=NT)
        turned_p = scr(8192, 512).rearrange("p (b k t) -> p b k t", b=2, k=2)
        rope_tmp = scr(8704, 512)
        masked = rows_x[:, 2, :].rearrange("p (b c) -> p b c", b=2)
        probs = rows_x[:, 3, :].rearrange("p (b c) -> p b c", b=2)
        q_rows = rows_h[:, 0:NT, :]
        k_rows = rows_h[:, NT:2 * NT, :]
        pooled = scr(0, 2048).rearrange("p (k t) -> p k t", k=KB)
        pool_y = scr(2048, 1024)
        hy_y = scr(0, 2048).rearrange("p (b t) -> p b t", b=4)
        hy_lags = scr(0, 1024).rearrange("p (j c) -> p j c", j=NT)
        hy_k = scr(1024, 1024).rearrange("p (f r c) -> p f r c", f=NT, r=2)
        hy_biased = scr(2048, 1024).rearrange("p (b t) -> p b t", b=2)
        hy_tmp = scr(2048, 512)
        hy_x2 = scr(3072, 1024).rearrange("p (a t) -> p a t", a=2)
        hy_v = scr(4096, 1024).rearrange("p (j c) -> p j c", j=NT)
        hy_x1 = scr(5120, 1024).rearrange("p (j c) -> p j c", j=NT)
        hy_spec = scr(6144, 2048).rearrange("p (f r c) -> p f r c", f=NT, r=2)
        hy_window = scr(8192, 512).rearrange("p (j c) -> p j c", j=NT)
        hy_z = rows_h.rearrange("p j d -> p (j d)").rearrange("p (k t) -> p k t", k=KB)
        mix_tmp = scr(0, D)
        sw_k_cols = scr(4096, 1024).rearrange("p (g t) -> p g t", g=2)
        sw_v = scr(5120, 1024).rearrange("p (k c) -> p k c", k=4)
        sw_k_rows = scr(6144, 1024).rearrange("p (k c) -> p k c", k=4)
        sw_turned = scr(7168, 1024).rearrange("p (b k t) -> p b k t", b=2, k=4)
        sw_tmp = scr(8192, 512)
        sw_masked = rows_h[:, 2, :].rearrange("p (b c) -> p b c", b=2)
        sw_probs = rows_h[:, 3, :].rearrange("p (b c) -> p b c", b=2)
        xe = [cols_x, scr(0, 4096).rearrange("p (k c) -> p k c", k=KB)]
        chosen = scr(4096, 2048).rearrange("p (i c) -> p i c", i=2 * NT)
        gate_part = scr(4096, 1024)
        up_part = scr(5120, 1024)
        down_part = gate_part
        taken = scr(6144, 512)
        silu_e = scr(6656, 512)
        gated_e = scr(7168, 512)
        spread_e = scr(7680, 512).rearrange("p (i c) -> p i c", i=2 * NT)
        spread_cols = scr(8192, 512).rearrange("p (i t) -> p i t", i=2 * NT)
        aff = scratch[0:E_N, 6656:7168]
        left = scratch[0:E_N, 7168:7680]
        picked = scratch[0:E_N, 7680:8192]
        count = scratch[0:E_N, 8192:8704]
        zeros16 = scratch[0:E_N, 8704:9216]
        logit = scr(6144, 64).rearrange("p (i e) -> p i e", i=2 * NT)
        logit_peak = scr(6208, 4)

        block = ctx.enter_context(nc.Block())

        @block.sync
        def _(sp):
            def load(n, dst_shape, src, more=0, rows=P):
                sp.wait_ge(loads_used, n + 1 + more)
                size = int(np.prod(dst_shape))
                dst = ring[0:rows, n % RING, 0:size]
                if len(dst_shape) == 2:
                    dst = dst.rearrange("p (a b) -> p a b", a=dst_shape[0])
                sp.dma_start(dst, src).then_inc(load_landed[n % RING], 16)

            def load_rows_out(n, w, blocks):
                for cb in range(blocks):
                    for half in range(2):
                        load(n, (4, 512), w[half * 512:half * 512 + 512, cb * 512:cb * 512 + 512]
                             .rearrange("(k p) c -> p k c", p=P))
                        n += 1
                return n

            def load_cols_out(n, w, c0, count):
                for cb in range(count):
                    load(n, (KB, 256), w[:, c0 + cb * 256:c0 + cb * 256 + 256].rearrange("(k p) c -> p k c", p=P))
                    n += 1
                return n

            def ffn(i):
                w_in, w_out = io["ffn_w_in"][i // 2, i % 2], io["ffn_w_out"][i // 2, i % 2]
                ada = i < DEPTH
                base = plan[f"ffn{i}"].loads

                def run(events, n0, i_loop, per):
                    step0 = 0 if i_loop is None else i_loop * FFN_BODY
                    more = 0 if i_loop is None else i_loop * per
                    for kind, what, _, at in events:
                        n = n0 + at
                        if kind == "in" and what[1] == 0:
                            for part in range(2):
                                c = (what[0] + step0) * FB + part * FF
                                load(n + part, (KB, FB), w_in[:, bass.ds(c, FB)].rearrange("(k p) c -> p k c", p=P), more)
                        elif kind == "out":
                            r = (what + step0) * FB
                            load(n, (2, D), w_out[bass.ds(r, FB), :].rearrange("(k p) c -> p k c", p=P), more)
                        elif kind == "part":
                            c = (what + i_loop * ADA_PER_BODY) * 512
                            for half in range(2):
                                load(n + half, (4, 512), io["ada_w"][i][half * 512:half * 512 + 512, bass.ds(c, 512)]
                                     .rearrange("(k p) c -> p k c", p=P), more)

                head, _, l0 = ffn_events(range(FFN_HEAD), False)
                body, _, l1 = ffn_events(range(FFN_HEAD, FFN_HEAD + FFN_BODY), ada)
                run(head, base, None, 0)
                with sp.Fori(0, FFN_LOOPS) as it:
                    run(body, base + l0, it, l1)
                n = base + l0 + FFN_LOOPS * l1
                load(n, (2, D), w_out[FF - FB:FF, :].rearrange("(k p) c -> p k c", p=P))

            for i in range(DEPTH):
                ffn(2 * i)
                if i == 0:
                    load_rows_out(plan["da_qkv"].loads, io["da_w_qkv"][0], 6)
                    load_rows_out(plan["da_out"].loads, io["da_w_o"][0], 2)
                else:
                    load(plan["pool_mix"].loads, (SLOT,), io["pool_tables"])
                    load(plan["pool_out"].loads, (8, 256), io["pool_w"][0].rearrange("g (k p) c -> p (g k) c", p=P))
                n = load_cols_out(plan[f"xa_kv{i}"].loads, io["xa_wkv"][i], 0, 4)
                load_rows_out(n, io["xa_wkv"][i][:, D:2 * D], 2)
                load_cols_out(plan[f"xa_q{i}"].loads, io["xa_wq"][i], 0, 4)
                load_rows_out(plan[f"xa_out{i}"].loads, io["xa_wo"][i], 2)
                ffn(2 * i + 1)
            for c in range(D // HC):
                n = plan[f"hy_u{c}"].loads
                for section in range(3):
                    load_cols_out(n + section, io["hy_w_in"], section * D + c * HC, 1)
                n = plan[f"hy_k{c}0"].loads
                load(n, (4, HC), io["hy_w3"].rearrange("p (a c) -> p a c", a=4)[:, :, c * HC:(c + 1) * HC], rows=HY_FFN)
                load(n + 1, (SLOT,), io["dft"])
            load_rows_out(plan["hy_out0"].loads, io["hy_w_out"], 2)

            def experts(layer):
                base = plan[f"experts{layer}"].loads
                with sp.Fori(0, E_N) as e:
                    n = base
                    for name in ("moe_gate", "moe_up", "moe_down"):
                        w = io[name][layer].rearrange("e k c -> (e k) c")
                        for cb in range(2):
                            for half in range(2):
                                load(n, (4, 512), w[bass.ds(e * D + half * 512, 512), cb * 512:cb * 512 + 512]
                                     .rearrange("(k p) c -> p k c", p=P), e * MOE_LOADS)
                                n += 1

            experts(0)
            load_rows_out(plan["sw_qkv"].loads, io["sw_w_in"], 3)
            load_rows_out(plan["sw_out"].loads, io["sw_w_out"], 2)
            experts(1)
            for j in range(NT):
                sp.wait_ge(rows_ready, plan["last_norm"].rows + j + 1)
                sp.dma_start(out[j * P:(j + 1) * P, :], rows_h[:, j, :]).then_inc(out_landed, 16)
            sp.wait_ge(out_landed, 16 * NT)

        @block.tensor
        def _(pe):
            owed = [0]

            def mm(o, lhsT, rhs, start, stop, signal=None, done=0, **kw):
                ins = nc.tensor.matmul(o, lhsT, rhs, start=start, stop=stop, **kw)
                owed[0] += done
                if signal is not None:
                    ins.then_inc(signal, 1)
                elif owed[0]:
                    ins.then_inc(loads_used, owed[0])
                    owed[0] = 0

            def turn(o, i, signal=None, size=P):
                ins = nc.tensor.transpose(o, i, ident[0:size, 0:size])
                if signal is not None:
                    ins.then_inc(signal, 1)
                elif owed[0]:
                    ins.then_inc(loads_used, owed[0])
                    owed[0] = 0

            def open_tile(t, more=0):
                if t >= 4:
                    pe.wait_ge(tile_read[t % 4], t // 4 + more)
                return work[:, t % 4, :]

            def landed(n, more=0):
                pe.wait_ge(load_landed[n % RING], 16 * (n // RING + 1) + more)

            def slot(n, a):
                return ring[:, n % RING, :].rearrange("p (a b) -> p a b", a=a)

            def rows_out(n, t, x, blocks, tok0=0, to_acc=False):
                for cb in range(blocks):
                    outs = []
                    for j in range(NT):
                        outs.append(acc[:, 2 * j + cb, :] if to_acc else open_tile(t + j))
                    for half in range(2):
                        landed(n)
                        w = slot(n, 4)
                        for j in range(NT):
                            for k in range(4):
                                kk = half * 4 + k
                                last = half == 1 and k == 3
                                sig = None
                                if last and not to_acc:
                                    sig = tile_full[(t + j) % 4]
                                if last and to_acc and cb == blocks - 1:
                                    sig = acc_full
                                mm(outs[j], x[:, kk, tok0 + j * P:tok0 + (j + 1) * P], w[:, k, :],
                                   kk == 0, kk == KB - 1, sig, done=int(j == NT - 1 and k == 3))
                        n += 1
                    t += 0 if to_acc else NT

            def cols_out(n, t, x, tok0, count):
                for cb in range(count):
                    landed(n)
                    w = slot(n, KB)
                    o = open_tile(t).rearrange("p (a t) -> p a t", a=2)
                    for a in range(2):
                        for k in range(KB):
                            last = k == KB - 1
                            mm(o[:, a, :], w[:, k, a * P:(a + 1) * P], x[:, k, tok0:tok0 + S], k == 0, last,
                               tile_full[t % 4] if last and a else None, done=int(last and a))
                    n, t = n + 1, t + 1

            def ffn(i):
                at = plan[f"ffn{i}"]
                ada = i < DEPTH
                _, t0, l0 = ffn_events(range(FFN_HEAD), False)
                _, t1, l1 = ffn_events(range(FFN_HEAD, FFN_HEAD + FFN_BODY), ada)

                def down(u, n, first_tile, tmore, lmore, last=False):
                    for h in range(2):
                        read_out(pe, first_tile + h, tmore)
                    landed(n, lmore)
                    w = slot(n, 2)
                    for h in range(2):
                        for j in range(NT):
                            for half in range(2):
                                final = last and h == 1 and half == 1
                                mm(acc[:, 2 * j + half, :], gated[:, (2 * u + h) % 4, j * P:(j + 1) * P],
                                   w[:, h, half * 512:half * 512 + 512], u == 0 and h == 0, last and h == 1,
                                   acc_full if final else None, done=int(h == 1 and j == NT - 1 and half == 1))

                def run(events, tb, lb, it, tper, lper):
                    tmore = 0 if it is None else it * (tper // 4)
                    lmore = 0 if it is None else it * (16 * (lper // RING))
                    for kind, what, dt, dn in events:
                        t, n = tb + dt, lb + dn
                        if kind == "in":
                            u, h = what
                            if h == 0:
                                landed(n, lmore)
                                landed(n + 1, lmore)
                            o = open_tile(t, tmore).rearrange("p (a t) -> p a t", a=2)
                            for a in range(2):
                                w = slot(n + a, KB)
                                for k in range(KB):
                                    fin = a == 1 and k == KB - 1
                                    mm(o[:, a, :], w[:, k, h * P:(h + 1) * P], cols_x[:, k, 0:S], k == 0, k == KB - 1,
                                       tile_full[t % 4] if fin else None, done=2 * int(fin and h == 1))
                        elif kind == "out":
                            if what == 0 and at.acc:
                                pe.wait_ge(acc_read, NT * at.acc)
                            down(what, n, t, tmore, lmore)
                        elif kind == "part":
                            o = open_tile(t, tmore)
                            for half in range(2):
                                landed(n + half, lmore)
                                w = slot(n + half, 4)
                                for g in range(4):
                                    fin = half == 1 and g == 3
                                    mm(o[32 * g:32 * g + 32, :], act_col[:, half * 4 + g, :], w[:, g, :],
                                       half == 0, half == 1, tile_full[t % 4] if fin else None,
                                       done=2 * int(fin), tile_position=(0, 32 * g))
                        else:
                            read_out(pe, tb + dn, tmore)
                            o = open_tile(t, tmore)
                            mm(o[0:32, :], const("lanes4")[:, 0:32], ada_part[:, what % 2, :], True, True, tile_full[t % 4])

                head, _, _ = ffn_events(range(FFN_HEAD), False)
                body, _, _ = ffn_events(range(FFN_HEAD, FFN_HEAD + FFN_BODY), ada)
                run(head, at.tiles, at.loads, None, 0, 0)
                owed_in = owed[0]
                with pe.Fori(0, FFN_LOOPS) as it:
                    run(body, at.tiles + t0, at.loads + l0, it, t1, l1)
                    assert owed[0] == owed_in, (owed[0], owed_in)
                down(FSTEPS - 1, at.loads + l0 + FFN_LOOPS * l1, at.tiles + t0 + FFN_LOOPS * t1 - 2, 0, 0, last=True)

            def attention(stage, heads, scores, values, width, key_tiles, probs=probs, turned_p=turned_p):
                units = NT * heads
                order = attention_order(units)
                at = plan[stage]
                for v in range(units + 2):
                    if v < units:
                        t = at.tiles + order["s", v]
                        scores(open_tile(t), v // heads, v % heads, tile_full[t % 4])
                    if 0 <= v - 1 < units:
                        u = v - 1
                        t = at.tiles + order["t", u]
                        o = open_tile(t)
                        pe.wait_ge(share_ready, at.units + u + 1)
                        n = key_tiles(u // heads)
                        for k in range(n):
                            turn(o[:, k * P:(k + 1) * P], probs[:, u % 2, k * P:(k + 1) * P],
                                 tile_full[t % 4] if k == n - 1 else None)
                    if 0 <= v - 2:
                        u = v - 2
                        t = at.tiles + order["o", u]
                        o = open_tile(t)
                        read_out(pe, at.tiles + order["t", u])
                        n = key_tiles(u // heads)
                        for k in range(n):
                            mm(o[:, 0:width], turned_p[:, u % 2, k, :], values(k, u % heads), k == 0, k == n - 1,
                               tile_full[t % 4] if k == n - 1 else None)

            def out_to_cols(stage, att, heads):
                order = attention_order(NT * heads)
                t = plan[stage].tiles
                for j in range(NT):
                    read_out(pe, plan[att].tiles + order["o", (j + 1) * heads - 1])
                    turn_rows(t + 2 * j, q_rows[:, j, :])
                all_read(t)

            def turn_rows(t, src):
                for piece in range(2):
                    o = open_tile(t + piece)
                    for k in range(4):
                        turn(o[:, k * P:(k + 1) * P], src[:, (4 * piece + k) * P:(4 * piece + k + 1) * P],
                             tile_full[(t + piece) % 4] if k == 3 else None)

            def all_read(t):
                for q in range(4):
                    read_out(pe, t + q)

            def normed_to_cols(stage, rows=rows_x, tiles=NT):
                at = plan[stage]
                for j in range(tiles):
                    pe.wait_ge(rows_ready, at.rows + j + 1)
                    turn_rows(at.tiles + 2 * j, rows[:, j, :])
                all_read(at.tiles + 2 * tiles - 4)

            def acc_open(stage):
                if plan[stage].acc:
                    pe.wait_ge(acc_read, NT * plan[stage].acc)

            def cross_attention(i):
                at = plan[f"xa_kv{i}"]
                cols_out(at.loads, at.tiles, cols_x, S, 4)
                rows_out(at.loads + 4, at.tiles + 4, cols_x, 2, tok0=S)
                normed_to_cols(f"mix_norm{i}")
                q = plan[f"xa_q{i}"]
                cols_out(q.loads, q.tiles, cols_x, 0, 4)
                all_read(at.tiles)
                all_read(at.tiles + 4)
                all_read(q.tiles)
                attention(f"xa_att{i}", XA_H, xa_scores, lambda k, h: v_rows[:, k, h * XA_DK:(h + 1) * XA_DK], XA_DK,
                          lambda j: NT)
                out_to_cols(f"xa_cols{i}", f"xa_att{i}", XA_H)
                acc_open(f"xa_out{i}")
                rows_out(plan[f"xa_out{i}"].loads, 0, cols_x, 2, to_acc=True)
                normed_to_cols(f"xa_norm{i}")

            def hyena_step(c):
                at = plan[f"hy_u{c}"]
                t = at.tiles

                def project(section):
                    nonlocal t
                    n = at.loads + section
                    landed(n)
                    w = slot(n, KB)
                    for a in range(2):
                        o = open_tile(t)
                        for k in range(KB):
                            mm(o, w[:, k, a * P:(a + 1) * P], cols_x[:, k, :], k == 0, k == KB - 1,
                               tile_full[t % 4] if k == KB - 1 else None, done=int(a == 1 and k == KB - 1))
                        t += 1

                def turn_section(section):
                    nonlocal t
                    pe.wait_ge(conv_ready, at.convs + 2 * section + 2)
                    for j in range(NT):
                        o = open_tile(t)
                        for s in range(2):
                            for a in range(2):
                                turn(o[:, s * HC + a * P:s * HC + (a + 1) * P],
                                     hy_y[:, 2 * section + a, s * S + j * P:s * S + (j + 1) * P],
                                     tile_full[t % 4] if s and a else None)
                        t += 1

                project(0)
                project(1)
                turn_section(0)
                project(2)
                turn_section(1)
                w3 = plan[f"hy_k{c}0"].loads
                landed(w3)
                landed(w3 + 1)
                filt = ring[0:HY_FFN, w3 % RING, 0:4 * HC].rearrange("p (a c) -> p a c", a=4)
                tabs = ring[:, (w3 + 1) % RING, :].rearrange("p (a j c) -> p a j c", a=4, j=NT)
                for o_ in range(2):
                    t = plan[f"hy_k{c}{o_}"].tiles
                    for j in range(NT):
                        o = open_tile(t).rearrange("p (a c) -> p a c", a=2)
                        for way in range(2):
                            mm(o[:, way, :], hy_h[:, 1, j * P:(j + 1) * P], filt[:, 2 * o_ + way, :], True, True,
                               tile_full[t % 4] if way else None, done=int(o_ == 1 and j == 1 and way == 1))
                        t += 1
                    pe.wait_ge(lags_ready, plan[f"hy_k{c}{o_}"].lags + NT)
                    for f in range(NT):
                        o = open_tile(t).rearrange("p (a c) -> p a c", a=2)
                        for r in range(2):
                            for j in range(NT):
                                mm(o[:, r, :], tabs[:, r, j, f * P:(f + 1) * P], hy_lags[:, j, r * HC:(r + 1) * HC],
                                   j == 0, j == 1, tile_full[t % 4] if r and j else None)
                        t += 1
                    if o_ == 0:
                        for q in (4, 5):
                            read_out(pe, at.tiles + q)
                    else:
                        for q in (0, 1):
                            read_out(pe, plan[f"hy_y{c}0"].tiles + q)
                    t = plan[f"hy_v{c}{o_}"].tiles
                    for f in range(NT):
                        for r in range(2):
                            o = open_tile(t)
                            for j in range(NT):
                                mm(o, tabs[:, r, j, f * P:(f + 1) * P], hy_v[:, j, :], j == 0, j == 1,
                                   tile_full[t % 4] if j else None)
                            t += 1
                    pe.wait_ge(spectra_ready, plan[f"hy_v{c}{o_}"].spectra + 2)
                    t = plan[f"hy_y{c}{o_}"].tiles
                    for b in range(2):
                        o = open_tile(t)
                        if o_ == 0:
                            for f in range(NT):
                                for r in range(2):
                                    mm(o, tabs[:, 2 + r, f, b * P:(b + 1) * P], hy_spec[:, f, r, :], f + r == 0, f + r == 2,
                                       tile_full[t % 4] if f + r == 2 else None)
                        else:
                            for s in range(2):
                                for f in range(NT):
                                    for r in range(2):
                                        fin = f + r == 2
                                        mm(o[:, s * S:(s + 1) * S], hy_spec[:, f, r, s * HC + b * P:s * HC + (b + 1) * P],
                                           tabs[:, 2 + r, f, :], f + r == 0, fin,
                                           tile_full[t % 4] if fin and s else None, done=int(fin and s == 1 and b == 1))
                        t += 1

            def experts(layer):
                streams = 2 - layer
                m = CAP * streams
                groups = P // m
                tiles = NT * streams
                at = plan[f"router{layer}"]
                t = at.tiles
                o = open_tile(t)
                for i in range(tiles):
                    for k in range(KB):
                        mm(o[:, i * E_N:(i + 1) * E_N], cols_x[:, k, i * P:(i + 1) * P], router_w[:, layer, k, :], k == 0,
                           k == KB - 1, tile_full[t % 4] if i == tiles - 1 and k == KB - 1 else None)
                pe.wait_ge(gates_ready, layer + 1)
                t += 1
                o = open_tile(t)
                for i in range(tiles):
                    turn(o[0:E_N, i * P:(i + 1) * P], gate[:, i, :], tile_full[t % 4] if i == tiles - 1 else None)
                pe.wait_ge(codes_ready, layer + 1)
                t += 1
                o = open_tile(t)
                for i in range(tiles):
                    turn(o[:, i * E_N:(i + 1) * E_N], picked[:, i * P:(i + 1) * P],
                         tile_full[t % 4] if i == tiles - 1 else None, size=E_N)
                pe.wait_ge(choice_ready, layer + 1)
                t = plan[f"gather{layer}"].tiles
                for s in range(streams):
                    for k in range(KB):
                        o = open_tile(t)
                        for j in range(NT):
                            mm(o, rows_h[:, NT * s + j, k * P:(k + 1) * P], chosen[:, NT * s + j, :], j == 0, j == 1,
                               tile_full[t % 4] if j else None)
                        t += 1
                per = moe_body_tiles(streams)
                base = plan[f"experts{layer}"]
                lanes = const("lanes4") if groups == 4 else const("lanes2")
                taken_v = taken[:, 0:KB * m].rearrange("p (k c) -> p k c", k=KB)
                gated_v = gated_e[:, 0:KB * m].rearrange("p (k c) -> p k c", k=KB)
                with pe.Fori(0, E_N) as e:
                    more = e * (per // 4)

                    def grouped(t, n, x):
                        o = open_tile(t, more)
                        for half in range(2):
                            landed(n + half, e * 16)
                            w = slot(n + half, 4)
                            for k in range(4):
                                kk = 4 * half + k
                                g = kk % groups
                                fin = kk == KB - 1
                                mm(o[m * g:m * g + m, :], x[:, kk, :], w[:, k, :], kk < groups, kk >= KB - groups,
                                   tile_full[t % 4] if fin else None, done=2 * int(fin), tile_position=(0, m * g))

                    t, n = base.tiles, base.loads
                    pe.wait_ge(taken_ready, base.experts + e + 1)
                    for q in range(4):
                        grouped(t + q, n + 2 * q, taken_v)
                    pe.wait_ge(spread_ready, base.experts + e + 1)
                    for q in range(2):
                        o = open_tile(t + 4 + q, more)
                        for i in range(streams):
                            turn(o[:, i * P:(i + 1) * P], spread_e[:, q * streams + i, :],
                                 tile_full[(t + 4 + q) % 4] if i == streams - 1 else None)
                    for q, (part, first) in enumerate(((gate_part, 0), (gate_part, 4), (up_part, 0), (up_part, 4))):
                        o = open_tile(t + 6 + q, more)
                        for k in range(4):
                            mm(o[:, k * P:(k + 1) * P], part[:, (first + k) * P:(first + k + 1) * P], lanes, True, True,
                               tile_full[(t + 6 + q) % 4] if k == 3 else None)
                    read_out(pe, t + 8, more)
                    read_out(pe, t + 9, more)
                    for q in range(2):
                        grouped(t + 10 + q, n + 8 + 2 * q, gated_v)
                    for cb in range(2):
                        read_out(pe, t + 10 + cb, more)
                        for i in range(tiles):
                            q = t + 12 + tiles * cb + i
                            o = open_tile(q, more)
                            for a in range(2):
                                c0 = a * 256
                                mm(o[:, c0:c0 + 256], spread_cols[:, i, :], down_part[:, cb * 512 + c0:cb * 512 + c0 + 256],
                                   True, True, tile_full[q % 4] if a else None)
                    assert owed[0] == 0

            def da_scores(o, j, h, signal):
                mm(o[:, 0:S], q_lo[:, h, j * P:(j + 1) * P], k_cols[:, h, :], True, True)
                mm(o[:, S:2 * S], q_hi[:, h, j * P:(j + 1) * P], k_cols[:, h, :], True, True, signal)

            def xa_scores(o, j, h, signal):
                for a in range(2):
                    mm(o[:, 0:S], q_lo[:, 2 * h + a, j * P:(j + 1) * P], k_cols[:, 2 * h + a, :], a == 0, a == 1,
                       signal if a else None)

            pe.sem_inc(loads_used, RING)
            pe.wait_ge(consts_landed, 16)
            pe.wait_ge(mem_landed, 16)
            for j in range(NT):
                turn_rows(plan["mem_cols"].tiles + 2 * j, rows_x[:, NT + j, :])
            pe.wait_ge(x_landed, 16)
            for j in range(NT):
                turn_rows(plan["x_cols"].tiles + 2 * j, rows_x[:, j, :])
            pe.wait_ge(hy_landed, 16 * 3)
            t = plan["hy_mlp1"].tiles
            mm(open_tile(t)[0:HY_FFN, 0:S], hy_small[0:HY_EMB, 0:HY_FFN], hy_z_in, True, True, tile_full[t % 4])
            all_read(plan["x_cols"].tiles)
            pe.wait_ge(cond_ready, 1)
            ffn(0)
            normed_to_cols("ffn_norm0")
            pe.wait_ge(mlp_sines, 1)
            t = plan["hy_mlp2"].tiles
            mm(open_tile(t)[0:HY_FFN, 0:S], hy_small[:, HY_FFN:2 * HY_FFN], hy_h[:, 0, :], True, True, tile_full[t % 4])

            at = plan["da_qkv"]
            rows_out(at.loads, at.tiles, cols_x, 6)
            t = plan["da_turn"].tiles
            for side, src in enumerate((q_rows, k_rows)):
                for j in range(NT):
                    read_out(pe, at.tiles + (2 * side + 1) * NT + j)
                    turn_rows(t, src[:, j, :])
                    t += 2
            pe.wait_ge(padded, 1)
            for q in range(8):
                read_out(pe, plan["da_turn"].tiles + q)
            for q in range(4):
                read_out(pe, at.tiles + 8 + q)
            attention("da_att", DA_H, da_scores, lambda k, h: v_rows[:, k, h * P:(h + 1) * P], P, lambda j: j + 1)
            pe.wait_ge(heads_normed, 1)
            out_to_cols("da_cols", "da_att", DA_H)
            acc_open("da_out")
            rows_out(plan["da_out"].loads, 0, cols_x, 2, to_acc=True)
            cross_attention(0)
            ffn(1)
            normed_to_cols("ffn_norm1")
            ffn(2)

            at = plan["pool_mix"]
            landed(at.loads)
            band = ring[:, at.loads % RING, :].rearrange("p (s g t) -> p s g t", s=NT, g=4)
            pe.wait_ge(rows_ready, plan["ffn_norm2"].rows + NT)
            for g in range(4):
                o = open_tile(at.tiles + g).rearrange("p (a t) -> p a t", a=2)
                for a in range(2):
                    for s in range(NT):
                        fin = a == 1 and s == NT - 1
                        mm(o[:, a, :], rows_x[:, s, (2 * g + a) * P:(2 * g + a + 1) * P], band[:, s, g, :], s == 0,
                           s == NT - 1, tile_full[(at.tiles + g) % 4] if fin else None, done=int(fin and g == 3))
            out_at = plan["pool_out"]
            landed(out_at.loads)
            acc_open("pool_out")
            all_read(at.tiles)
            w = slot(out_at.loads, 8)
            for j in range(NT):
                for g in range(4):
                    for a in range(2):
                        fin = g == 3 and a == 1
                        mm(acc[:, 2 * j + g // 2, (g % 2) * 256:(g % 2) * 256 + 256],
                           pooled[:, 2 * g + a, j * P:(j + 1) * P], w[:, 2 * g + a, :], a == 0, a == 1,
                           acc_full if fin else None, done=int(fin and j == NT - 1))
            cross_attention(1)
            ffn(3)
            normed_to_cols("ffn_norm3")

            normed_to_cols("mod_norm0", rows_h, 2 * NT)
            pe.wait_ge(mlp_sines, 2)
            for c in range(D // HC):
                hyena_step(c)
            for q in range(2):
                read_out(pe, plan[f"hy_y{D // HC - 1}1"].tiles + q)
            at = plan["hy_out0"]
            for s in range(2):
                acc_open(f"hy_out{s}")
                for cb in range(2):
                    for half in range(2):
                        n = at.loads + 2 * cb + half
                        if s == 0:
                            landed(n)
                        w = slot(n, 4)
                        for j in range(NT):
                            for k in range(4):
                                kk = 4 * half + k
                                last = half == 1 and k == 3
                                mm(acc[:, 2 * j + cb, :], hy_z[:, kk, s * S + j * P:s * S + (j + 1) * P], w[:, k, :],
                                   kk == 0, kk == KB - 1, acc_full if last and cb == 1 else None,
                                   done=int(s == 1 and j == NT - 1 and k == 3))
            normed_to_cols("moe_norm0", rows_h, 2 * NT)
            experts(0)

            normed_to_cols("mod_norm1", rows_h, 2 * NT)
            at = plan["sw_qkv"]
            rows_out(at.loads, at.tiles, cols_x, 2)
            kv = at.tiles + 2 * NT
            n = at.loads + 4
            outs = [open_tile(kv + q) for q in range(2 * NT)]
            for half in range(2):
                landed(n + half)
                w = slot(n + half, 4)
                for q in range(2 * NT):
                    for k in range(4):
                        kk = 4 * half + k
                        mm(outs[q], cols_x[:, kk, q * P:(q + 1) * P], w[:, k, :], kk == 0, kk == KB - 1,
                           tile_full[(kv + q) % 4] if kk == KB - 1 else None, done=int(q == 2 * NT - 1 and k == 3))
            t = plan["sw_turn"].tiles
            for j in range(NT):
                read_out(pe, at.tiles + NT + j)
                turn_rows(t + 2 * j, q_rows[:, j, :])
            all_read(kv)
            t += 4
            for g in range(2):
                o = open_tile(t)
                for k in range(4):
                    turn(o[:, k * P:(k + 1) * P], sw_k_rows[:, k, g * P:(g + 1) * P], tile_full[t % 4] if k == 3 else None)
                t += 1
            for q in range(6):
                read_out(pe, plan["sw_turn"].tiles + q)
            pe.wait_ge(padded, 2)

            def sw_scores(o, j, h, signal):
                g, r = divmod(h, SW_HQ // SW_HKV)
                q = q_hi if g % 2 else q_lo
                mm(o, q[:, 4 * (g // 2) + r, j * P:(j + 1) * P], sw_k_cols[:, g // 2, :], True, True, signal)

            attention("sw_att", SW_HQ, sw_scores, lambda k, h: sw_v[:, k, (h // 4) * SW_HD:(h // 4 + 1) * SW_HD], SW_HD,
                      lambda j: 4, probs=sw_probs, turned_p=sw_turned)
            out_to_cols("sw_cols", "sw_att", SW_HQ)
            acc_open("sw_out")
            rows_out(plan["sw_out"].loads, 0, cols_x, 2, to_acc=True)
            normed_to_cols("moe_norm1", rows_h, NT)
            experts(1)

        @block.scalar
        def _(act):
            act.dma_start(consts[:, :], io["consts"]).then_inc(consts_landed, 16)
            act.dma_start(rows_x[:, NT:2 * NT, :], io["mem"][0].rearrange("(j p) d -> p j d", p=P)).then_inc(mem_landed, 16)
            act.dma_start(rows_x[:, 0:NT, :], io["x"][0].rearrange("(j p) d -> p j d", p=P)).then_inc(x_landed, 16)
            act.dma_start(act_in[:, :, :], io["cond_cols"].rearrange("p (k s) -> p k s", s=2)).then_inc(cond_landed, 16)

            def copy_tile(t, dst, src):
                filled(act, t)
                nc.scalar.activation(dst, src, ACT.Copy).then_inc(tile_read[t % 4], 1)

            def cols_from_rows(t, tok):
                for piece in range(2):
                    copy_tile(t + piece, cols_x[:, 4 * piece:4 * piece + 4, tok:tok + P],
                              work[:, (t + piece) % 4, :].rearrange("p (k t) -> p k t", k=4))

            def ffn(i):
                at = plan[f"ffn{i}"]
                ada = i < DEPTH

                def run(events, tb, it, tper):
                    tmore = 0 if it is None else it * (tper // 4)
                    for kind, what, dt, _ in events:
                        t = tb + dt
                        if kind == "in":
                            filled(act, t, tmore)
                            nc.scalar.activation(silu_buf[:, (2 * what[0] + what[1]) % 4, :], work[:, t % 4, 0:S],
                                                 ACT.Silu).then_inc(silu_ready, 1)
                        elif kind == "part":
                            filled(act, t, tmore)
                            nc.scalar.activation(ada_part[:, what % 2, :], work[:, t % 4, :],
                                                 ACT.Copy).then_inc(tile_read[t % 4], 1)

                head, t0, _ = ffn_events(range(FFN_HEAD), False)
                body, t1, _ = ffn_events(range(FFN_HEAD, FFN_HEAD + FFN_BODY), ada)
                run(head, at.tiles, None, 0)
                with act.Fori(0, FFN_LOOPS) as it:
                    run(body, at.tiles + t0, it, t1)

            def norm_root(stage, tiles=NT):
                at = plan[stage]
                act.wait_ge(var_ready, at.norms + 1)
                nc.scalar.activation(root[:, 0:tiles], spread[:, 0:tiles], ACT.Sqrt).then_inc(root_ready, 1)

            def normed_to_cols(stage, tiles=NT):
                at = plan[stage]
                for j in range(tiles):
                    cols_from_rows(at.tiles + 2 * j, j * P)

            def attention(stage, heads, exps, key_tiles, turned_p=turned_p):
                units = NT * heads
                order = attention_order(units)
                at = plan[stage]
                for v in range(units + 1):
                    if v < units:
                        act.wait_ge(low_ready, at.units + v + 1)
                        exps(v, at.tiles + order["s", v])
                    if v >= 1:
                        u = v - 1
                        t = at.tiles + order["t", u]
                        n = key_tiles(u // heads)
                        copy_tile(t, turned_p[:, u % 2, 0:n, :],
                                  work[:, t % 4, 0:n * P].rearrange("p (k t) -> p k t", k=n))

            def da_exps(u, t):
                for c in range(2):
                    ins = nc.scalar.activation(probs[:, u % 2, c * S:(c + 1) * S], masked[:, u % 2, c * S:(c + 1) * S],
                                               ACT.Exp, bias=low[:, u % 2, c:c + 1], scale=DA_DK ** -0.5,
                                               accum_out=mass[:, u % 2, c:c + 1])
                ins.then_inc(exp_ready, 1)

            def xa_exps(u, t):
                nc.scalar.activation(probs[:, u % 2, 0:S], work[:, t % 4, 0:S], ACT.Exp, bias=low[:, u % 2, 0:1],
                                     scale=XA_DK ** -0.5, accum_out=mass[:, u % 2, 0:1]).then_inc(tile_read[t % 4], 1)

            def sw_exps(u, t):
                h = u % SW_HQ
                nc.scalar.activation(sink_exp[:, u % 2:u % 2 + 1], sink[:, h:h + 1], ACT.Exp, bias=low[:, u % 2, 0:1])
                nc.scalar.activation(sw_probs[:, u % 2, :], sw_masked[:, u % 2, :], ACT.Exp, bias=low[:, u % 2, 0:1],
                                     scale=SW_HD ** -0.5, accum_out=mass[:, u % 2, 0:1]).then_inc(exp_ready, 1)

            def turned_queries(t0):
                for j in range(NT):
                    for piece in range(2):
                        t = t0 + 2 * j + piece
                        src = work[:, t % 4, :].rearrange("p (k t) -> p k t", k=4)
                        filled(act, t)
                        nc.scalar.activation(q_lo[0:64, 4 * piece:4 * piece + 4, j * P:(j + 1) * P], src[0:64], ACT.Copy)
                        nc.scalar.activation(q_hi[64:128, 4 * piece:4 * piece + 4, j * P:(j + 1) * P], src[64:128],
                                             ACT.Copy).then_inc(tile_read[t % 4], 1)

            def experts(layer):
                streams = 2 - layer
                m = CAP * streams
                tiles = NT * streams
                t = plan[f"router{layer}"].tiles
                act.wait_ge(logits_low, layer + 1)
                nc.scalar.activation(logit[:, 0:tiles, :], logit[:, 0:tiles, :], ACT.Exp).then_inc(logits_exp, 1)
                copy_tile(t + 1, aff[:, 0:tiles * P], work[0:E_N, (t + 1) % 4, 0:tiles * P])
                t = plan[f"gather{layer}"].tiles
                for s in range(streams):
                    for k in range(KB):
                        copy_tile(t, xe[s][:, k, :], work[:, t % 4, :])
                        t += 1
                per = moe_body_tiles(streams)
                base = plan[f"experts{layer}"]
                for q in range(4):
                    read_out(act, base.tiles - 1 - q)
                with act.Fori(0, E_N) as e:
                    t = base.tiles
                    more = e * (per // 4)

                    def copy(q, dst, src):
                        filled(act, t + q, more)
                        nc.scalar.activation(dst, src, ACT.Copy).then_inc(tile_read[(t + q) % 4], 1)

                    tk = taken[:, 0:KB * m].rearrange("p (k c) -> p k c", k=KB)
                    for s in range(streams):
                        ins = nc.scalar.activation(tk[:, :, s * CAP:(s + 1) * CAP], xe[s][:, :, bass.ds(e * CAP, CAP)], ACT.Copy)
                    ins.then_inc(taken_ready, 1)
                    for q in range(2):
                        copy(q, gate_part[:, q * 512:q * 512 + 512], work[:, (t + q) % 4, :])
                    for q in range(2):
                        copy(4 + q, spread_cols[:, q * streams:(q + 1) * streams, :],
                             work[:, (t + 4 + q) % 4, 0:streams * P].rearrange("p (i t) -> p i t", i=streams))
                    sv = silu_e[:, 0:KB * m].rearrange("p (k c) -> p k c", k=KB)
                    for q in range(2):
                        b = t + 6 + q
                        filled(act, b, more)
                        nc.scalar.activation(sv[:, 4 * q:4 * q + 4, :],
                                             work[:, b % 4, :].rearrange("p (k c) -> p k c", k=4)[:, :, 0:m],
                                             ACT.Silu).then_inc(tile_read[b % 4], 1)
                    copy(10, down_part[:, 0:512], work[:, (t + 10) % 4, :])

            def cross_attention(i):
                at = plan[f"xa_kv{i}"]
                for q in range(4):
                    copy_tile(at.tiles + q, k_cols[:, 2 * q:2 * q + 2, :],
                              work[:, (at.tiles + q) % 4, :].rearrange("p (a t) -> p a t", a=2))
                for q in range(4):
                    copy_tile(at.tiles + 4 + q, v_rows[:, q % 2, (q // 2) * 512:(q // 2) * 512 + 512],
                              work[:, (at.tiles + q) % 4, :])
                norm_root(f"mix_norm{i}")
                normed_to_cols(f"mix_norm{i}")
                at = plan[f"xa_q{i}"]
                for q in range(4):
                    copy_tile(at.tiles + q, q_lo[:, 2 * q:2 * q + 2, :],
                              work[:, (at.tiles + q) % 4, :].rearrange("p (a t) -> p a t", a=2))
                attention(f"xa_att{i}", XA_H, xa_exps, lambda j: NT)
                normed_to_cols(f"xa_cols{i}")
                norm_root(f"xa_norm{i}")
                normed_to_cols(f"xa_norm{i}")

            act.wait_ge(cond_landed, 16)
            act.wait_ge(cond_zeroed, 1)
            nc.scalar.activation(act_col[:, :, 0:2], act_in[:, :, :], ACT.Silu).then_inc(cond_ready, 1)
            for j in range(NT):
                cols_from_rows(plan["mem_cols"].tiles + 2 * j, S + j * P)
            normed_to_cols("x_cols")
            act.wait_ge(mlp_angles, 1)
            nc.scalar.activation(hy_h[:, 0, :], hy_h[:, 0, :], ACT.Sin).then_inc(mlp_sines, 1)
            ffn(0)
            act.wait_ge(angles_ready, 1)
            nc.scalar.activation(da_cs[:, :, :, :], angle[:, :, :, :], ACT.Sin).then_inc(sines_ready, 1)
            act.wait_ge(lam_sums, 1)
            nc.scalar.activation(lam[:, 2:4], lam[:, 0:2], ACT.Exp).then_inc(lam_exp, 1)
            norm_root("ffn_norm0")
            normed_to_cols("ffn_norm0")
            act.wait_ge(mlp_angles, 2)
            nc.scalar.activation(hy_h[:, 1, :], hy_h[:, 1, :], ACT.Sin).then_inc(mlp_sines, 1)

            turned_at = plan["da_turn"].tiles
            act.wait_ge(padded, 1)
            turned_queries(turned_at)
            for j in range(NT):
                for piece in range(2):
                    t = turned_at + 4 + 2 * j + piece
                    copy_tile(t, k_cols[:, 4 * piece:4 * piece + 4, j * P:(j + 1) * P],
                              work[:, t % 4, :].rearrange("p (k t) -> p k t", k=4))
            attention("da_att", DA_H, da_exps, lambda j: j + 1)
            act.wait_ge(var_ready, plan["da_cols"].norms + 1)
            nc.scalar.activation(head_sq[:, 1, :], head_sq[:, 0, :], ACT.Sqrt).then_inc(root_ready, 1)
            normed_to_cols("da_cols")
            cross_attention(0)
            ffn(1)
            norm_root("ffn_norm1")
            normed_to_cols("ffn_norm1")
            ffn(2)
            norm_root("ffn_norm2")
            at = plan["pool_mix"]
            for q in range(4):
                copy_tile(at.tiles + q, pooled[:, 2 * q:2 * q + 2, :],
                          work[:, (at.tiles + q) % 4, :].rearrange("p (a t) -> p a t", a=2))
            cross_attention(1)
            ffn(3)
            norm_root("ffn_norm3")
            normed_to_cols("ffn_norm3")

            norm_root("mod_norm0", 2 * NT)
            normed_to_cols("mod_norm0", 2 * NT)
            for c in range(D // HC):
                t = plan[f"hy_u{c}"].tiles
                convs = plan[f"hy_u{c}"].convs

                def add_bias(section):
                    nonlocal t
                    for a in range(2):
                        done = 2 * section + a
                        filled(act, t)
                        if done >= 2:
                            act.wait_ge(conv_ready, convs + done - 1)
                        b = section * KB + 2 * c + a
                        nc.scalar.activation(hy_biased[:, a, :], work[:, t % 4, :], ACT.Identity,
                                             bias=hy_cols[:, b, 0:1]).then_inc(tile_read[t % 4], 1)
                        t += 1

                def copy_turned(dst):
                    nonlocal t
                    for j in range(NT):
                        copy_tile(t, dst[:, j, :], work[:, t % 4, :])
                        t += 1

                add_bias(0)
                add_bias(1)
                copy_turned(hy_v)
                add_bias(2)
                copy_turned(hy_x1)
            norm_root("moe_norm0", 2 * NT)
            normed_to_cols("moe_norm0", 2 * NT)
            experts(0)

            norm_root("mod_norm1", 2 * NT)
            normed_to_cols("mod_norm1", 2 * NT)
            at = plan["sw_qkv"]
            t = plan["sw_turn"].tiles
            act.wait_ge(padded, 2)
            turned_queries(t)
            for g in range(2):
                copy_tile(t + 4 + g, sw_k_cols[:, g, :], work[:, (t + g) % 4, :])
            attention("sw_att", SW_HQ, sw_exps, lambda j: 4, turned_p=sw_turned)
            normed_to_cols("sw_cols")
            norm_root("moe_norm1", NT)
            normed_to_cols("moe_norm1", NT)
            experts(1)
            norm_root("last_norm", NT)

        @block.vector
        def _(dve):
            step = Steps(dve, vec_steps)
            next_row = [0]

            def param_row():
                r = next_row[0]
                next_row[0] += 1
                dve.wait_ge(row_landed[r % PR_RING], 16 * (r // PR_RING + 1))
                return prow[:, r % PR_RING, :]

            def newton_root(v, s, r, tmp):
                step(nc.vector.reciprocal(r, s))
                step.settle()
                step(nc.vector.tensor_tensor(tmp, r, r, ALU.mult))
                step.settle()
                step(nc.vector.tensor_tensor(tmp, tmp, v, ALU.mult))
                step.settle()
                step(nc.vector.tensor_scalar(tmp, tmp, -0.5, 1.5, ALU.mult, ALU.add))
                step.settle()
                step(nc.vector.tensor_tensor(r, r, tmp, ALU.mult))
                step.settle()

            def ffn(i):
                at = plan[f"ffn{i}"]
                ada = i < DEPTH

                def run(events, tb, it, tper):
                    tmore = 0 if it is None else it * (tper // 4)
                    smore = 0 if it is None else it * (2 * FFN_BODY)
                    cmore = 0 if it is None else it * ADA_PER_BODY
                    for kind, what, dt, _ in events:
                        t = tb + dt
                        if kind == "in":
                            m = 2 * what[0] + what[1]
                            dve.wait_ge(silu_ready, at.silu + m + 1 + smore)
                            nc.vector.tensor_tensor(gated[:, m % 4, :], silu_buf[:, m % 4, :], work[:, t % 4, S:2 * S],
                                                    ALU.mult).then_inc(tile_read[t % 4], 1)
                        elif kind == "sum":
                            filled(dve, t, tmore)
                            there = mods[0:2, bass.ds((what + cmore) * 512, 512)]
                            nc.vector.tensor_tensor(there, there, work[0:2, t % 4, :],
                                                    ALU.add).then_inc(tile_read[t % 4], 1)

                if ada:
                    dve.wait_ge(ada_bias_landed, 16 * (i + 1))
                head, t0, _ = ffn_events(range(FFN_HEAD), False)
                body, t1, _ = ffn_events(range(FFN_HEAD, FFN_HEAD + FFN_BODY), ada)
                run(head, at.tiles, None, 0)
                with dve.Fori(0, FFN_LOOPS) as it:
                    run(body, at.tiles + t0, it, t1)

            def layer_norm(stage, acc_stage, x_scale, eps, prepare=None):
                at, use = plan[stage], plan[acc_stage].acc
                for j in range(NT):
                    dve.wait_ge(acc_full, NT * use + j + 1)
                    if prepare is not None:
                        prepare(j)
                    else:
                        for h in range(2):
                            x = rows_x[:, j, h * 512:(h + 1) * 512]
                            ins = nc.vector.scalar_tensor_tensor(out=x, in0=x, scalar=x_scale, in1=acc[:, 2 * j + h, :],
                                                                 op0=ALU.mult, op1=ALU.add)
                        ins.then_inc(acc_read, 1)
                        dve.wait_ge(acc_read, NT * use + j + 1)
                    for h in range(2):
                        step(nc.vector.bn_stats(stats[:, j, h, :], rows_x[:, j, h * 512:(h + 1) * 512]))
                    step.settle()
                    step(nc.vector.bn_aggr(mean_var[:, j, :], stats[:, j, :, :]))
                step.settle()
                nc.vector.tensor_scalar(spread[:, 0:NT], mean_var[:, 0:NT, 1], eps, None, ALU.add).then_inc(var_ready, 1)
                dve.wait_ge(root_ready, at.norms + 1)
                newton_root(spread[:, 0:NT], root[:, 0:NT], rstd[:, 0:NT], newton[:, 0:NT])
                gain, bias = param_row(), param_row()
                for j in range(NT):
                    x = rows_x[:, j, :]
                    step(nc.vector.tensor_scalar(x, x, mean_var[:, j, 0:1], rstd[:, j:j + 1], ALU.subtract, ALU.mult))
                    step.settle()
                    ins = nc.vector.tensor_tensor(x, x, gain, ALU.mult)
                    if j == NT - 1:
                        ins.then_inc(rows_used, 1)
                        dve.wait_ge(rows_used, next_row[0] - 1)
                    else:
                        step(ins)
                        step.settle()
                    ins = nc.vector.tensor_tensor(x, x, bias, ALU.add)
                    ins.then_inc(rows_ready, 1)
                dve.wait_ge(rows_ready, at.rows + NT)
                nc.vector.tensor_copy(newton[:, 0:1], bias[:, 0:1]).then_inc(rows_used, 1)

            def mod_norm(stage, streams, last=False):
                at = plan[stage]
                tiles = NT * streams
                for i in range(tiles):
                    for h in range(2):
                        step(nc.vector.bn_stats(stats[:, i % 2, h, :], rows_x[:, i, h * 512:(h + 1) * 512]))
                    step.settle()
                    step(nc.vector.bn_aggr(mean_var[:, i, :], stats[:, i % 2, :, :]))
                    step.settle()
                step(nc.vector.tensor_tensor(spread[:, 0:tiles], mean_var[:, 0:tiles, 0], mean_var[:, 0:tiles, 0], ALU.mult))
                step.settle()
                nc.vector.scalar_tensor_tensor(out=spread[:, 0:tiles], in0=mean_var[:, 0:tiles, 1], scalar=EPS,
                                               in1=spread[:, 0:tiles], op0=ALU.add, op1=ALU.add).then_inc(var_ready, 1)
                dve.wait_ge(root_ready, at.norms + 1)
                newton_root(spread[:, 0:tiles], root[:, 0:tiles], rstd[:, 0:tiles], newton[:, 0:tiles])
                for s in range(streams):
                    gain = param_row()
                    if not last:
                        scale, shift = param_row(), param_row()
                    for j in range(NT):
                        i = NT * s + j
                        x, h = rows_x[:, i, :], rows_h[:, i, :]
                        ins = nc.vector.scalar_tensor_tensor(out=h, in0=x, scalar=rstd[:, i:i + 1], in1=gain,
                                                             op0=ALU.mult, op1=ALU.mult)
                        if last:
                            ins.then_inc(rows_ready, 1)
                            continue
                        step(ins)
                        step.settle()
                        step(nc.vector.scalar_tensor_tensor(out=h, in0=scale, scalar=1.0, in1=h, op0=ALU.add, op1=ALU.mult))
                        step.settle()
                        nc.vector.tensor_tensor(h, h, shift, ALU.add).then_inc(rows_ready, 1)
                    if not last:
                        give_back(3, at.rows + NT * (s + 1))

            def give_back(n, normed=None):
                if normed is not None:
                    dve.wait_ge(rows_ready, normed)
                step.settle()
                nc.vector.tensor_copy(newton[:, 0:1], rstd[:, 0:1]).then_inc(rows_used, n)
                dve.wait_ge(rows_used, next_row[0])

            def attention(stage, heads, begin, weigh, width):
                units = NT * heads
                order = attention_order(units)
                at = plan[stage]
                for v in range(units + 2):
                    if v < units:
                        begin(v, at.tiles + order["s", v], v // heads, v % heads)
                    if 0 <= v - 1 < units:
                        weigh(v - 1, at)
                    if v >= 2:
                        u = v - 2
                        j, h = divmod(u, heads)
                        t = at.tiles + order["o", u]
                        filled(dve, t)
                        nc.vector.tensor_copy(q_rows[:, j, h * width:(h + 1) * width],
                                              work[:, t % 4, 0:width]).then_inc(tile_read[t % 4], 1)

            def da_begin(u, t, j, h):
                filled(dve, t)
                m = masked[:, u % 2, :].rearrange("p (c k) -> p c k", c=2)
                nc.vector.tensor_tensor(m, work[:, t % 4, :].rearrange("p (c k) -> p c k", c=2),
                                        mask[:, j:j + 1, :].broadcast_to([P, 2, S]), ALU.add).then_inc(tile_read[t % 4], 1)
                read_out(dve, t)
                step(nc.vector.tensor_reduce(peak[:, u % 2, :], m, AX_X, ALU.max))
                step.settle()
                nc.vector.tensor_scalar(low[:, u % 2, :], peak[:, u % 2, :], -DA_DK ** -0.5, None,
                                        ALU.mult).then_inc(low_ready, 1)

            def da_weigh(u, at):
                dve.wait_ge(exp_ready, at.units + u + 1)
                s = share[:, u % 2, :]
                step(nc.vector.reciprocal(s, mass[:, u % 2, :]))
                step.settle()
                step(nc.vector.tensor_tensor(s[:, 1:2], s[:, 1:2], lam[:, 0:1], ALU.mult))
                first, second = probs[:, u % 2, 0:S], probs[:, u % 2, S:2 * S]
                step(nc.vector.tensor_scalar(first, first, s[:, 0:1], None, ALU.mult))
                step.settle()
                nc.vector.scalar_tensor_tensor(out=first, in0=second, scalar=s[:, 1:2], in1=first, op0=ALU.mult,
                                               op1=ALU.add).then_inc(share_ready, 1)

            def xa_begin(u, t, j, h):
                filled(dve, t)
                step(nc.vector.tensor_reduce(peak[:, u % 2, 0:1], work[:, t % 4, 0:S], AX_X, ALU.max))
                step.settle()
                nc.vector.tensor_scalar(low[:, u % 2, 0:1], peak[:, u % 2, 0:1], -XA_DK ** -0.5, None,
                                        ALU.mult).then_inc(low_ready, 1)

            def xa_weigh_at(stage):
                order = attention_order(NT * XA_H)

                def weigh(u, at):
                    read_out(dve, at.tiles + order["s", u])
                    step(nc.vector.reciprocal(share[:, u % 2, 0:1], mass[:, u % 2, 0:1]))
                    step.settle()
                    p = probs[:, u % 2, 0:S]
                    nc.vector.tensor_scalar(p, p, share[:, u % 2, 0:1], None, ALU.mult).then_inc(share_ready, 1)

                return weigh

            def cross_attention(i):
                attention(f"xa_att{i}", XA_H, xa_begin, xa_weigh_at(i), XA_DK)
                layer_norm(f"xa_norm{i}", f"xa_out{i}", ALPHA, LN_EPS)

            def wrapped_angle(a, turns):
                step(nc.vector.tensor_scalar(turns, turns, MAGIC, MAGIC, ALU.add, ALU.subtract))
                step.settle()
                for part in two_pi_parts():
                    step(nc.vector.scalar_tensor_tensor(out=a, in0=turns, scalar=-part, in1=a, op0=ALU.mult, op1=ALU.add))
                    step.settle()

            def mlp_layer(n):
                t = plan[f"hy_mlp{n + 1}"].tiles
                filled(dve, t)
                a = hy_h[:, n, :]
                c = 2 * HY_FFN
                nc.vector.tensor_scalar(a, work[0:HY_FFN, t % 4, 0:S], hy_small[:, c + n:c + n + 1],
                                        hy_small[:, c + 2 + n:c + 3 + n], ALU.add, ALU.mult).then_inc(tile_read[t % 4], 1)
                read_out(dve, t)
                turns = mlp_turns[:, :]
                step(nc.vector.tensor_scalar(turns, a, 1.0 / TWO_PI, None, ALU.mult))
                step.settle()
                wrapped_angle(a, turns)
                nc.vector.tensor_scalar(a, a, PI_BELOW, -PI_BELOW, ALU.min, ALU.max).then_inc(mlp_angles, 1)

            def hyena_step(c, biases):
                t = plan[f"hy_u{c}"].tiles
                for section in range(3):
                    if section == 2:
                        t += NT
                    for a in range(2):
                        m = 2 * section + a
                        b = section * KB + 2 * c + a
                        read_out(dve, t)
                        x = hy_biased[:, a, :].rearrange("p (s t) -> p s t", s=2)
                        y = (hy_y[:, m, :] if section < 2 else hy_x2[:, a, :]).rearrange("p (s t) -> p s t", s=2)
                        step(nc.vector.tensor_scalar(y, x, hy_cols[:, b, 3:4], hy_cols[:, b, 1:2], ALU.mult, ALU.add))
                        step.settle()
                        step(nc.vector.scalar_tensor_tensor(out=y[:, :, 1:S], in0=x[:, :, 0:S - 1], scalar=hy_cols[:, b, 2:3],
                                                            in1=y[:, :, 1:S], op0=ALU.mult, op1=ALU.add))
                        step.settle()
                        nc.vector.scalar_tensor_tensor(out=y[:, :, 0:S - 1], in0=x[:, :, 1:S], scalar=hy_cols[:, b, 4:5],
                                                       in1=y[:, :, 0:S - 1], op0=ALU.mult, op1=ALU.add).then_inc(conv_ready, 1)
                        t += 1
                dve.wait_ge(conv_ready, plan[f"hy_u{c}"].convs + 6)
                dve.wait_ge(window_landed, 16 * (c + 1))
                for o in range(2):
                    at = plan[f"hy_k{c}{o}"]
                    t = at.tiles
                    tmp = hy_tmp.rearrange("p (a c) -> p a c", a=2)
                    for j in range(NT):
                        filled(dve, t)
                        src = work[:, t % 4, :].rearrange("p (a c) -> p a c", a=2)
                        step(nc.vector.tensor_tensor(tmp[:, 0, :], src[:, 0, :], hy_window[:, j, :], ALU.mult))
                        nc.vector.scalar_tensor_tensor(out=tmp[:, 1, :], in0=src[:, 1, :], scalar=const("not_first")[:, j:j + 1],
                                                       in1=hy_window[:, j, :], op0=ALU.mult,
                                                       op1=ALU.mult).then_inc(tile_read[t % 4], 1)
                        read_out(dve, t)
                        step.settle()
                        step(nc.vector.tensor_tensor(hy_lags[:, j, 0:HC], tmp[:, 0, :], tmp[:, 1, :], ALU.add))
                        nc.vector.tensor_tensor(hy_lags[:, j, HC:2 * HC], tmp[:, 0, :], tmp[:, 1, :],
                                                ALU.subtract).then_inc(lags_ready, 1)
                        dve.wait_ge(lags_ready, at.lags + j + 1)
                        step.settle()
                        t += 1
                    for f in range(NT):
                        filled(dve, t)
                        src = work[:, t % 4, :].rearrange("p (a c) -> p a c", a=2)
                        step(nc.vector.tensor_tensor(hy_k[:, f, 0, :], src[:, 0, :], biases[o][:, c * HC:(c + 1) * HC], ALU.add))
                        nc.vector.tensor_copy(hy_k[:, f, 1, :], src[:, 1, :]).then_inc(tile_read[t % 4], 1)
                        read_out(dve, t)
                        t += 1
                    step.settle()
                    at = plan[f"hy_v{c}{o}"]
                    t = at.tiles
                    both = hy_tmp.rearrange("p (s c) -> p s c", s=2)
                    for f in range(NT):
                        vr = work[:, t % 4, :].rearrange("p (s c) -> p s c", s=2)
                        vi = work[:, (t + 1) % 4, :].rearrange("p (s c) -> p s c", s=2)
                        kr = hy_k[:, f, 0:1, :].broadcast_to([P, 2, HC])
                        ki = hy_k[:, f, 1:2, :].broadcast_to([P, 2, HC])
                        yr = hy_spec[:, f, 0, :].rearrange("p (s c) -> p s c", s=2)
                        yi = hy_spec[:, f, 1, :].rearrange("p (s c) -> p s c", s=2)
                        filled(dve, t)
                        step(nc.vector.tensor_tensor(yr, vr, kr, ALU.mult))
                        nc.vector.tensor_tensor(yi, vr, ki, ALU.mult).then_inc(tile_read[t % 4], 1)
                        filled(dve, t + 1)
                        step(nc.vector.tensor_tensor(both, vi, ki, ALU.mult))
                        step.settle()
                        step(nc.vector.tensor_tensor(yr, yr, both, ALU.subtract))
                        step.settle()
                        nc.vector.tensor_tensor(both, vi, kr, ALU.mult).then_inc(tile_read[(t + 1) % 4], 1)
                        read_out(dve, t)
                        read_out(dve, t + 1)
                        nc.vector.tensor_tensor(yi, yi, both, ALU.add).then_inc(spectra_ready, 1)
                        dve.wait_ge(spectra_ready, at.spectra + f + 1)
                        t += 2
                    t = plan[f"hy_y{c}{o}"].tiles
                    for b in range(2):
                        filled(dve, t)
                        if o == 0:
                            if b == 0:
                                for q in (8, 9):
                                    read_out(dve, plan[f"hy_u{c}"].tiles + q)
                            nc.vector.tensor_tensor(hy_v[:, b, :], work[:, t % 4, :], hy_x1[:, b, :],
                                                    ALU.mult).then_inc(tile_read[t % 4], 1)
                        else:
                            nc.vector.tensor_tensor(hy_z[:, 2 * c + b, :], work[:, t % 4, :], hy_x2[:, b, :],
                                                    ALU.mult).then_inc(tile_read[t % 4], 1)
                        t += 1
                nc.vector.tensor_copy(newton[:, 0:1], hy_window[:, 0, 0:1]).then_inc(filters_done, 1)

            def modulated_sum(src, j, i, scale, signal=None, count=None, bias=None):
                step.settle()
                if bias is not None:
                    ins = nc.vector.tensor_tensor(mix_tmp, src, bias, ALU.add)
                    scaled = mix_tmp
                    if signal is not None:
                        ins.then_inc(signal, 1)
                        dve.wait_ge(signal, count)
                    else:
                        step(ins)
                        step.settle()
                    step(nc.vector.tensor_tensor(mix_tmp, mix_tmp, scale, ALU.mult))
                else:
                    ins = nc.vector.tensor_tensor(mix_tmp, src, scale, ALU.mult)
                    if signal is not None:
                        ins.then_inc(signal, 1)
                        dve.wait_ge(signal, count)
                    else:
                        step(ins)
                step.settle()
                step(nc.vector.tensor_tensor(rows_x[:, i, :], rows_x[:, i, :], mix_tmp, ALU.add))

            def experts(layer):
                streams = 2 - layer
                m = CAP * streams
                groups = P // m
                tiles = NT * streams
                t = plan[f"router{layer}"].tiles
                filled(dve, t)
                src = work[:, t % 4, 0:tiles * E_N].rearrange("p (i e) -> p i e", i=tiles)
                lg = logit[:, 0:tiles, :]
                pk = logit_peak[:, 0:tiles]
                step(nc.vector.tensor_reduce(pk, src, AX_X, ALU.max))
                step.settle()
                nc.vector.tensor_tensor(lg, src, pk.unsqueeze(2).broadcast_to([P, tiles, E_N]), ALU.subtract)                    .then_inc(tile_read[t % 4], 1)
                read_out(dve, t)
                nc.vector.tensor_copy(newton[:, 0:1], pk[:, 0:1]).then_inc(logits_low, 1)
                dve.wait_ge(logits_exp, layer + 1)
                step(nc.vector.tensor_reduce(pk, lg, AX_X, ALU.add))
                step.settle()
                step(nc.vector.reciprocal(pk, pk))
                step.settle()
                nc.vector.tensor_tensor(gate[:, 0:tiles, :], lg, pk.unsqueeze(2).broadcast_to([P, tiles, E_N]), ALU.mult)                    .then_inc(gates_ready, 1)
                step(nc.vector.memset(zeros16, 0.0))
                read_out(dve, t + 1)
                step(nc.vector.tensor_copy(left[:, 0:tiles * P], aff[:, 0:tiles * P]))
                step.settle()
                for s in range(streams):
                    mine = left[:, s * S:(s + 1) * S]
                    for _ in range(CAP // 8):
                        step(nc.vector.max(top8[:, :], mine))
                        step.settle()
                        step(nc.vector.match_replace(mine, top8[:, :], mine, -1.0))
                        step.settle()
                step(nc.vector.tensor_scalar(picked[:, 0:tiles * P], left[:, 0:tiles * P], 0.0, None, ALU.is_lt))
                step.settle()
                for s in range(streams):
                    step(nc.vector.tensor_tensor_scan(count[:, s * S:(s + 1) * S], picked[:, s * S:(s + 1) * S],
                                                      zeros16[:, 0:S], 0.0, ALU.add, ALU.add))
                step.settle()
                nc.vector.tensor_tensor(picked[:, 0:tiles * P], picked[:, 0:tiles * P], count[:, 0:tiles * P], ALU.mult)                    .then_inc(codes_ready, 1)
                filled(dve, t + 2)
                nc.vector.tensor_copy(codes[:, 0:tiles, :], work[:, (t + 2) % 4, 0:tiles * E_N].rearrange("p (i e) -> p i e", i=tiles))                    .then_inc(tile_read[(t + 2) % 4], 1)
                read_out(dve, t + 2)
                for i in range(tiles):
                    ins = nc.vector.tensor_tensor(chosen[:, i, :].rearrange("p (e c) -> p e c", e=E_N),
                                                  codes[:, i, :].unsqueeze(2).broadcast_to([P, E_N, CAP]),
                                                  const("iota").unsqueeze(1).broadcast_to([P, E_N, CAP]), ALU.is_equal)
                    if i < tiles - 1:
                        step(ins)
                ins.then_inc(choice_ready, 1)
                dve.wait_ge(choice_ready, layer + 1)
                per = moe_body_tiles(streams)
                base = plan[f"experts{layer}"]
                read_out(dve, base.tiles - 1)
                step(nc.vector.memset(rows_h[:, 0:tiles, :], 0.0))
                step(nc.vector.memset(spread_e[:, :, :], 0.0))
                step.settle()
                n_steps = tiles + 2
                with dve.Fori(0, E_N) as e:
                    t = base.tiles
                    more = e * (per // 4)
                    for i in range(tiles):
                        s = i // NT
                        dst = spread_e[:, i, :].rearrange("p (g s c) -> p g s c", g=groups, s=streams)[:, :, s, :]
                        ins = nc.vector.tensor_scalar(dst, const("iota").unsqueeze(1).broadcast_to([P, groups, CAP]),
                                                      codes[:, i, bass.ds(e, 1)], gate[:, i, bass.ds(e, 1)],
                                                      ALU.is_equal, ALU.mult)
                    ins.then_inc(spread_ready, 1)
                    for q in range(2):
                        b = t + 2 + q
                        filled(dve, b, more)
                        nc.vector.tensor_copy(up_part[:, q * 512:q * 512 + 512], work[:, b % 4, :]).then_inc(tile_read[b % 4], 1)
                    gv = gated_e[:, 0:KB * m].rearrange("p (k c) -> p k c", k=KB)
                    sv = silu_e[:, 0:KB * m].rearrange("p (k c) -> p k c", k=KB)
                    for q in range(2):
                        b = t + 8 + q
                        filled(dve, b, more)
                        read_out(dve, t + 6 + q, more)
                        nc.vector.tensor_tensor(gv[:, 4 * q:4 * q + 4, :], sv[:, 4 * q:4 * q + 4, :],
                                                work[:, b % 4, :].rearrange("p (k c) -> p k c", k=4)[:, :, 0:m],
                                                ALU.mult).then_inc(tile_read[b % 4], 1)
                    b = t + 11
                    filled(dve, b, more)
                    nc.vector.tensor_copy(down_part[:, 512:1024], work[:, b % 4, :]).then_inc(tile_read[b % 4], 1)
                    for cb in range(2):
                        for i in range(tiles):
                            b = t + 12 + tiles * cb + i
                            filled(dve, b, more)
                            there = rows_h[:, i, cb * 512:cb * 512 + 512]
                            nc.vector.tensor_tensor(there, there, work[:, b % 4, :], ALU.add).then_inc(tile_read[b % 4], 1)
                for q in range(4):
                    read_out(dve, base.tiles + E_N * per - 1 - q)
                for s in range(streams):
                    scale = param_row()
                    for j in range(NT):
                        modulated_sum(rows_h[:, NT * s + j, :], j, NT * s + j, scale)
                    give_back(1)

            step(nc.vector.memset(act_col[:, :, :], 0.0))
            step.settle()
            nc.vector.memset(newton[:, :], 0.0).then_inc(cond_zeroed, 1)

            dve.wait_ge(consts_landed, 16)
            dve.wait_ge(small_landed, 16 * 4)
            step(nc.vector.tensor_copy(pos_f[:, :], pos_i[:, :]))
            step.settle()
            for c in range(2):
                for j in range(NT):
                    step(nc.vector.tensor_scalar(angle[:, c, j, :], const("da_inv"), pos_f[:, j:j + 1], None, ALU.mult))
            step.settle()
            for c in range(2):
                step(nc.vector.tensor_scalar(turns[:, c, :, :], angle[:, c, :, :], 1.0 / TWO_PI, 0.25 * (1 - c), ALU.mult, ALU.add))
            step.settle()
            step(nc.vector.tensor_scalar(turns[:, :, :, :], turns[:, :, :, :], MAGIC, MAGIC, ALU.add, ALU.subtract))
            step.settle()
            for part in two_pi_parts():
                step(nc.vector.scalar_tensor_tensor(out=angle[:, :, :, :], in0=turns[:, :, :, :], scalar=-part,
                                                    in1=angle[:, :, :, :], op0=ALU.mult, op1=ALU.add))
                step.settle()
            step(nc.vector.tensor_scalar(angle[:, 0, :, :], angle[:, 0, :, :], math.pi / 2, None, ALU.add))
            step.settle()
            nc.vector.tensor_scalar(angle[:, :, :, :], angle[:, :, :, :], PI_BELOW, -PI_BELOW, ALU.min, ALU.max)\
                .then_inc(angles_ready, 1)
            step(nc.vector.tensor_tensor(lam_in[:, 0, :], lam_in[:, 0, :], lam_in[:, 1, :], ALU.mult))
            step(nc.vector.tensor_scalar(subln[:, :], subln[:, :], 1.0 - LAM_INIT, None, ALU.mult))
            step.settle()
            nc.vector.tensor_reduce(lam[:, 0:2], lam_in[:, 0, :].rearrange("p (c d) -> p c d", c=2), AX_X, ALU.add)\
                .then_inc(lam_sums, 1)
            dve.wait_ge(hy_landed, 16 * 3)
            mlp_layer(0)
            ffn(0)
            dve.wait_ge(lam_exp, 1)
            step(nc.vector.tensor_tensor(lam[:, 0:1], lam[:, 3:4], lam[:, 2:3], ALU.subtract))
            step.settle()
            step(nc.vector.tensor_scalar(lam[:, 0:1], lam[:, 0:1], -LAM_INIT, None, ALU.add))
            layer_norm("ffn_norm0", "ffn0", 2.0 * ALPHA, 4.0 * LN_EPS)

            mlp_layer(1)

            dve.wait_ge(sines_ready, 1)
            dve.wait_ge(mods_stored, 16)
            step(nc.vector.memset(q_lo[64:128, :, :], 0.0))
            nc.vector.memset(q_hi[0:64, :, :], 0.0).then_inc(padded, 1)
            at = plan["da_qkv"]
            for cb in range(6):
                for j in range(NT):
                    t = at.tiles + NT * cb + j
                    filled(dve, t)
                    c0 = (cb % 2) * 512
                    if cb < 4:
                        dst = (q_rows if cb < 2 else k_rows)[:, j, c0:c0 + 512].rearrange("p (h c d) -> p h c d", c=2, d=32)
                        src = work[:, t % 4, :].rearrange("p (h c d) -> p h c d", c=2, d=32)
                        tmp = rope_tmp.rearrange("p (h c d) -> p h c d", c=2, d=32)
                        sin = da_cs[:, 1, j:j + 1, :].broadcast_to([P, 8, 32])
                        cos = da_cs[:, 0, j:j + 1, :].broadcast_to([P, 8, 32])
                        if t > at.tiles:
                            step.settle()
                            read_out(dve, t - 1)
                        for c in range(2):
                            step(nc.vector.tensor_tensor(dst[:, :, c, :], src[:, :, c, :], cos, ALU.mult))
                            step(nc.vector.tensor_tensor(tmp[:, :, c, :], src[:, :, 1 - c, :], sin, ALU.mult))
                        step.settle()
                        step(nc.vector.tensor_tensor(dst[:, :, 0, :], dst[:, :, 0, :], tmp[:, :, 0, :], ALU.subtract))
                        nc.vector.tensor_tensor(dst[:, :, 1, :], dst[:, :, 1, :], tmp[:, :, 1, :], ALU.add)\
                            .then_inc(tile_read[t % 4], 1)
                    else:
                        nc.vector.tensor_copy(v_rows[:, j, c0:c0 + 512], work[:, t % 4, :]).then_inc(tile_read[t % 4], 1)
            dve.wait_ge(mask_landed, 16)
            attention("da_att", DA_H, da_begin, da_weigh, 2 * DA_DK)
            read_last = plan["da_att"].tiles + attention_order(NT * DA_H)["o", NT * DA_H - 1]
            read_out(dve, read_last)
            for j in range(NT):
                step(nc.vector.tensor_tensor(k_rows[:, j, :], q_rows[:, j, :], q_rows[:, j, :], ALU.mult))
            step.settle()
            step(nc.vector.tensor_reduce(head_sq[:, 0, :], k_rows.rearrange("p j (h d) -> p (j h) d", h=DA_H), AX_X, ALU.add))
            step.settle()
            nc.vector.tensor_scalar(head_sq[:, 0, :], head_sq[:, 0, :], 1.0 / (2 * DA_DK), LN_EPS, ALU.mult, ALU.add)\
                .then_inc(var_ready, 1)
            dve.wait_ge(root_ready, plan["da_cols"].norms + 1)
            newton_root(head_sq[:, 0, :], head_sq[:, 1, :], head_sq[:, 2, :], head_tmp[:, :])
            heads = q_rows.rearrange("p j (h d) -> p (j h) d", h=DA_H)
            step(nc.vector.tensor_tensor(heads, heads, head_sq[:, 2, :].unsqueeze(2).broadcast_to([P, NT * DA_H, 2 * DA_DK]), ALU.mult))
            step.settle()
            nc.vector.tensor_tensor(heads, heads, subln[:, :].unsqueeze(1).broadcast_to([P, NT * DA_H, 2 * DA_DK]), ALU.mult)\
                .then_inc(heads_normed, 1)
            layer_norm("mix_norm0", "da_out", ALPHA, LN_EPS)
            cross_attention(0)
            ffn(1)
            dve.wait_ge(mods_stored, 32)
            layer_norm("ffn_norm1", "ffn1", 2.0 * ALPHA, 4.0 * LN_EPS)
            ffn(2)
            layer_norm("ffn_norm2", "ffn2", 2.0 * ALPHA, 4.0 * LN_EPS)

            pool_bias, pool_scale = param_row(), param_row()

            def pool_residual(j):
                use = plan["pool_out"].acc
                nc.vector.tensor_tensor(pool_y, acc[:, 2 * j:2 * j + 2, :].rearrange("p a c -> p (a c)"), pool_bias,
                                        ALU.add).then_inc(acc_read, 1)
                dve.wait_ge(acc_read, NT * use + j + 1)
                ins = nc.vector.tensor_tensor(pool_y, pool_y, pool_scale, ALU.mult)
                step(ins)
                step.settle()
                x = rows_x[:, j, :]
                ins = nc.vector.scalar_tensor_tensor(out=x, in0=x, scalar=ALPHA, in1=pool_y, op0=ALU.mult, op1=ALU.add)
                if j == NT - 1:
                    ins.then_inc(rows_used, 2)
                    dve.wait_ge(rows_used, next_row[0])
                else:
                    step(ins)
                    step.settle()

            layer_norm("mix_norm1", "pool_out", ALPHA, LN_EPS, prepare=pool_residual)
            cross_attention(1)
            ffn(3)
            layer_norm("ffn_norm3", "ffn3", 2.0 * ALPHA, 4.0 * LN_EPS)

            dve.wait_ge(rows_ready, plan["ffn_norm3"].rows + NT)
            dve.wait_ge(ctx_landed, 16)
            mod_norm("mod_norm0", 2)
            biases = [param_row(), param_row()]
            for c in range(D // HC):
                hyena_step(c, biases)
            dve.wait_ge(filters_done, D // HC)
            give_back(2)
            scales = [param_row()]
            out_bias = param_row()
            scales.append(param_row())
            for s in range(2):
                at = plan[f"hy_out{s}"]
                for j in range(NT):
                    dve.wait_ge(acc_full, NT * at.acc + j + 1)
                    modulated_sum(acc[:, 2 * j:2 * j + 2, :].rearrange("p a c -> p (a c)"), j, NT * s + j, scales[s],
                                  acc_read, NT * at.acc + j + 1, bias=out_bias)
            give_back(3)
            mod_norm("moe_norm0", 2)
            experts(0)

            mod_norm("mod_norm1", 2)
            step(nc.vector.memset(q_lo[64:128, :, :], 0.0))
            nc.vector.memset(q_hi[0:64, :, :], 0.0).then_inc(padded, 1)
            at = plan["sw_qkv"]
            tmp = sw_tmp

            def rotate(dst, src, tmp, j, shape):
                cos = const("sw_cos")[:, j * 32:(j + 1) * 32]
                sin = const("sw_sin")[:, j * 32:(j + 1) * 32]
                for _ in shape:
                    cos, sin = cos.unsqueeze(1), sin.unsqueeze(1)
                cos, sin = cos.broadcast_to([P, *shape, 32]), sin.broadcast_to([P, *shape, 32])
                for c in range(2):
                    step(nc.vector.tensor_tensor(dst(c), src(c), cos, ALU.mult))
                    step(nc.vector.tensor_tensor(tmp(c), src(1 - c), sin, ALU.mult))
                step.settle()
                step(nc.vector.tensor_tensor(dst(0), dst(0), tmp(0), ALU.subtract))
                return nc.vector.tensor_tensor(dst(1), dst(1), tmp(1), ALU.add)

            for cb in range(2):
                for j in range(NT):
                    t = at.tiles + NT * cb + j
                    filled(dve, t)
                    s4 = work[:, t % 4, :].rearrange("p (g r c d) -> p g r c d", g=2, r=4, c=2)
                    d4 = q_rows[:, j, cb * 512:cb * 512 + 512].rearrange("p (r g c d) -> p g r c d", g=2, r=4, c=2)
                    t4 = tmp.rearrange("p (g r c d) -> p g r c d", g=2, r=4, c=2)
                    rotate(lambda c: d4[:, :, :, c, :], lambda c: s4[:, :, :, c, :], lambda c: t4[:, :, :, c, :], j, (2, 4))                        .then_inc(tile_read[t % 4], 1)
                    read_out(dve, t)
                    step.settle()
            for q in range(2 * NT):
                t = at.tiles + 2 * NT + q
                kt = (q + NT) % (2 * NT)
                filled(dve, t)
                step(nc.vector.tensor_copy(sw_v[:, kt, :], work[:, t % 4, 256:512]))
                if q < NT:
                    s3 = work[:, t % 4, 0:256].rearrange("p (g c d) -> p g c d", g=4, c=2)
                    d3 = sw_k_rows[:, kt, :].rearrange("p (g c d) -> p g c d", g=4, c=2)
                    t3 = tmp[:, 0:256].rearrange("p (g c d) -> p g c d", g=4, c=2)
                    ins = rotate(lambda c: d3[:, :, c, :], lambda c: s3[:, :, c, :], lambda c: t3[:, :, c, :], q, (4,))
                else:
                    ins = nc.vector.tensor_copy(sw_k_rows[:, kt, :], work[:, t % 4, 0:256])
                ins.then_inc(tile_read[t % 4], 1)
                read_out(dve, t)
                step.settle()

            def sw_begin(u, t, j, h):
                filled(dve, t)
                step(nc.vector.tensor_copy(sw_masked[:, u % 2, 0:S], work[:, t % 4, 0:S]))
                nc.vector.tensor_tensor(sw_masked[:, u % 2, S:2 * S], work[:, t % 4, S:2 * S], mask[:, j, :],
                                        ALU.add).then_inc(tile_read[t % 4], 1)
                read_out(dve, t)
                step.settle()
                pk = peak[:, u % 2, 0:1]
                step(nc.vector.tensor_reduce(pk, sw_masked[:, u % 2, :], AX_X, ALU.max))
                step.settle()
                step(nc.vector.tensor_scalar(pk, pk, SW_HD ** -0.5, sink[:, h:h + 1], ALU.mult, ALU.max))
                step.settle()
                nc.vector.tensor_scalar(low[:, u % 2, 0:1], pk, -1.0, None, ALU.mult).then_inc(low_ready, 1)

            def sw_weigh(u, at):
                dve.wait_ge(exp_ready, NT * DA_H + u + 1)
                sh = share[:, u % 2, 0:1]
                step(nc.vector.tensor_tensor(sh, mass[:, u % 2, 0:1], sink_exp[:, u % 2:u % 2 + 1], ALU.add))
                step.settle()
                step(nc.vector.reciprocal(sh, sh))
                step.settle()
                pr = sw_probs[:, u % 2, :]
                nc.vector.tensor_scalar(pr, pr, sh, None, ALU.mult).then_inc(share_ready, 1)

            dve.wait_ge(mask_landed, 32)
            attention("sw_att", SW_HQ, sw_begin, sw_weigh, SW_HD)
            scale = param_row()
            at = plan["sw_out"]
            for j in range(NT):
                dve.wait_ge(acc_full, NT * at.acc + j + 1)
                modulated_sum(acc[:, 2 * j:2 * j + 2, :].rearrange("p a c -> p (a c)"), j, j, scale,
                              acc_read, NT * at.acc + j + 1)
            give_back(1)
            mod_norm("moe_norm1", 1)
            experts(1)
            mod_norm("last_norm", 1, last=True)

        @block.gpsimd
        def _(pool):
            rows = param_rows(io, mod_rows)
            r = 0

            def load_row():
                nonlocal r
                if r >= PR_RING:
                    pool.wait_ge(rows_used, r - PR_RING + 1)
                pool.dma_start(prow[:, r % PR_RING, :], rows[r].partition_broadcast(P)).then_inc(row_landed[r % PR_RING], 16)
                r += 1

            def load_ada_bias(i):
                pool.dma_start(mods[0:2, :], io["ada_b"][i].partition_broadcast(2)).then_inc(ada_bias_landed, 16)

            def store_mods(i):
                at = plan[f"ffn{i}"]
                _, t0, _ = ffn_events(range(FFN_HEAD), False)
                body, t1, _ = ffn_events(range(FFN_HEAD, FFN_HEAD + FFN_BODY), True)
                last = max(t for kind, _, t, _ in body if kind == "sum")
                read_out(pool, at.tiles + t0 + last, (FFN_LOOPS - 1) * (t1 // 4))
                pool.dma_start(mod_rows[i], mods[0:2, :]).then_inc(mods_stored, 16)

            pool.dma_start(hy_cols[:, :, :], io["hy_cols"].rearrange("p (k n) -> p k n", n=5)).then_inc(hy_landed, 16)
            pool.dma_start(hy_small[:, :], io["hy_small"]).then_inc(hy_landed, 16)
            pool.dma_start(hy_z_in, io["hy_z"]).then_inc(hy_landed, 16)
            pool.dma_start(router_w[:, :, :, :], io["router_cols"].rearrange("p (l k e) -> p l k e", l=DEPTH, k=KB)).then_inc(router_landed, 16)
            pool.dma_start(sink[:, :], io["sw_sink"].partition_broadcast(P)).then_inc(router_landed, 16)
            pool.dma_start(pos_i[:, :], io["pos_cols"]).then_inc(small_landed, 16)
            for c, name in enumerate(("da_lam_q", "da_lam_k")):
                pool.dma_start(lam_in[:, c, :], io[name][0].rearrange("a d -> (a d)").partition_broadcast(P)).then_inc(small_landed, 16)
            pool.dma_start(subln[:, :], io["da_subln_g"][0].partition_broadcast(P)).then_inc(small_landed, 16)
            load_ada_bias(0)
            pool.dma_start(mask[:, :, :], io["masks"][0].rearrange("p (j k) -> p j k", j=NT)).then_inc(mask_landed, 16)
            def rows_until(n):
                while r < n:
                    load_row()

            def load_window(c):
                if c:
                    pool.wait_ge(filters_done, c)
                pool.dma_start(hy_window[:, :, :], io["hy_window"][:, :, c * HC:(c + 1) * HC]).then_inc(window_landed, 16)

            rows_until(PR_RING)
            store_mods(0)
            rows_until(8)
            pool.wait_ge(mods_stored, 16)
            pool.wait_ge(rows_ready, plan["xa_norm0"].rows + NT)
            load_ada_bias(1)
            pool.dma_start(mask[:, :, :], io["masks"][1].rearrange("p (j k) -> p j k", j=NT)).then_inc(mask_landed, 16)
            store_mods(1)
            pool.wait_ge(mods_stored, 32)
            ln_rows = 8 * DEPTH + 2
            rows_until(ln_rows)
            pool.wait_ge(rows_ready, plan["xa_norm1"].rows + NT)
            pool.dma_start(rows_x[:, NT:2 * NT, :], io["ctx"][0].rearrange("(j p) d -> p j d", p=P)).then_inc(ctx_landed, 16)
            hyena_rows = ln_rows + 8
            rows_until(hyena_rows)
            pool.wait_ge(rows_ready, plan["mod_norm0"].rows + NT)
            for c in range(D // HC):
                load_window(c)
            rows_until(len(rows))


IN_NAMES = ["x", "mem", "ffn_w_in", "ffn_w_out", "ln_g", "ln_b", "da_w_qkv", "da_w_o", "da_lam_q", "da_lam_k",
            "da_subln_g", "pool_w", "pool_b", "pool_scale", "xa_wq", "xa_wkv", "xa_wo"]


def lay_out(inputs):
    a = {n: np.ascontiguousarray(inputs[n]) for n in IN_NAMES}
    a["ada_w"] = np.ascontiguousarray(inputs["ada_w_2"])
    a["ada_b"] = np.ascontiguousarray(inputs["ada_b_2"])
    cond = np.stack([np.asarray(inputs["c_2"])[0], np.asarray(inputs["c_ctx_2"])])
    a["cond_cols"] = np.ascontiguousarray(cond.reshape(2, KB, P).transpose(2, 1, 0).reshape(P, 2 * KB))
    a["pos_cols"] = np.ascontiguousarray(np.asarray(inputs["positions"]).reshape(NT, P).T)
    a["ctx"] = np.ascontiguousarray(inputs["ctx_2"])
    for name in ("norm1_w", "norm2_w"):
        a[name] = np.ascontiguousarray(inputs[name + "_2"])
    a["final_w"] = np.ascontiguousarray(inputs["final_norm_w_2"])
    a["hy_bias"] = np.ascontiguousarray(inputs["hy_filter_bias_2"])
    a["hy_b_out"] = np.ascontiguousarray(inputs["hy_b_out_2"])
    a["hy_w_in"] = np.ascontiguousarray(inputs["hy_w_in_2"])
    a["hy_w3"] = np.ascontiguousarray(inputs["hy_ffn_w3_2"])
    a["hy_w_out"] = np.ascontiguousarray(inputs["hy_w_out_2"])
    a["sw_w_in"] = np.ascontiguousarray(inputs["sw_w_in_2"])
    a["sw_w_out"] = np.ascontiguousarray(inputs["sw_w_out_2"])
    a["sw_sink"] = np.ascontiguousarray(inputs["sw_sink_2"])
    a["moe_gate"] = np.ascontiguousarray(inputs["moe_w_gate_2"])
    a["moe_up"] = np.ascontiguousarray(inputs["moe_w_up_2"])
    a["moe_down"] = np.ascontiguousarray(inputs["moe_w_down_2"])
    taps = np.asarray(inputs["hy_short_w_2"])
    cols = np.stack([np.asarray(inputs["hy_b_in_2"]), np.asarray(inputs["hy_short_b_2"]), *taps])
    a["hy_cols"] = np.ascontiguousarray(cols.reshape(5, 3 * KB, P).transpose(2, 1, 0).reshape(P, -1))
    small = np.zeros((HY_FFN, 2 * HY_FFN + 4), np.float32)
    small[:HY_EMB, :HY_FFN] = inputs["hy_ffn_w1_2"]
    small[:, HY_FFN:2 * HY_FFN] = inputs["hy_ffn_w2_2"]
    for n, col in enumerate((inputs["hy_ffn_b1_2"], inputs["hy_ffn_b2_2"], *np.asarray(inputs["hy_sin_freq_2"]))):
        small[:, 2 * HY_FFN + n] = col
    a["hy_small"] = small
    router = np.asarray(inputs["moe_router_2"])
    a["router_cols"] = np.ascontiguousarray(router.reshape(DEPTH, KB, P, E_N).transpose(2, 0, 1, 3).reshape(P, -1))
    a["hy_z"] = position_features()
    a["dft"] = dft_tables()
    a["hy_window"] = window_table()
    a["consts"] = CONSTS
    a["masks"] = mask_tables()
    a["pool_tables"] = pool_tables()
    return a


def kernel(**inputs):
    import concourse.bacc as bacc
    from concourse.bass_utils import run_bass_kernel_spmd

    nc = bacc.Bacc("TRN2", target_bir_lowering=False, num_devices=1)
    arrays, io = {}, {}
    for name, a in lay_out(inputs).items():
        arrays[f"in_{name}"] = a
        io[name] = nc.dram_tensor(f"in_{name}", a.shape, mybir.dt.from_np(a.dtype), kind="ExternalInput").ap()
    out = nc.dram_tensor("out", (1, S, D), F32, kind="ExternalOutput").ap()
    mod_rows = nc.dram_tensor("mod_rows", (DEPTH, 2, NMOD * D), F32, kind="Internal").ap()
    build_program(nc, io, out[0], mod_rows)
    r = run_bass_kernel_spmd(nc, [arrays], core_ids=[0])
    return r.results[0]["out"]
```

```python
from collections import namedtuple
from contextlib import ExitStack
import math

import numpy as np

import concourse.bass as bass
from concourse import mybir

F32 = mybir.dt.float32
F32R = mybir.dt.float32r
I32 = mybir.dt.int32
ACT = mybir.ActivationFunctionType
ALU = mybir.AluOpType
AX_X = mybir.AxisListType.X

P = 128
S = 256
D = 1024
KB = D // P
NT = S // P
DEPTH = 2
FF = 2816
FB = 256
FSTEPS = FF // FB
ALPHA = (2 * DEPTH) ** 0.25
LN_EPS = 1e-5
EPS = 1e-6
NEG = -1e30
DA_H, DA_DK = 8, 64
LAM_INIT = 0.8 - 0.6 * math.exp(0.0)
XA_H = 4
XA_DK = D // XA_H
POOL_WINDOWS = (2, 4, 8, 16)
NMOD = 6
HY_LFFT = 2 * S - 1
HY_EMB, HY_FFN = 33, 64
HC = 256
SW_HQ, SW_HKV, SW_HD, SW_WINDOW = 16, 4, 64, 128
E_N, E_FF, CAP = 16, 1024, 2 * S // 16

RING = 12
SLOT = 2048
PR_RING = 4
SCRATCH = 9216

TWO_PI = 2.0 * math.pi
PI_BELOW = 3.1415925
MAGIC = 12582912.0


def two_pi_parts():
    c1 = float(np.float32(6.28125))
    c2 = float(np.float32(int((TWO_PI - c1) * 2 ** 21) / 2 ** 21))
    return c1, c2, float(np.float32(TWO_PI - c1 - c2))


def const_pack():
    p = np.arange(P)
    tok = np.arange(NT)[:, None] * P + p[None, :]
    parts = {}
    parts["ident"] = np.eye(P)
    parts["lanes4"] = (p[:, None] % 32 == p[None, :] % 32)
    parts["lanes2"] = (p[:, None] % 64 == p[None, :] % 64)
    parts["iota"] = np.broadcast_to(np.arange(1, CAP + 1), (P, CAP))
    inv = (1.0 / (np.float32(10000.0) ** (np.arange(0, DA_DK, 2, dtype=np.float32) / np.float32(DA_DK)))).astype(np.float32)
    parts["da_inv"] = np.broadcast_to(inv, (P, DA_DK // 2))
    nf = SW_HD // 4
    sinv = (np.float32(10000.0) ** (-np.arange(nf, dtype=np.float32) / np.float32(nf))).astype(np.float32)
    row, col = (tok // 64).astype(np.float32), (tok % 64).astype(np.float32)
    ang = np.concatenate([row[..., None] * sinv, col[..., None] * sinv], -1).astype(np.float64)
    parts["sw_cos"] = np.cos(ang).transpose(1, 0, 2).reshape(P, -1)
    parts["sw_sin"] = np.sin(ang).transpose(1, 0, 2).reshape(P, -1)
    parts["not_first"] = (tok.T > 0)
    where, at, cols = {}, 0, []
    for name, a in parts.items():
        a = np.asarray(a, np.float32).reshape(P, -1)
        where[name] = (at, a.shape[1])
        at += a.shape[1]
        cols.append(a)
    return np.ascontiguousarray(np.concatenate(cols, 1)), where


def mask_tables():
    q = (np.arange(NT)[:, None] * P + np.arange(P)[None, :]).T[..., None]
    k = np.arange(S)[None, None, :]
    causal = np.where(k <= q, 0.0, NEG)
    band = np.where(np.abs(q - k) <= SW_WINDOW, 0.0, NEG)
    return np.stack([causal, band]).reshape(2, P, NT * S).astype(np.float32)


def pool_tables():
    out = np.zeros((S, len(POOL_WINDOWS), S))
    for g, w in enumerate(POOL_WINDOWS):
        for t in range(S):
            out[max(0, t - w + 1):t + 1, g, t] = 1.0 / min(t + 1, w)
            out[t, g, t] -= 1.0
    return np.ascontiguousarray(out.reshape(NT, P, -1).transpose(1, 0, 2).reshape(P, -1)).astype(np.float32)


def dft_tables():
    a = np.arange(S)
    ang = 2 * np.pi * ((a[:, None] * a[None, :]) % HY_LFFT) / HY_LFFT
    c = np.where(a == 0, 1.0, 2.0)[:, None] / HY_LFFT
    tabs = np.stack([np.cos(ang), np.sin(ang), c * np.cos(ang), c * np.sin(ang)])
    return np.ascontiguousarray(tabs.reshape(4, NT, P, S).transpose(2, 0, 1, 3).reshape(P, -1)).astype(np.float32)


def position_features():
    t = np.linspace(0.0, 1.0, S)
    w = 2.0 * np.pi * np.arange(S) / S
    f = np.linspace(1e-4, (HY_EMB - 1) // 2 - 1, (HY_EMB - 1) // 2)
    z = np.concatenate([t[:, None], np.cos(f * w[:, None]), -np.sin(f * w[:, None])], -1)
    return np.ascontiguousarray(z.T).astype(np.float32)


def window_table():
    lo, hi = math.log(1e-2) / 1.5, math.log(1e-2) / 0.3
    deltas = np.abs(np.linspace(lo, hi, D))
    w = np.exp(-np.linspace(0.0, 1.0, S)[:, None] * deltas) + 0.05
    return np.ascontiguousarray(w.reshape(NT, P, D).transpose(1, 0, 2)).astype(np.float32)


CONSTS, CONST_AT = const_pack()

SUMS_BEFORE_IN = ((), (), (), (4, 5))
SUMS_AFTER_IN = ((), (0, 1), (2, 3), ())
PARTS_AFTER_OUT = ((0, 1), (2, 3), (4, 5), ())
ADA_PER_BODY = 6


def ffn_events(steps, ada):
    out, tile, load, before, parts = [], 0, 0, -2, {}

    def sums(cs):
        nonlocal tile
        for c in cs:
            out.append(("sum", c, tile, parts[c]))
            tile += 1

    for n, u in enumerate(steps):
        if ada:
            sums(SUMS_BEFORE_IN[n])
        mine = tile
        for half in range(2):
            out.append(("in", (u, half), tile, load))
            tile += 1
        load += 4
        if ada:
            sums(SUMS_AFTER_IN[n])
        if u > 0:
            out.append(("out", u - 1, before, load))
            load += 2
        before = mine
        if ada:
            for c in PARTS_AFTER_OUT[n]:
                out.append(("part", c, tile, load))
                parts[c] = tile
                tile += 1
                load += 2
    assert before == tile - 2
    return out, tile, load


def sums_last(events):
    out, held = [], []
    for e in events:
        if e[0] == "sum":
            held.append(e)
            continue
        if e[0] == "part":
            out, held = out + held, []
        out.append(e)
    return out + held


FFN_BODY = 4
FFN_HEAD = (FSTEPS - 1) % FFN_BODY + 1
FFN_LOOPS = (FSTEPS - FFN_HEAD) // FFN_BODY


def attention_order(units):
    at, order = 0, {}
    for v in range(units + 3):
        for kind, u in (("s", v), ("t", v - 2), ("o", v - 3)):
            if 0 <= u < units:
                order[kind, u] = at
                at += 1
    return order


class Plan:

    FIELDS = ("splits", "loads", "tiles", "acc", "rows", "norms", "silu", "units", "convs", "lags",
              "spectra", "experts")

    At = namedtuple("At", FIELDS)

    def __init__(self):
        self.now = dict.fromkeys(self.FIELDS, 0)
        self.stages = {}

    def add(self, stage, **n):
        self.stages[stage] = self.At(**self.now)
        for f, more in n.items():
            self.now[f] += more

    def __getitem__(self, stage):
        return self.stages[stage]


def ffn_totals(ada):
    _, t0, l0 = ffn_events(range(FFN_HEAD), False)
    _, t1, l1 = ffn_events(range(FFN_HEAD, FFN_HEAD + FFN_BODY), ada)
    assert t1 % 4 == 0 and l1 % RING == 0
    return t0, l0, t1, l1


def make_plan():
    plan = Plan()
    plan.add("x_cols", tiles=4)
    plan.add("mem_cols", tiles=4)
    plan.add("hy_mlp1", tiles=1)
    for i in range(DEPTH):
        for j in (0, 1):
            if j:
                if i == 0:
                    plan.add("hy_mlp2", tiles=1)
                    plan.add("da_qkv", loads=12, tiles=12)
                    plan.add("da_turn", tiles=8)
                    plan.add("da_att", tiles=3 * NT * DA_H, units=NT * DA_H)
                    plan.add("xa_k0a", loads=2, tiles=2)
                    plan.add("xa_k0b", loads=2, tiles=2)
                    plan.add("da_cols", tiles=4, norms=1)
                    plan.add("da_out", loads=4, acc=1)
                else:
                    plan.add("pool_mix", loads=1, tiles=4)
                    plan.add("pool_out", loads=1, acc=1)
                plan.add(f"xa_v{i}", loads=4, tiles=4)
                plan.add(f"mix_norm{i}", tiles=4, rows=NT, norms=NT)
                plan.add(f"xa_q{i}", loads=4, tiles=4)
                plan.add(f"xa_att{i}", tiles=3 * NT * XA_H, units=NT * XA_H)
                plan.add(f"xa_cols{i}", tiles=4)
                plan.add(f"xa_out{i}", loads=4, acc=1)
                if i == 1:
                    plan.add("ctx_norm", tiles=4, rows=NT, norms=NT)
                plan.add(f"xa_norm{i}", tiles=4, rows=NT, norms=NT)
            n = 2 * i + j
            t0, l0, t1, l1 = ffn_totals(n < DEPTH)
            plan.add(f"ffn{n}", loads=l0 + FFN_LOOPS * l1 + 2, splits=3 * FSTEPS, tiles=t0 + FFN_LOOPS * t1, acc=1,
                     silu=2 * FSTEPS)
            if n in (1, 2):
                plan.add("xa_k1a" if n == 1 else "xa_k1b", loads=2, tiles=2)
            plan.add(f"ffn_norm{n}", tiles=4 * int(n < 2), rows=NT, norms=NT)
    plan.add("mod_norm0", tiles=4, rows=NT, norms=NT)
    for c in range(D // HC):
        plan.add(f"hy_u{c}", loads=3, tiles=6, convs=6)
        plan.add(f"hy_f{c}0", loads=2, tiles=2, lags=NT)
        plan.add(f"hy_w{c}", tiles=4)
        for o in range(2):
            plan.add(f"hy_k{c}{o}", tiles=2)
            plan.add(f"hy_v{c}{o}", tiles=4, spectra=2)
            if o == 0:
                plan.add(f"hy_f{c}1", tiles=2, lags=NT)
            plan.add(f"hy_y{c}{o}", tiles=2)
    plan.add("hy_out0", loads=4, acc=1)
    plan.add("hy_out1", acc=1)
    plan.add("moe_norm0", tiles=4 * NT, rows=2 * NT, norms=2 * NT)
    plan_moe(plan, 0)
    plan.add("mod_norm1", tiles=2 * NT, rows=2 * NT, norms=2 * NT)
    plan.add("sw_q", loads=4, tiles=4)
    plan.add("ctx_cols", tiles=4)
    plan.add("sw_kv", loads=2, tiles=4)
    plan.add("sw_turn", tiles=6)
    plan.add("sw_att", tiles=3 * NT * SW_HQ, units=NT * SW_HQ)
    plan.add("sw_cols", tiles=4)
    plan.add("sw_out", loads=4, acc=1)
    plan.add("moe_norm1", tiles=2 * NT, rows=NT, norms=NT)
    plan_moe(plan, 1)
    plan.add("last_norm", rows=NT, norms=NT)
    return plan


MOE_LOADS = 12


def moe_body_tiles(streams):
    return 12 + 4 * streams


def plan_moe(plan, layer):
    streams = 2 - layer
    plan.add(f"router{layer}", tiles=3)
    plan.add(f"gather{layer}", tiles=KB * streams)
    plan.add(f"experts{layer}", loads=MOE_LOADS * E_N, tiles=moe_body_tiles(streams) * E_N, experts=E_N)


class Steps:

    def __init__(self, eng, sem):
        self.eng, self.sem, self.n, self.more = eng, sem, 0, 0

    def __call__(self, ins):
        ins.then_inc(self.sem, 1)
        self.n += 1

    def settle(self):
        self.eng.wait_ge(self.sem, self.n + self.more)

    def loop_in(self, i, per):
        self.at, self.per, self.more = self.n, per, i * per

    def loop_out(self, times):
        assert self.n - self.at == self.per, (self.n - self.at, self.per)
        self.n, self.more = self.at + self.per * times, 0


def param_rows(io, mod_rows):
    rows = []

    def ln(i, j):
        rows.extend([io["ln_g"][i, j], io["ln_b"][i, j]])

    def mod(layer, stream, n):
        rows.append(mod_rows[layer, stream, n * D:(n + 1) * D])

    def mod_norm(name, layer, stream, n):
        rows.append(io[name][layer])
        mod(layer, stream, n + 1)
        mod(layer, stream, n)

    for i in range(DEPTH):
        ln(i, 0)
        if i == 1:
            rows.extend([io["pool_b"][0].rearrange("g c -> (g c)"), io["pool_scale"][0]])
        ln(i, 1)
        if i == 1:
            mod_norm("norm1_w", 0, 1, 0)
        ln(i, 2)
        ln(i, 3)
    mod_norm("norm1_w", 0, 0, 0)
    rows.extend([io["hy_bias"][0], io["hy_bias"][1]])
    for s in range(2):
        mod(0, s, 2)
        rows.append(io["hy_b_out"])
        mod_norm("norm2_w", 0, s, 3)
    for s in range(2):
        mod(0, s, 5)
        mod_norm("norm1_w", 1, s, 0)
    mod(1, 0, 2)
    mod_norm("norm2_w", 1, 0, 3)
    mod(1, 0, 5)
    rows.append(io["final_w"])
    return rows


def build_program(nc, io, out, mod_rows):
    plan = make_plan()
    with ExitStack() as ctx:
        def sb(name, shape, dt=F32):
            return ctx.enter_context(nc.sbuf_tensor(name, shape, dt))

        def sem(name):
            return ctx.enter_context(nc.semaphore(name))

        shapes = {"ring": [P, RING, SLOT], "rows_h": [P, 2 * NT, D], "cols_x": [P, KB, 2 * S], "scratch": [P, SCRATCH]}
        with ExitStack() as first_names:
            ring, rows_h, cols_x, scratch = (
                first_names.enter_context(nc.sbuf_tensor(n, shape, F32)) for n, shape in shapes.items())
        ring_parts, rows_h_parts, cols_parts, scratch_parts = (
            sb(n + "_parts", shape, F32R) for n, shape in shapes.items())
        rows_x = sb("rows_x", [P, 2 * NT, D])
        prow = sb("prow", [P, PR_RING, D])
        consts = sb("consts", [P, CONSTS.shape[1]])
        mask = sb("mask", [P, NT, S])
        stats = sb("stats", [P, NT, 2, 6])
        mean_var = sb("mean_var", [P, 2 * NT, 2])
        spread = sb("spread", [P, 2 * NT])
        root = sb("root", [P, 2 * NT])
        rstd = sb("rstd", [P, 2 * NT])
        newton = sb("newton", [P, 2 * NT])
        pos_i = sb("pos_i", [P, NT], I32)
        pos_f = sb("pos_f", [P, NT])
        da_cs = sb("da_cs", [P, 2, NT, DA_DK // 2])
        subln = sb("subln", [P, 2 * DA_DK])
        lam = sb("lam", [P, 4])
        head_sq = sb("head_sq", [P, 3, NT * DA_H])
        peak = sb("peak", [P, 4, 2])
        low = sb("low", [P, 4, 2])
        mass = sb("mass", [P, 4, 2])
        share = sb("share", [P, 4, 2])
        head_tmp = sb("head_tmp", [P, NT * DA_H])
        hy_cols = sb("hy_cols", [P, 3 * KB, 5])
        hy_small = sb("hy_small", [HY_FFN, 2 * HY_FFN + 4])
        hy_h = sb("hy_h", [HY_FFN, 2, S])
        router_w = sb("router_w", [P, DEPTH, KB, E_N])
        neg_sink = sb("neg_sink", [P, SW_HQ])
        sink_exp = sb("sink_exp", [P, 4])
        gate = sb("gate", [P, 2 * NT, E_N])
        codes = sb("codes", [P, 2 * NT, E_N])
        top8 = sb("top8", [E_N, 8])
        act_in = sb("act_in", [P, KB, 2])
        act_col = sb("act_col", [P, KB, 32])

        def const(name, rows=P):
            at, n = CONST_AT[name]
            return consts[0:rows, at:at + n]

        ident = const("ident")

        def scr(at, n):
            return scratch[:, at:at + n]

        work = ctx.enter_context(nc.psum_tensor("work", [P, 4, 512], F32))
        acc = ctx.enter_context(nc.psum_tensor("acc", [P, 4, 512], F32))

        load_landed = [sem(f"load_landed{i}") for i in range(RING)]
        loads_used = sem("loads_used")
        tile_full = [sem(f"tile_full{i}") for i in range(4)]
        tile_read = [sem(f"tile_read{i}") for i in range(4)]
        acc_full = sem("acc_full")
        acc_read = sem("acc_read")
        row_landed = [sem(f"row_landed{i}") for i in range(PR_RING)]
        rows_used = sem("rows_used")
        rows_ready = sem("rows_ready")
        silu_ready = sem("silu_ready")
        split_ready = sem("split_ready")
        x_split = sem("x_split")
        var_ready = sem("var_ready")
        root_ready = sem("root_ready")
        x_landed = sem("x_landed")
        mem_landed = sem("mem_landed")
        consts_landed = sem("consts_landed")
        cond_landed = sem("cond_landed")
        small_landed = sem("small_landed")
        mask_landed = sem("mask_landed")
        ada_bias_landed = sem("ada_bias_landed")
        cond_zeroed = sem("cond_zeroed")
        cond_ready = sem("cond_ready")
        part_ready = sem("part_ready")
        mods_summed = sem("mods_summed")
        mods_stored = sem("mods_stored")
        angles_ready = sem("angles_ready")
        sines_ready = sem("sines_ready")
        lam_sums = sem("lam_sums")
        lam_exp = sem("lam_exp")
        padded = sem("padded")
        low_ready = sem("low_ready")
        share_ready = sem("share_ready")
        heads_normed = sem("heads_normed")
        out_landed = sem("out_landed")
        hy_landed = sem("hy_landed")
        ctx_landed = sem("ctx_landed")
        window_landed = sem("window_landed")
        mlp_angles = sem("mlp_angles")
        mlp_sines = sem("mlp_sines")
        conv_ready = sem("conv_ready")
        lags_ready = sem("lags_ready")
        spectra_ready = sem("spectra_ready")
        logits_low = sem("logits_low")
        logits_exp = sem("logits_exp")
        gates_ready = sem("gates_ready")
        codes_ready = sem("codes_ready")
        choice_ready = sem("choice_ready")
        taken_ready = sem("taken_ready")
        spread_ready = sem("spread_ready")
        filters_done = sem("filters_done")
        router_landed = sem("router_landed")
        vec_steps = sem("vec_steps")

        def filled(eng, t, more=0):
            eng.wait_ge(tile_full[t % 4], t // 4 + 1 + more)

        def read_out(eng, t, more=0):
            eng.wait_ge(tile_read[t % 4], t // 4 + 1 + more)

        silu_buf = scr(0, 1024).rearrange("p (b t) -> p b t", b=4)
        gated = scr(1024, 1024).rearrange("p (b t) -> p b t", b=4)
        gated_low = scratch_parts[:, 1024:2048].rearrange("p (b t) -> p b t", b=4)
        ada_part = scr(2048, 1024).rearrange("p (b c) -> p b c", b=2)
        mods = scr(3072, NMOD * D)
        mlp_turns = rows_h[0:HY_FFN, 0, 512:512 + S]
        x_low = cols_parts[:, :, 0:S]
        x_high = rows_h_parts[:, NT:2 * NT, :].rearrange("p j d -> p (j d)").rearrange("p (k t) -> p k t", k=KB)
        gated_high = rows_h_parts[:, 1, :].rearrange("p (b t) -> p b t", b=4)
        lam_in = rows_h[:, 0, 0:4 * DA_DK].rearrange("p (c d) -> p c d", c=2)
        angle = rows_h[:, 0, 256:384].rearrange("p (c j d) -> p c j d", c=2, j=NT)
        turns = rows_h[:, 0, 384:512].rearrange("p (c j d) -> p c j d", c=2, j=NT)
        hy_z_in = rows_h[0:HY_EMB, 1, 0:S]
        q_lo = scr(0, 2048).rearrange("p (h t) -> p h t", h=8)
        q_hi = scr(2048, 2048).rearrange("p (h t) -> p h t", h=8)
        k_cols = scr(4096, 2048).rearrange("p (h t) -> p h t", h=8)
        v_rows = scr(6144, 2048).rearrange("p (j c) -> p j c", j=NT)
        turned_p = scr(8192, 512).rearrange("p (b k t) -> p b k t", b=2, k=2)
        rope_tmp = scr(8704, 512)
        probs = rows_x[:, 3, :].rearrange("p (b c) -> p b c", b=2)
        q_rows = rows_h[:, 0:NT, :]
        k_rows = rows_h[:, NT:2 * NT, :]
        pooled = scr(0, 2048).rearrange("p (k t) -> p k t", k=KB)
        pool_y = scr(2048, 1024)
        hy_y = scr(0, 2048).rearrange("p (b t) -> p b t", b=4)
        hy_lags = [scr(at, 1024).rearrange("p (j c) -> p j c", j=NT) for at in (6144, 0)]
        hy_lags_tmp = [scr(at, 512).rearrange("p (a c) -> p a c", a=2) for at in (7168, 2048)]
        hy_k = scr(1024, 1024).rearrange("p (f r c) -> p f r c", f=NT, r=2)
        hy_biased = scr(2048, 1024).rearrange("p (b t) -> p b t", b=2)
        hy_tmp = scr(2048, 512)
        hy_x2 = scr(3072, 1024).rearrange("p (a t) -> p a t", a=2)
        hy_v = scr(4096, 1024).rearrange("p (j c) -> p j c", j=NT)
        hy_x1 = scr(5120, 1024).rearrange("p (j c) -> p j c", j=NT)
        hy_spec = scr(6144, 2048).rearrange("p (f r c) -> p f r c", f=NT, r=2)
        hy_window = scr(8192, 512).rearrange("p (j c) -> p j c", j=NT)
        hy_z = rows_h.rearrange("p j d -> p (j d)").rearrange("p (k t) -> p k t", k=KB)
        mix_tmp = scr(NT * D, D)
        h_main = scr(0, NT * D).rearrange("p (j d) -> p j d", j=NT)
        sw_k_cols = scr(4096, 1024).rearrange("p (g t) -> p g t", g=2)
        sw_v = scr(5120, 1024).rearrange("p (k c) -> p k c", k=4)
        sw_k_rows = scr(6144, 1024).rearrange("p (k c) -> p k c", k=4)
        sw_turned = scr(7168, 1024).rearrange("p (b k t) -> p b k t", b=2, k=4)
        sw_tmp = scr(8192, 512)
        sw_probs = rows_h[:, 3, :].rearrange("p (b c) -> p b c", b=2)
        xe = [cols_x, scr(0, 4096).rearrange("p (k c) -> p k c", k=KB)]
        chosen = scr(4096, 2048).rearrange("p (i c) -> p i c", i=2 * NT)
        gate_part = scr(4096, 1024)
        up_part = scr(5120, 1024)
        down_part = gate_part
        taken = scr(6144, 512)
        silu_e = scr(6656, 512)
        gated_e = scr(7168, 512)
        spread_e = scr(7680, 512).rearrange("p (i c) -> p i c", i=2 * NT)
        spread_cols = scr(8192, 512).rearrange("p (i t) -> p i t", i=2 * NT)
        aff = scratch[0:E_N, 6656:7168]
        left = scratch[0:E_N, 7168:7680]
        picked = scratch[0:E_N, 7680:8192]
        count = scratch[0:E_N, 8192:8704]
        zeros16 = scratch[0:E_N, 8704:9216]
        logit = scr(6144, 64).rearrange("p (i e) -> p i e", i=2 * NT)
        logit_peak = scr(6208, 4)

        block = ctx.enter_context(nc.Block())

        @block.sync
        def _(sp):
            def load(n, dst_shape, src, more=0, rows=P):
                sp.wait_ge(loads_used, n + 1 + more)
                size = int(np.prod(dst_shape))
                dst = ring[0:rows, n % RING, 0:size]
                if len(dst_shape) == 2:
                    dst = dst.rearrange("p (a b) -> p a b", a=dst_shape[0])
                sp.dma_start(dst, src).then_inc(load_landed[n % RING], 16)

            def load_rows_out(n, w, blocks):
                for cb in range(blocks):
                    for half in range(2):
                        load(n, (4, 512), w[half * 512:half * 512 + 512, cb * 512:cb * 512 + 512]
                             .rearrange("(k p) c -> p k c", p=P))
                        n += 1
                return n

            def load_cols_out(n, w, c0, count):
                for cb in range(count):
                    load(n, (KB, 256), w[:, c0 + cb * 256:c0 + cb * 256 + 256].rearrange("(k p) c -> p k c", p=P))
                    n += 1
                return n

            def ffn(i):
                w_in, w_out = io["ffn_w_in"][i // 2, i % 2], io["ffn_w_out"][i // 2, i % 2]
                ada = i < DEPTH
                base = plan[f"ffn{i}"].loads

                def run(events, n0, i_loop, per):
                    step0 = 0 if i_loop is None else i_loop * FFN_BODY
                    more = 0 if i_loop is None else i_loop * per
                    for kind, what, _, at in events:
                        n = n0 + at
                        if kind == "in" and what[1] == 0:
                            for part in range(2):
                                c = (what[0] + step0) * FB + part * FF
                                load(n + 2 * part, (KB, FB), w_in[:, bass.ds(c, FB)].rearrange("(k p) c -> p k c", p=P), more)
                        elif kind == "out":
                            r = (what + step0) * FB
                            load(n, (2, D), w_out[bass.ds(r, FB), :].rearrange("(k p) c -> p k c", p=P), more)
                        elif kind == "part":
                            c = (what + i_loop * ADA_PER_BODY) * 512
                            for half in range(2):
                                load(n + half, (4, 512), io["ada_w"][i][half * 512:half * 512 + 512, bass.ds(c, 512)]
                                     .rearrange("(k p) c -> p k c", p=P), more)

                head, _, l0 = ffn_events(range(FFN_HEAD), False)
                body, _, l1 = ffn_events(range(FFN_HEAD, FFN_HEAD + FFN_BODY), ada)
                run(head, base, None, 0)
                with sp.Fori(0, FFN_LOOPS) as it:
                    run(body, base + l0, it, l1)
                n = base + l0 + FFN_LOOPS * l1
                load(n, (2, D), w_out[FF - FB:FF, :].rearrange("(k p) c -> p k c", p=P))

            def load_keys(stage, i, half):
                load_cols_out(plan[stage].loads, io["xa_wkv"][i], half * (D // 2), 2)

            for i in range(DEPTH):
                ffn(2 * i)
                if i == 0:
                    load_rows_out(plan["da_qkv"].loads, io["da_w_qkv"][0], 6)
                    load_keys("xa_k0a", 0, 0)
                    load_keys("xa_k0b", 0, 1)
                    load_rows_out(plan["da_out"].loads, io["da_w_o"][0], 2)
                else:
                    load_keys("xa_k1b", 1, 1)
                    load(plan["pool_mix"].loads, (SLOT,), io["pool_tables"])
                    load(plan["pool_out"].loads, (8, 256), io["pool_w"][0].rearrange("g (k p) c -> p (g k) c", p=P))
                load_rows_out(plan[f"xa_v{i}"].loads, io["xa_wkv"][i][:, D:2 * D], 2)
                load_cols_out(plan[f"xa_q{i}"].loads, io["xa_wq"][i], 0, 4)
                load_rows_out(plan[f"xa_out{i}"].loads, io["xa_wo"][i], 2)
                ffn(2 * i + 1)
                if i == 0:
                    load_keys("xa_k1a", 1, 0)
            for c in range(D // HC):
                n = plan[f"hy_u{c}"].loads
                for section in range(3):
                    load_cols_out(n + section, io["hy_w_in"], section * D + c * HC, 1)
                n = plan[f"hy_f{c}0"].loads
                load(n, (4, HC), io["hy_w3"].rearrange("p (a c) -> p a c", a=4)[:, :, c * HC:(c + 1) * HC], rows=HY_FFN)
                load(n + 1, (SLOT,), io["dft"])
            load_rows_out(plan["hy_out0"].loads, io["hy_w_out"], 2)

            def experts(layer):
                base = plan[f"experts{layer}"].loads
                with sp.Fori(0, E_N) as e:
                    n = base
                    for name in ("moe_gate", "moe_up", "moe_down"):
                        w = io[name][layer].rearrange("e k c -> (e k) c")
                        for cb in range(2):
                            for half in range(2):
                                load(n, (4, 512), w[bass.ds(e * D + half * 512, 512), cb * 512:cb * 512 + 512]
                                     .rearrange("(k p) c -> p k c", p=P), e * MOE_LOADS)
                                n += 1

            experts(0)
            load_rows_out(plan["sw_q"].loads, io["sw_w_in"], 3)
            load_rows_out(plan["sw_out"].loads, io["sw_w_out"], 2)
            experts(1)
            for j in range(NT):
                sp.wait_ge(rows_ready, plan["last_norm"].rows + j + 1)
                sp.dma_start(out[j * P:(j + 1) * P, :], rows_h[:, j, :]).then_inc(out_landed, 16)
            sp.wait_ge(out_landed, 16 * NT)

        @block.tensor
        def _(pe):
            owed = [0]

            def mm(o, lhsT, rhs, start, stop, signal=None, done=0, **kw):
                ins = nc.tensor.matmul(o, lhsT, rhs, start=start, stop=stop, **kw)
                owed[0] += done
                if signal is not None:
                    ins.then_inc(signal, 1)
                elif owed[0]:
                    ins.then_inc(loads_used, owed[0])
                    owed[0] = 0

            def mm_split(o, lhsT, rhs, start, stop, signal=None, done=0):
                for n, (a, b) in enumerate(((0, 0), (0, 1), (1, 0))):
                    mm(o, lhsT[a], rhs[b], start and n == 0, stop and n == 2,
                       signal if n == 2 else None, done if n == 2 else 0)

            def turn(o, i, signal=None, size=P):
                ins = nc.tensor.transpose(o, i, ident[0:size, 0:size])
                if signal is not None:
                    ins.then_inc(signal, 1)
                elif owed[0]:
                    ins.then_inc(loads_used, owed[0])
                    owed[0] = 0

            def open_tile(t, more=0):
                if t >= 4:
                    pe.wait_ge(tile_read[t % 4], t // 4 + more)
                return work[:, t % 4, :]

            def landed(n, more=0):
                pe.wait_ge(load_landed[n % RING], 16 * (n // RING + 1) + more)

            def slot(n, a):
                return ring[:, n % RING, :].rearrange("p (a b) -> p a b", a=a)

            def parts(n, a):
                return tuple(ring_parts[:, m % RING, :].rearrange("p (a b) -> p a b", a=a) for m in (n + 1, n))

            def rows_out(n, t, x, blocks, tok0=0):
                for cb in range(blocks):
                    outs = [open_tile(t + j) for j in range(NT)]
                    for half in range(2):
                        landed(n)
                        w = slot(n, 4)
                        for j in range(NT):
                            for k in range(4):
                                kk = half * 4 + k
                                mm(outs[j], x[:, kk, tok0 + j * P:tok0 + (j + 1) * P], w[:, k, :],
                                   kk == 0, kk == KB - 1, tile_full[(t + j) % 4] if kk == KB - 1 else None,
                                   done=int(j == NT - 1 and k == 3))
                        n += 1
                    t += NT

            def tile_to_acc(stage, n, x, j, last):
                if plan[stage].acc:
                    pe.wait_ge(acc_read, NT * plan[stage].acc - NT + j + 1)
                for cb in range(2):
                    for half in range(2):
                        landed(n + 2 * cb + half)
                        w = slot(n + 2 * cb + half, 4)
                        for k in range(4):
                            kk = 4 * half + k
                            fin = kk == KB - 1
                            mm(acc[:, 2 * j + cb, :], x(kk, j), w[:, k, :], kk == 0, fin,
                               acc_full if fin and cb == 1 else None, done=int(last and k == 3))

            def out_product(stage):
                for j in range(NT):
                    tile_to_acc(stage, plan[stage].loads, lambda k, j: cols_x[:, k, j * P:(j + 1) * P], j, j == NT - 1)

            def cols_out(n, t, x, tok0, count):
                for cb in range(count):
                    landed(n)
                    w = slot(n, KB)
                    o = open_tile(t).rearrange("p (a t) -> p a t", a=2)
                    for a in range(2):
                        for k in range(KB):
                            last = k == KB - 1
                            mm(o[:, a, :], w[:, k, a * P:(a + 1) * P], x[:, k, tok0:tok0 + S], k == 0, last,
                               tile_full[t % 4] if last and a else None, done=int(last and a))
                    n, t = n + 1, t + 1

            def ffn(i):
                at = plan[f"ffn{i}"]
                ada = i < DEPTH
                _, t0, l0 = ffn_events(range(FFN_HEAD), False)
                _, t1, l1 = ffn_events(range(FFN_HEAD, FFN_HEAD + FFN_BODY), ada)

                def split(k, more):
                    pe.wait_ge(split_ready, at.splits + k + 1 + more)

                def down(u, n, first_tile, tmore, smore, last=False):
                    for h in range(2):
                        read_out(pe, first_tile + h, tmore)
                    split(3 * u + 4 if not last else 3 * FSTEPS - 1, smore)
                    high, low = parts(n, 2)
                    order = [(h, j) for h in range(2) for j in range(NT)]
                    if last:
                        order = [(h, j) for j in range(NT) for h in range(2)]
                    for h, j in order:
                        for half in range(2):
                            final = last and h == 1 and half == 1
                            b, c = (2 * u + h) % 4, slice(half * 512, half * 512 + 512)
                            mm_split(acc[:, 2 * j + half, :],
                                     (gated_high[:, b, j * P:(j + 1) * P], gated_low[:, b, j * P:(j + 1) * P]),
                                     (high[:, h, c], low[:, h, c]), u == 0 and h == 0, last and h == 1,
                                     acc_full if final else None, done=2 * int(h == 1 and j == NT - 1 and half == 1))

                def run(events, tb, lb, it, tper, lper):
                    tmore = 0 if it is None else it * (tper // 4)
                    lmore = 0 if it is None else it * (16 * (lper // RING))
                    smore = 0 if it is None else it * (3 * FFN_BODY)
                    for kind, what, dt, dn in events:
                        t, n = tb + dt, lb + dn
                        if kind == "in":
                            u, h = what
                            o = open_tile(t, tmore).rearrange("p (a t) -> p a t", a=2)
                            for a in range(2):
                                if h == 0:
                                    split(3 * u + a - int(u > 0), smore)
                                high, low = parts(n + 2 * a, KB)
                                for k in range(KB):
                                    fin = a == 1 and k == KB - 1
                                    c = slice(h * P, (h + 1) * P)
                                    mm_split(o[:, a, :], (high[:, k, c], low[:, k, c]), (x_high[:, k, :], x_low[:, k, :]),
                                             k == 0, k == KB - 1, tile_full[t % 4] if fin else None,
                                             done=4 * int(fin and h == 1))
                        elif kind == "out":
                            if what == 0 and at.acc:
                                pe.wait_ge(acc_read, NT * at.acc)
                            down(what, n, t, tmore, smore)
                        elif kind == "part":
                            o = open_tile(t, tmore)
                            for half in range(2):
                                landed(n + half, lmore)
                                w = slot(n + half, 4)
                                for g in range(4):
                                    fin = half == 1 and g == 3
                                    mm(o[32 * g:32 * g + 32, :], act_col[:, half * 4 + g, :], w[:, g, :],
                                       half == 0, half == 1, tile_full[t % 4] if fin else None,
                                       done=2 * int(fin), tile_position=(0, 32 * g))
                        else:
                            read_out(pe, tb + dn, tmore)
                            o = open_tile(t, tmore)
                            mm(o[0:32, :], const("lanes4")[:, 0:32], ada_part[:, what % 2, :], True, True, tile_full[t % 4])

                head, _, _ = ffn_events(range(FFN_HEAD), False)
                body, _, _ = ffn_events(range(FFN_HEAD, FFN_HEAD + FFN_BODY), ada)
                pe.wait_ge(x_split, NT * (i + 1))
                run(head, at.tiles, at.loads, None, 0, 0)
                owed_in = owed[0]
                with pe.Fori(0, FFN_LOOPS) as it:
                    run(body, at.tiles + t0, at.loads + l0, it, t1, l1)
                    assert owed[0] == owed_in, (owed[0], owed_in)
                down(FSTEPS - 1, at.loads + l0 + FFN_LOOPS * l1, at.tiles + t0 + FFN_LOOPS * t1 - 2, 0, 0, last=True)

            def attention(stage, heads, scores, values, width, key_tiles, weighed=False, probs=probs, turned_p=turned_p):
                units = NT * heads
                order = attention_order(units)
                at = plan[stage]
                for v in range(units + 3):
                    if v < units:
                        t = at.tiles + order["s", v]
                        scores(open_tile(t), v // heads, v % heads, tile_full[t % 4])
                    if 0 <= v - 2 < units:
                        u = v - 2
                        t = at.tiles + order["t", u]
                        o = open_tile(t)
                        if weighed:
                            pe.wait_ge(share_ready, at.units + u + 1)
                        else:
                            read_out(pe, at.tiles + order["s", u])
                        n = key_tiles(u // heads)
                        for k in range(n):
                            turn(o[:, k * P:(k + 1) * P], probs[:, u % 2, k * P:(k + 1) * P],
                                 tile_full[t % 4] if k == n - 1 else None)
                    if 0 <= v - 3:
                        u = v - 3
                        t = at.tiles + order["o", u]
                        o = open_tile(t)
                        read_out(pe, at.tiles + order["t", u])
                        n = key_tiles(u // heads)
                        for k in range(n):
                            mm(o[:, 0:width], turned_p[:, u % 2, k, :], values(k, u % heads), k == 0, k == n - 1,
                               tile_full[t % 4] if k == n - 1 else None)

            def out_to_cols(stage, att, heads):
                order = attention_order(NT * heads)
                t = plan[stage].tiles
                for j in range(NT):
                    read_out(pe, plan[att].tiles + order["o", (j + 1) * heads - 1])
                    turn_rows(t + 2 * j, q_rows[:, j, :])
                all_read(t)

            def turn_rows(t, src):
                for piece in range(2):
                    o = open_tile(t + piece)
                    for k in range(4):
                        turn(o[:, k * P:(k + 1) * P], src[:, (4 * piece + k) * P:(4 * piece + k + 1) * P],
                             tile_full[(t + piece) % 4] if k == 3 else None)

            def all_read(t):
                for q in range(4):
                    read_out(pe, t + q)

            def normed_to_cols(stage, rows=rows_x, tiles=NT):
                at = plan[stage]
                for j in range(tiles):
                    pe.wait_ge(rows_ready, at.rows + j + 1)
                    turn_rows(at.tiles + 2 * j, rows[:, j, :])
                all_read(at.tiles + 2 * tiles - 4)

            def acc_open(stage):
                if plan[stage].acc:
                    pe.wait_ge(acc_read, NT * plan[stage].acc)

            def memory_keys(stage):
                cols_out(plan[stage].loads, plan[stage].tiles, cols_x, S, 2)

            def cross_attention(i):
                at = plan[f"xa_v{i}"]
                rows_out(at.loads, at.tiles, cols_x, 2, tok0=S)
                normed_to_cols(f"mix_norm{i}")
                q = plan[f"xa_q{i}"]
                cols_out(q.loads, q.tiles, cols_x, 0, 4)
                for half in "ab":
                    for t in range(2):
                        read_out(pe, plan[f"xa_k{i}{half}"].tiles + t)
                all_read(at.tiles)
                all_read(q.tiles)
                attention(f"xa_att{i}", XA_H, xa_scores, lambda k, h: v_rows[:, k, h * XA_DK:(h + 1) * XA_DK], XA_DK,
                          lambda j: NT)
                out_to_cols(f"xa_cols{i}", f"xa_att{i}", XA_H)
                out_product(f"xa_out{i}")
                if i == 1:
                    normed_to_cols("ctx_norm", rows_h[:, NT:2 * NT])
                normed_to_cols(f"xa_norm{i}")

            def hyena_step(c):
                at = plan[f"hy_u{c}"]
                t = at.tiles

                def project(section, t):
                    n = at.loads + section
                    landed(n)
                    w = slot(n, KB)
                    for a in range(2):
                        o = open_tile(t)
                        for k in range(KB):
                            mm(o, w[:, k, a * P:(a + 1) * P], cols_x[:, k, :], k == 0, k == KB - 1,
                               tile_full[t % 4] if k == KB - 1 else None, done=int(a == 1 and k == KB - 1))
                        t += 1

                def turn_section(section, t):
                    pe.wait_ge(conv_ready, at.convs + 2 * section + 2)
                    for j in range(NT):
                        o = open_tile(t)
                        for s in range(2):
                            for a in range(2):
                                turn(o[:, s * HC + a * P:s * HC + (a + 1) * P],
                                     hy_y[:, 2 * section + a, s * S + j * P:s * S + (j + 1) * P],
                                     tile_full[t % 4] if s and a else None)
                        t += 1

                w3 = plan[f"hy_f{c}0"].loads
                filt = ring[0:HY_FFN, w3 % RING, 0:4 * HC].rearrange("p (a c) -> p a c", a=4)
                tabs = ring[:, (w3 + 1) % RING, :].rearrange("p (a j c) -> p a j c", a=4, j=NT)

                def filters(o_):
                    t = plan[f"hy_f{c}{o_}"].tiles
                    for j in range(NT):
                        o = open_tile(t).rearrange("p (a c) -> p a c", a=2)
                        for way in range(2):
                            mm(o[:, way, :], hy_h[:, 1, j * P:(j + 1) * P], filt[:, 2 * o_ + way, :], True, True,
                               tile_full[t % 4] if way else None, done=int(o_ == 1 and j == 1 and way == 1))
                        t += 1

                project(0, t)
                project(1, t + 2)
                turn_section(0, t + 4)
                landed(w3)
                filters(0)
                project(2, plan[f"hy_w{c}"].tiles)
                turn_section(1, plan[f"hy_w{c}"].tiles + 2)
                landed(w3 + 1)
                for o_ in range(2):
                    t = plan[f"hy_k{c}{o_}"].tiles
                    pe.wait_ge(lags_ready, plan[f"hy_f{c}{o_}"].lags + NT)
                    for f in range(NT):
                        o = open_tile(t).rearrange("p (a c) -> p a c", a=2)
                        for r in range(2):
                            for j in range(NT):
                                mm(o[:, r, :], tabs[:, r, j, f * P:(f + 1) * P], hy_lags[o_][:, j, r * HC:(r + 1) * HC],
                                   j == 0, j == 1, tile_full[t % 4] if r and j else None)
                        t += 1
                    if o_ == 0:
                        for q in (4, 5):
                            read_out(pe, at.tiles + q)
                    else:
                        for q in (0, 1):
                            read_out(pe, plan[f"hy_y{c}0"].tiles + q)
                    t = plan[f"hy_v{c}{o_}"].tiles
                    for f in range(NT):
                        for r in range(2):
                            o = open_tile(t)
                            for j in range(NT):
                                mm(o, tabs[:, r, j, f * P:(f + 1) * P], hy_v[:, j, :], j == 0, j == 1,
                                   tile_full[t % 4] if j else None)
                            t += 1
                    if o_ == 0:
                        filters(1)
                    pe.wait_ge(spectra_ready, plan[f"hy_v{c}{o_}"].spectra + 2)
                    t = plan[f"hy_y{c}{o_}"].tiles
                    for b in range(2):
                        o = open_tile(t)
                        if o_ == 0:
                            for f in range(NT):
                                for r in range(2):
                                    mm(o, tabs[:, 2 + r, f, b * P:(b + 1) * P], hy_spec[:, f, r, :], f + r == 0, f + r == 2,
                                       tile_full[t % 4] if f + r == 2 else None)
                        else:
                            for s in range(2):
                                for f in range(NT):
                                    for r in range(2):
                                        fin = f + r == 2
                                        mm(o[:, s * S:(s + 1) * S], hy_spec[:, f, r, s * HC + b * P:s * HC + (b + 1) * P],
                                           tabs[:, 2 + r, f, :], f + r == 0, fin,
                                           tile_full[t % 4] if fin and s else None, done=int(fin and s == 1 and b == 1))
                        t += 1

            def experts(layer):
                streams = 2 - layer
                m = CAP * streams
                groups = P // m
                tiles = NT * streams
                at = plan[f"router{layer}"]
                t = at.tiles
                o = open_tile(t)
                for i in range(tiles):
                    for k in range(KB):
                        mm(o[:, i * E_N:(i + 1) * E_N], cols_x[:, k, i * P:(i + 1) * P], router_w[:, layer, k, :], k == 0,
                           k == KB - 1, tile_full[t % 4] if i == tiles - 1 and k == KB - 1 else None)
                pe.wait_ge(gates_ready, layer + 1)
                t += 1
                o = open_tile(t)
                for i in range(tiles):
                    turn(o[0:E_N, i * P:(i + 1) * P], gate[:, i, :], tile_full[t % 4] if i == tiles - 1 else None)
                pe.wait_ge(codes_ready, layer + 1)
                t += 1
                o = open_tile(t)
                for i in range(tiles):
                    turn(o[:, i * E_N:(i + 1) * E_N], picked[:, i * P:(i + 1) * P],
                         tile_full[t % 4] if i == tiles - 1 else None, size=E_N)
                pe.wait_ge(choice_ready, layer + 1)
                t = plan[f"gather{layer}"].tiles
                for s in range(streams):
                    for k in range(KB):
                        o = open_tile(t)
                        for j in range(NT):
                            h = h_main[:, j, :] if streams == 2 and s == 0 else rows_h[:, NT * s + j, :]
                            mm(o, h[:, k * P:(k + 1) * P], chosen[:, NT * s + j, :], j == 0, j == 1,
                               tile_full[t % 4] if j else None)
                        t += 1
                per = moe_body_tiles(streams)
                base = plan[f"experts{layer}"]
                lanes = const("lanes4") if groups == 4 else const("lanes2")
                taken_v = taken[:, 0:KB * m].rearrange("p (k c) -> p k c", k=KB)
                gated_v = gated_e[:, 0:KB * m].rearrange("p (k c) -> p k c", k=KB)
                with pe.Fori(0, E_N) as e:
                    more = e * (per // 4)

                    def grouped(t, n, x):
                        o = open_tile(t, more)
                        for half in range(2):
                            landed(n + half, e * 16)
                            w = slot(n + half, 4)
                            for k in range(4):
                                kk = 4 * half + k
                                g = kk % groups
                                fin = kk == KB - 1
                                mm(o[m * g:m * g + m, :], x[:, kk, :], w[:, k, :], kk < groups, kk >= KB - groups,
                                   tile_full[t % 4] if fin else None, done=2 * int(fin), tile_position=(0, m * g))

                    t, n = base.tiles, base.loads
                    pe.wait_ge(taken_ready, base.experts + e + 1)
                    for q in range(4):
                        grouped(t + q, n + 2 * q, taken_v)
                    pe.wait_ge(spread_ready, base.experts + e + 1)
                    for q in range(2):
                        o = open_tile(t + 4 + q, more)
                        for i in range(streams):
                            turn(o[:, i * P:(i + 1) * P], spread_e[:, q * streams + i, :],
                                 tile_full[(t + 4 + q) % 4] if i == streams - 1 else None)
                    for q, (part, first) in enumerate(((gate_part, 0), (gate_part, 4), (up_part, 0), (up_part, 4))):
                        o = open_tile(t + 6 + q, more)
                        for k in range(4):
                            mm(o[:, k * P:(k + 1) * P], part[:, (first + k) * P:(first + k + 1) * P], lanes, True, True,
                               tile_full[(t + 6 + q) % 4] if k == 3 else None)
                    read_out(pe, t + 8, more)
                    read_out(pe, t + 9, more)
                    for q in range(2):
                        grouped(t + 10 + q, n + 8 + 2 * q, gated_v)
                    for cb in range(2):
                        read_out(pe, t + 10 + cb, more)
                        for i in range(tiles):
                            q = t + 12 + tiles * cb + i
                            o = open_tile(q, more)
                            for a in range(2):
                                c0 = a * 256
                                mm(o[:, c0:c0 + 256], spread_cols[:, i, :], down_part[:, cb * 512 + c0:cb * 512 + c0 + 256],
                                   True, True, tile_full[q % 4] if a else None)
                    assert owed[0] == 0

            def da_scores(o, j, h, signal):
                mm(o[:, 0:S], q_lo[:, h, j * P:(j + 1) * P], k_cols[:, h, :], True, False)
                mm(o[:, 0:S], ident, mask[:, j, :], False, True)
                mm(o[:, S:2 * S], q_hi[:, h, j * P:(j + 1) * P], k_cols[:, h, :], True, False)
                mm(o[:, S:2 * S], ident, mask[:, j, :], False, True, signal)

            def xa_scores(o, j, h, signal):
                for a in range(2):
                    mm(o[:, 0:S], q_lo[:, 2 * h + a, j * P:(j + 1) * P], k_cols[:, 2 * h + a, :], a == 0, a == 1,
                       signal if a else None)

            pe.sem_inc(loads_used, RING)
            pe.wait_ge(consts_landed, 16)
            pe.wait_ge(x_landed, 16)
            for j in range(NT):
                turn_rows(plan["x_cols"].tiles + 2 * j, rows_x[:, j, :])
            pe.wait_ge(mem_landed, 16)
            for j in range(NT):
                turn_rows(plan["mem_cols"].tiles + 2 * j, rows_x[:, NT + j, :])
            pe.wait_ge(hy_landed, 16 * 3)
            t = plan["hy_mlp1"].tiles
            mm(open_tile(t)[0:HY_FFN, 0:S], hy_small[0:HY_EMB, 0:HY_FFN], hy_z_in, True, True, tile_full[t % 4])
            pe.wait_ge(cond_ready, 1)
            ffn(0)
            normed_to_cols("ffn_norm0")
            pe.wait_ge(mlp_sines, 1)
            t = plan["hy_mlp2"].tiles
            mm(open_tile(t)[0:HY_FFN, 0:S], hy_small[:, HY_FFN:2 * HY_FFN], hy_h[:, 0, :], True, True, tile_full[t % 4])

            at = plan["da_qkv"]
            rows_out(at.loads, at.tiles, cols_x, 6)
            t = plan["da_turn"].tiles
            for side, src in enumerate((q_rows, k_rows)):
                for j in range(NT):
                    read_out(pe, at.tiles + (2 * side + 1) * NT + j)
                    turn_rows(t, src[:, j, :])
                    t += 2
            pe.wait_ge(padded, 1)
            for q in range(8):
                read_out(pe, plan["da_turn"].tiles + q)
            for q in range(4):
                read_out(pe, at.tiles + 8 + q)
            pe.wait_ge(mask_landed, 16)
            attention("da_att", DA_H, da_scores, lambda k, h: v_rows[:, k, h * P:(h + 1) * P], P, lambda j: j + 1,
                      weighed=True)
            memory_keys("xa_k0a")
            memory_keys("xa_k0b")
            pe.wait_ge(heads_normed, 1)
            out_to_cols("da_cols", "da_att", DA_H)
            out_product("da_out")
            cross_attention(0)
            ffn(1)
            memory_keys("xa_k1a")
            normed_to_cols("ffn_norm1")
            ffn(2)
            memory_keys("xa_k1b")

            at = plan["pool_mix"]
            landed(at.loads)
            band = ring[:, at.loads % RING, :].rearrange("p (s g t) -> p s g t", s=NT, g=4)
            pe.wait_ge(rows_ready, plan["ffn_norm2"].rows + NT)
            for g in range(4):
                o = open_tile(at.tiles + g).rearrange("p (a t) -> p a t", a=2)
                for a in range(2):
                    for s in range(NT):
                        fin = a == 1 and s == NT - 1
                        mm(o[:, a, :], rows_x[:, s, (2 * g + a) * P:(2 * g + a + 1) * P], band[:, s, g, :], s == 0,
                           s == NT - 1, tile_full[(at.tiles + g) % 4] if fin else None, done=int(fin and g == 3))
            out_at = plan["pool_out"]
            landed(out_at.loads)
            acc_open("pool_out")
            all_read(at.tiles)
            w = slot(out_at.loads, 8)
            for j in range(NT):
                for g in range(4):
                    for a in range(2):
                        fin = g == 3 and a == 1
                        mm(acc[:, 2 * j + g // 2, (g % 2) * 256:(g % 2) * 256 + 256],
                           pooled[:, 2 * g + a, j * P:(j + 1) * P], w[:, 2 * g + a, :], a == 0, a == 1,
                           acc_full if fin else None, done=int(fin and j == NT - 1))
            cross_attention(1)
            ffn(3)

            normed_to_cols("mod_norm0", rows_h)
            pe.wait_ge(mlp_sines, 2)
            for c in range(D // HC):
                hyena_step(c)
            for q in range(2):
                read_out(pe, plan[f"hy_y{D // HC - 1}1"].tiles + q)
            n = plan["hy_out0"].loads
            at = plan["moe_norm0"]
            for s in range(2):
                for j in range(NT):
                    tile_to_acc(f"hy_out{s}", n, lambda k, j: hy_z[:, k, s * S + j * P:s * S + (j + 1) * P], j,
                                s == 1 and j == NT - 1)
                    if s == 1 and j == 0:
                        for i in range(NT):
                            pe.wait_ge(rows_ready, at.rows + i + 1)
                            turn_rows(at.tiles + 2 * i, h_main[:, i, :])
            for i in range(NT, 2 * NT):
                pe.wait_ge(rows_ready, at.rows + i + 1)
                turn_rows(at.tiles + 2 * i, rows_h[:, i, :])
            all_read(at.tiles + 4)
            experts(0)

            normed_to_cols("mod_norm1", rows_h)
            at = plan["sw_q"]
            rows_out(at.loads, at.tiles, cols_x, 2)
            for i in range(NT, 2 * NT):
                pe.wait_ge(rows_ready, plan["mod_norm1"].rows + i + 1)
                turn_rows(plan["ctx_cols"].tiles + 2 * (i - NT), rows_h[:, i, :])
            all_read(plan["ctx_cols"].tiles)
            kv = plan["sw_kv"].tiles
            n = plan["sw_kv"].loads
            outs = [open_tile(kv + q) for q in range(2 * NT)]
            for half in range(2):
                landed(n + half)
                w = slot(n + half, 4)
                for q in range(2 * NT):
                    for k in range(4):
                        kk = 4 * half + k
                        mm(outs[q], cols_x[:, kk, q * P:(q + 1) * P], w[:, k, :], kk == 0, kk == KB - 1,
                           tile_full[(kv + q) % 4] if kk == KB - 1 else None, done=int(q == 2 * NT - 1 and k == 3))
            t = plan["sw_turn"].tiles
            for j in range(NT):
                read_out(pe, at.tiles + NT + j)
                turn_rows(t + 2 * j, q_rows[:, j, :])
            all_read(kv)
            t += 4
            for g in range(2):
                o = open_tile(t)
                for k in range(4):
                    turn(o[:, k * P:(k + 1) * P], sw_k_rows[:, k, g * P:(g + 1) * P], tile_full[t % 4] if k == 3 else None)
                t += 1
            for q in range(6):
                read_out(pe, plan["sw_turn"].tiles + q)
            pe.wait_ge(padded, 2)

            def sw_scores(o, j, h, signal):
                g, r = divmod(h, SW_HQ // SW_HKV)
                q = q_hi if g % 2 else q_lo
                queries = q[:, 4 * (g // 2) + r, j * P:(j + 1) * P]
                mm(o[:, 0:S], queries, sw_k_cols[:, g // 2, 0:S], True, True)
                assert SW_WINDOW >= P - 1 and NT == 2
                other = (1 - j) * P
                mm(o[:, S:2 * S], queries, sw_k_cols[:, g // 2, S:2 * S], True, False)
                mm(o[:, S + other:S + other + P], ident, mask[:, j, other:other + P], False, True, signal)

            pe.wait_ge(mask_landed, 32)
            attention("sw_att", SW_HQ, sw_scores, lambda k, h: sw_v[:, k, (h // 4) * SW_HD:(h // 4 + 1) * SW_HD], SW_HD,
                      lambda j: 4, probs=sw_probs, turned_p=sw_turned)
            out_to_cols("sw_cols", "sw_att", SW_HQ)
            out_product("sw_out")
            normed_to_cols("moe_norm1", rows_h, NT)
            experts(1)

        @block.scalar
        def _(act):
            act.dma_start(consts[:, :], io["consts"]).then_inc(consts_landed, 16)
            act.dma_start(rows_x[:, 0:NT, :], io["x"][0].rearrange("(j p) d -> p j d", p=P)).then_inc(x_landed, 16)
            act.dma_start(rows_x[:, NT:2 * NT, :], io["mem"][0].rearrange("(j p) d -> p j d", p=P)).then_inc(mem_landed, 16)
            act.dma_start(act_in[:, :, :], io["cond_cols"].rearrange("p (k s) -> p k s", s=2)).then_inc(cond_landed, 16)

            def copy_tile(t, dst, src):
                filled(act, t)
                nc.scalar.activation(dst, src, ACT.Copy).then_inc(tile_read[t % 4], 1)

            def cols_from_rows(t, tok):
                for piece in range(2):
                    copy_tile(t + piece, cols_x[:, 4 * piece:4 * piece + 4, tok:tok + P],
                              work[:, (t + piece) % 4, :].rearrange("p (k t) -> p k t", k=4))

            def ffn(i):
                at = plan[f"ffn{i}"]
                ada = i < DEPTH

                def run(events, tb, it, tper):
                    tmore = 0 if it is None else it * (tper // 4)
                    for kind, what, dt, _ in events:
                        t = tb + dt
                        if kind == "in":
                            filled(act, t, tmore)
                            nc.scalar.activation(silu_buf[:, (2 * what[0] + what[1]) % 4, :], work[:, t % 4, 0:S],
                                                 ACT.Silu).then_inc(silu_ready, 1)
                        elif kind == "part":
                            filled(act, t, tmore)
                            nc.scalar.activation(ada_part[:, what % 2, :], work[:, t % 4, :],
                                                 ACT.Copy).then_inc(tile_read[t % 4], 1)

                head, t0, _ = ffn_events(range(FFN_HEAD), False)
                body, t1, _ = ffn_events(range(FFN_HEAD, FFN_HEAD + FFN_BODY), ada)
                run(head, at.tiles, None, 0)
                with act.Fori(0, FFN_LOOPS) as it:
                    run(body, at.tiles + t0, it, t1)

            def norm_root(stage, n, i):
                act.wait_ge(var_ready, plan[stage].norms + n + 1)
                nc.scalar.activation(root[:, i:i + 1], spread[:, i:i + 1], ACT.Sqrt).then_inc(root_ready, 1)

            def norm(stage, rooted=0):
                for n in range(NT):
                    if n >= rooted:
                        norm_root(stage, n, n)
                    cols_from_rows(plan[stage].tiles + 2 * n, n * P)

            def rows_to_cols(stage):
                for j in range(NT):
                    cols_from_rows(plan[stage].tiles + 2 * j, j * P)

            def attention(stage, heads, exps, key_tiles, turned_p=turned_p):
                units = NT * heads
                order = attention_order(units)
                at = plan[stage]
                for v in range(units + 2):
                    if v >= 2:
                        u = v - 2
                        t = at.tiles + order["t", u]
                        n = key_tiles(u // heads)
                        copy_tile(t, turned_p[:, u % 2, 0:n, :],
                                  work[:, t % 4, 0:n * P].rearrange("p (k t) -> p k t", k=n))
                    if v < units:
                        act.wait_ge(low_ready, at.units + v + 1)
                        exps(v, at.tiles + order["s", v])

            def da_exps(u, t):
                for c in range(2):
                    ins = nc.scalar.activation(probs[:, u % 2, c * S:(c + 1) * S], work[:, t % 4, c * S:(c + 1) * S],
                                               ACT.Exp, bias=low[:, u % 4, c:c + 1], scale=DA_DK ** -0.5,
                                               accum_out=mass[:, u % 4, c:c + 1])
                ins.then_inc(tile_read[t % 4], 1)

            def xa_exps(u, t):
                nc.scalar.activation(probs[:, u % 2, 0:S], work[:, t % 4, 0:S], ACT.Exp, bias=low[:, u % 4, 0:1],
                                     scale=XA_DK ** -0.5, accum_out=mass[:, u % 4, 0:1]).then_inc(tile_read[t % 4], 1)

            def sw_exps(u, t):
                h = u % SW_HQ
                nc.scalar.activation(sink_exp[:, u % 4:u % 4 + 1], neg_sink[:, h:h + 1], ACT.Exp,
                                     bias=low[:, u % 4, 0:1], scale=-1.0)
                nc.scalar.activation(sw_probs[:, u % 2, :], work[:, t % 4, :], ACT.Exp, bias=low[:, u % 4, 0:1],
                                     scale=SW_HD ** -0.5, accum_out=mass[:, u % 4, 0:1]).then_inc(tile_read[t % 4], 1)

            def turned_queries(t0):
                for j in range(NT):
                    for piece in range(2):
                        t = t0 + 2 * j + piece
                        src = work[:, t % 4, :].rearrange("p (k t) -> p k t", k=4)
                        filled(act, t)
                        nc.scalar.activation(q_lo[0:64, 4 * piece:4 * piece + 4, j * P:(j + 1) * P], src[0:64], ACT.Copy)
                        nc.scalar.activation(q_hi[64:128, 4 * piece:4 * piece + 4, j * P:(j + 1) * P], src[64:128],
                                             ACT.Copy).then_inc(tile_read[t % 4], 1)

            def experts(layer):
                streams = 2 - layer
                m = CAP * streams
                tiles = NT * streams
                t = plan[f"router{layer}"].tiles
                act.wait_ge(logits_low, layer + 1)
                nc.scalar.activation(logit[:, 0:tiles, :], logit[:, 0:tiles, :], ACT.Exp).then_inc(logits_exp, 1)
                copy_tile(t + 1, aff[:, 0:tiles * P], work[0:E_N, (t + 1) % 4, 0:tiles * P])
                t = plan[f"gather{layer}"].tiles
                for s in range(streams):
                    for k in range(KB):
                        copy_tile(t, xe[s][:, k, :], work[:, t % 4, :])
                        t += 1
                per = moe_body_tiles(streams)
                base = plan[f"experts{layer}"]
                for q in range(4):
                    read_out(act, base.tiles - 1 - q)
                with act.Fori(0, E_N) as e:
                    t = base.tiles
                    more = e * (per // 4)

                    def copy(q, dst, src):
                        filled(act, t + q, more)
                        nc.scalar.activation(dst, src, ACT.Copy).then_inc(tile_read[(t + q) % 4], 1)

                    tk = taken[:, 0:KB * m].rearrange("p (k c) -> p k c", k=KB)
                    for s in range(streams):
                        ins = nc.scalar.activation(tk[:, :, s * CAP:(s + 1) * CAP], xe[s][:, :, bass.ds(e * CAP, CAP)], ACT.Copy)
                    ins.then_inc(taken_ready, 1)
                    for q in range(2):
                        copy(q, gate_part[:, q * 512:q * 512 + 512], work[:, (t + q) % 4, :])
                    for q in range(2):
                        copy(4 + q, spread_cols[:, q * streams:(q + 1) * streams, :],
                             work[:, (t + 4 + q) % 4, 0:streams * P].rearrange("p (i t) -> p i t", i=streams))
                    sv = silu_e[:, 0:KB * m].rearrange("p (k c) -> p k c", k=KB)
                    for q in range(2):
                        b = t + 6 + q
                        filled(act, b, more)
                        nc.scalar.activation(sv[:, 4 * q:4 * q + 4, :],
                                             work[:, b % 4, :].rearrange("p (k c) -> p k c", k=4)[:, :, 0:m],
                                             ACT.Silu).then_inc(tile_read[b % 4], 1)
                    copy(10, down_part[:, 0:512], work[:, (t + 10) % 4, :])

            def memory_keys(stage, half):
                for q in range(2):
                    t, b = plan[stage].tiles + q, 4 * half + 2 * q
                    copy_tile(t, k_cols[:, b:b + 2, :], work[:, t % 4, :].rearrange("p (a t) -> p a t", a=2))

            def cross_attention(i):
                at = plan[f"xa_v{i}"]
                for q in range(4):
                    copy_tile(at.tiles + q, v_rows[:, q % 2, (q // 2) * 512:(q // 2) * 512 + 512],
                              work[:, (at.tiles + q) % 4, :])
                norm(f"mix_norm{i}")
                at = plan[f"xa_q{i}"]
                for q in range(4):
                    copy_tile(at.tiles + q, q_lo[:, 2 * q:2 * q + 2, :],
                              work[:, (at.tiles + q) % 4, :].rearrange("p (a t) -> p a t", a=2))
                attention(f"xa_att{i}", XA_H, xa_exps, lambda j: NT)
                rows_to_cols(f"xa_cols{i}")
                if i == 1:
                    for j in range(NT):
                        norm_root("ctx_norm", j, NT + j)
                    norm_root("xa_norm1", 0, 0)
                    for j in range(NT):
                        cols_from_rows(plan["ctx_norm"].tiles + 2 * j, (NT + j) * P)
                    norm("xa_norm1", rooted=1)
                else:
                    norm("xa_norm0")

            act.wait_ge(cond_landed, 16)
            act.wait_ge(cond_zeroed, 1)
            nc.scalar.activation(act_col[:, :, 0:2], act_in[:, :, :], ACT.Silu).then_inc(cond_ready, 1)
            rows_to_cols("x_cols")
            for j in range(NT):
                cols_from_rows(plan["mem_cols"].tiles + 2 * j, S + j * P)
            ffn(0)
            act.wait_ge(mlp_angles, 1)
            nc.scalar.activation(hy_h[:, 0, :], hy_h[:, 0, :], ACT.Sin).then_inc(mlp_sines, 1)
            act.wait_ge(angles_ready, 1)
            nc.scalar.activation(da_cs[:, :, :, :], angle[:, :, :, :], ACT.Sin).then_inc(sines_ready, 1)
            act.wait_ge(lam_sums, 1)
            nc.scalar.activation(lam[:, 2:4], lam[:, 0:2], ACT.Exp).then_inc(lam_exp, 1)
            norm("ffn_norm0")
            act.wait_ge(mlp_angles, 2)
            nc.scalar.activation(hy_h[:, 1, :], hy_h[:, 1, :], ACT.Sin).then_inc(mlp_sines, 1)

            turned_at = plan["da_turn"].tiles
            act.wait_ge(padded, 1)
            turned_queries(turned_at)
            for j in range(NT):
                for piece in range(2):
                    t = turned_at + 4 + 2 * j + piece
                    copy_tile(t, k_cols[:, 4 * piece:4 * piece + 4, j * P:(j + 1) * P],
                              work[:, t % 4, :].rearrange("p (k t) -> p k t", k=4))
            attention("da_att", DA_H, da_exps, lambda j: j + 1)
            act.wait_ge(var_ready, plan["da_cols"].norms + 1)
            nc.scalar.activation(head_sq[:, 1, :], head_sq[:, 0, :], ACT.Sqrt).then_inc(root_ready, 1)
            memory_keys("xa_k0a", 0)
            memory_keys("xa_k0b", 1)
            rows_to_cols("da_cols")
            cross_attention(0)
            ffn(1)
            for j in range(NT):
                norm_root("ffn_norm1", j, j)
            act.wait_ge(mods_stored, 32)
            memory_keys("xa_k1a", 0)
            norm("ffn_norm1", rooted=NT)
            ffn(2)
            for j in range(NT):
                norm_root("ffn_norm2", j, j)
            memory_keys("xa_k1b", 1)
            at = plan["pool_mix"]
            for q in range(4):
                copy_tile(at.tiles + q, pooled[:, 2 * q:2 * q + 2, :],
                          work[:, (at.tiles + q) % 4, :].rearrange("p (a t) -> p a t", a=2))
            cross_attention(1)
            ffn(3)
            for j in range(NT):
                norm_root("ffn_norm3", j, j)
            norm("mod_norm0")
            for c in range(D // HC):
                t = plan[f"hy_u{c}"].tiles
                convs = plan[f"hy_u{c}"].convs

                def add_bias(section):
                    nonlocal t
                    for a in range(2):
                        done = 2 * section + a
                        filled(act, t)
                        if done >= 2:
                            act.wait_ge(conv_ready, convs + done - 1)
                        b = section * KB + 2 * c + a
                        nc.scalar.activation(hy_biased[:, a, :], work[:, t % 4, :], ACT.Identity,
                                             bias=hy_cols[:, b, 0:1]).then_inc(tile_read[t % 4], 1)
                        t += 1

                def copy_turned(dst):
                    nonlocal t
                    for j in range(NT):
                        copy_tile(t, dst[:, j, :], work[:, t % 4, :])
                        t += 1

                add_bias(0)
                add_bias(1)
                copy_turned(hy_v)
                t = plan[f"hy_w{c}"].tiles
                add_bias(2)
                copy_turned(hy_x1)
            at = plan["moe_norm0"]
            for s in range(2):
                for i in range(NT * s, NT * (s + 1)):
                    norm_root("moe_norm0", i, i)
                for i in range(NT * s, NT * (s + 1)):
                    cols_from_rows(at.tiles + 2 * i, i * P)
            experts(0)

            norm("mod_norm1")
            for j in range(NT):
                norm_root("mod_norm1", NT + j, NT + j)
            for j in range(NT):
                cols_from_rows(plan["ctx_cols"].tiles + 2 * j, (NT + j) * P)
            t = plan["sw_turn"].tiles
            act.wait_ge(padded, 2)
            turned_queries(t)
            for g in range(2):
                copy_tile(t + 4 + g, sw_k_cols[:, g, :], work[:, (t + g) % 4, :])
            attention("sw_att", SW_HQ, sw_exps, lambda j: 4, turned_p=sw_turned)
            rows_to_cols("sw_cols")
            norm("moe_norm1")
            experts(1)
            for j in range(NT):
                norm_root("last_norm", j, j)

        @block.vector
        def _(dve):
            step = Steps(dve, vec_steps)
            next_row = [0]
            returned = [0]

            def param_row():
                r = next_row[0]
                next_row[0] += 1
                dve.wait_ge(row_landed[r % PR_RING], 16 * (r // PR_RING + 1))
                return prow[:, r % PR_RING, :]

            def split(high, low, x):
                step(nc.vector.tensor_copy(high, x))
                step.settle()
                return nc.vector.tensor_tensor(low, x, high.bitcast(F32), ALU.subtract)

            def split_load(n, turns, more):
                dve.wait_ge(load_landed[n % RING], 16 * (n // RING + 1) + 16 * turns)
                dve.wait_ge(loads_used, n + 2 + more)
                w, low, high = ring[:, n % RING, :], ring_parts[:, n % RING, :], ring_parts[:, (n + 1) % RING, :]
                arrived = load_landed[(n + 1) % RING]
                nc.vector.tensor_copy(high, w).then_inc(arrived, 16)
                dve.wait_ge(arrived, 16 * ((n + 1) // RING + 1) + 16 * turns)
                nc.vector.tensor_tensor(low, w, high.bitcast(F32), ALU.subtract).then_inc(split_ready, 1)

            def newton_root(v, s, r, tmp):
                step(nc.vector.reciprocal(r, s))
                step.settle()
                step(nc.vector.tensor_tensor(tmp, r, r, ALU.mult))
                step.settle()
                step(nc.vector.tensor_tensor(tmp, tmp, v, ALU.mult))
                step.settle()
                step(nc.vector.tensor_scalar(tmp, tmp, -0.5, 1.5, ALU.mult, ALU.add))
                step.settle()
                step(nc.vector.tensor_tensor(r, r, tmp, ALU.mult))
                step.settle()

            split_ahead = [0] * (2 * DEPTH)

            def split_first(i, loads):
                for k in range(split_ahead[i], loads):
                    split_load(plan[f"ffn{i}"].loads + 2 * k, 0, 0)
                split_ahead[i] = loads

            def ffn(i, first=None, between=None):
                at = plan[f"ffn{i}"]
                ada = i < DEPTH

                def gate(m, t, tmore, smore):
                    dve.wait_ge(silu_ready, at.silu + m + 1 + smore)
                    g = gated[:, m % 4, :]
                    step(nc.vector.tensor_tensor(g, silu_buf[:, m % 4, :], work[:, t % 4, S:2 * S], ALU.mult))
                    step.settle()
                    split(gated_high[:, m % 4, :], gated_low[:, m % 4, :], g).then_inc(tile_read[t % 4], 1)

                def run(events, tb, lb, it, tper, lper):
                    tmore = 0 if it is None else it * (tper // 4)
                    smore = 0 if it is None else it * (2 * FFN_BODY)
                    cmore = 0 if it is None else it * ADA_PER_BODY
                    lmore = 0 if it is None else it * (lper // RING)
                    more = 0 if it is None else it * lper
                    before = tb - 2
                    for kind, what, dt, dn in sums_last(events):
                        t = tb + dt
                        if kind == "in":
                            m = 2 * what[0] + what[1]
                            if m >= 2:
                                split_load(lb + dn + 2 * what[1], lmore, more)
                            if what[0] > 0:
                                gate(m - 2, before + what[1], tmore, smore)
                            if what[1]:
                                before = t - 1
                        elif kind == "out":
                            split_load(lb + dn, lmore, more)
                        elif kind == "sum":
                            filled(dve, t, tmore)
                            there = mods[0:2, bass.ds((what + cmore) * 512, 512)]
                            nc.vector.tensor_tensor(there, there, work[0:2, t % 4, :],
                                                    ALU.add).then_inc(tile_read[t % 4], 1)

                split_first(i, 2)
                source = plan[("x_cols", "xa_norm0", "ffn_norm1", "xa_norm1")[i]].tiles
                for j in range(NT):
                    for piece in range(2):
                        read_out(dve, source + 2 * j + piece)
                        k, c = slice(4 * piece, 4 * piece + 4), slice(j * P, (j + 1) * P)
                        ins = split(x_high[:, k, c], x_low[:, k, c], cols_x[:, k, c])
                        if piece == 0:
                            step(ins)
                    ins.then_inc(x_split, 1)
                if first is not None:
                    first()
                head, t0, l0 = ffn_events(range(FFN_HEAD), False)
                body, t1, l1 = ffn_events(range(FFN_HEAD, FFN_HEAD + FFN_BODY), ada)
                run(head, at.tiles, at.loads, None, 0, 0)
                if between is not None:
                    between()
                if ada:
                    dve.wait_ge(ada_bias_landed, 16 * (i + 1))
                with dve.Fori(0, FFN_LOOPS) as it:
                    step.loop_in(it, 2 * 2 * FFN_BODY)
                    run(body, at.tiles + t0, at.loads + l0, it, t1, l1)
                    step.loop_out(FFN_LOOPS)
                t = at.tiles + t0 + FFN_LOOPS * t1 - 2
                for h in range(2):
                    gate(2 * FSTEPS - 2 + h, t + h, 0, 0)
                split_load(at.loads + l0 + FFN_LOOPS * l1, 0, 0)

            def layer_norm(stage, acc_stage, x_scale, eps, prepare=None):
                at, use = plan[stage], plan[acc_stage].acc
                for j in range(NT):
                    dve.wait_ge(acc_full, NT * use + j + 1)
                    if prepare is not None:
                        prepare(j)
                    else:
                        for h in range(2):
                            x = rows_x[:, j, h * 512:(h + 1) * 512]
                            ins = nc.vector.scalar_tensor_tensor(out=x, in0=x, scalar=x_scale, in1=acc[:, 2 * j + h, :],
                                                                 op0=ALU.mult, op1=ALU.add)
                        ins.then_inc(acc_read, 1)
                        dve.wait_ge(acc_read, NT * use + j + 1)
                    x = rows_x[:, j, :]
                    for h in range(2):
                        step(nc.vector.bn_stats(stats[:, j, h, :], rows_x[:, j, h * 512:(h + 1) * 512]))
                    step.settle()
                    step(nc.vector.bn_aggr(mean_var[:, j, :], stats[:, j, :, :]))
                    step.settle()
                    nc.vector.tensor_scalar(spread[:, j:j + 1], mean_var[:, j, 1:2], eps, None, ALU.add).then_inc(var_ready, 1)
                    if j == 0:
                        gain = param_row()
                    step(nc.vector.scalar_tensor_tensor(out=x, in0=x, scalar=mean_var[:, j, 0:1], in1=gain,
                                                        op0=ALU.subtract, op1=ALU.mult))
                    tile_root(at.norms + j + 1, j)
                    if j == 0:
                        bias = param_row()
                    nc.vector.scalar_tensor_tensor(out=x, in0=x, scalar=rstd[:, j:j + 1], in1=bias, op0=ALU.mult,
                                                   op1=ALU.add).then_inc(rows_ready, 1)
                    dve.wait_ge(rows_ready, at.rows + j + 1)
                give_back(2)

            def tile_root(norms, i):
                dve.wait_ge(root_ready, norms)
                c = slice(i, i + 1)
                newton_root(spread[:, c], root[:, c], rstd[:, c], newton[:, c])

            def mod_norm(stage, streams, mix=None, out_bias=False, last=False, dst=lambda i: rows_h[:, i, :]):
                at = plan[stage]
                n = 0

                def norm_tile(i, factor, shift):
                    nonlocal n
                    x, h, c = rows_x[:, i, :], dst(i), slice(i, i + 1)
                    for half in range(2):
                        step(nc.vector.bn_stats(stats[:, i % 2, half, :], rows_x[:, i, half * 512:(half + 1) * 512]))
                    step.settle()
                    step(nc.vector.bn_aggr(mean_var[:, i, :], stats[:, i % 2, :, :]))
                    step.settle()
                    step(nc.vector.tensor_tensor(spread[:, c], mean_var[:, i, 0:1], mean_var[:, i, 0:1], ALU.mult))
                    step.settle()
                    nc.vector.scalar_tensor_tensor(out=spread[:, c], in0=mean_var[:, i, 1:2], scalar=EPS, in1=spread[:, c],
                                                   op0=ALU.add, op1=ALU.add).then_inc(var_ready, 1)
                    if not last:
                        step(nc.vector.tensor_tensor(h, x, factor, ALU.mult))
                    tile_root(at.norms + n + 1, i)
                    if last:
                        ins = nc.vector.scalar_tensor_tensor(out=h, in0=x, scalar=rstd[:, c], in1=factor, op0=ALU.mult,
                                                             op1=ALU.mult)
                    else:
                        ins = nc.vector.scalar_tensor_tensor(out=h, in0=h, scalar=rstd[:, c], in1=shift, op0=ALU.mult,
                                                             op1=ALU.add)
                    ins.then_inc(rows_ready, 1)
                    n += 1
                    dve.wait_ge(rows_ready, at.rows + n)

                for s in streams:
                    mine = range(NT * s, NT * (s + 1))
                    if mix is not None:
                        scale = param_row()
                    if out_bias:
                        bias = param_row()
                        step(nc.vector.tensor_tensor(bias, bias, scale, ALU.mult))
                        step.settle()
                        for i in mine:
                            step(nc.vector.tensor_tensor(rows_x[:, i, :], rows_x[:, i, :], bias, ALU.add))
                    factor, shift = param_row(), None
                    if not last:
                        gain, factor = factor, param_row()
                        step(nc.vector.scalar_tensor_tensor(out=factor, in0=factor, scalar=1.0, in1=gain, op0=ALU.add,
                                                            op1=ALU.mult))
                    step.settle()
                    if out_bias:
                        for i in mine:
                            mix(i, scale)
                        give_back(2)
                    for i in mine:
                        if mix is not None and not out_bias:
                            mix(i, scale)
                        if not last and shift is None:
                            shift = param_row()
                        norm_tile(i, factor, shift)
                    give_back(2 * int(not last) + 1 + int(mix is not None and not out_bias))

            def give_back(rows):
                step.settle()
                nc.vector.tensor_copy(newton[:, 0:1], rstd[:, 0:1]).then_inc(rows_used, rows)
                returned[0] += rows
                dve.wait_ge(rows_used, returned[0])

            def attention(stage, heads, begin, weigh, width, weighed=False):
                units = NT * heads
                order = attention_order(units)
                at = plan[stage]
                for v in range(units + 3):
                    if v < units:
                        begin(v, at.tiles + order["s", v], v // heads, v % heads)
                    if 0 <= v - 1 < units:
                        read_out(dve, at.tiles + order["s", v - 1])
                        weigh(v - 1)
                    if v >= 3:
                        u = v - 3
                        j, h = divmod(u, heads)
                        t = at.tiles + order["o", u]
                        if v >= units:
                            step.settle()
                        filled(dve, t)
                        dst, src = q_rows[:, j, h * width:(h + 1) * width], work[:, t % 4, 0:width]
                        if weighed:
                            ins = nc.vector.tensor_copy(dst, src)
                        else:
                            ins = nc.vector.tensor_scalar(dst, src, share[:, u % 4, 0:1], None, ALU.mult)
                        ins.then_inc(tile_read[t % 4], 1)

            def da_begin(u, t, j, h):
                filled(dve, t)
                step(nc.vector.tensor_reduce(peak[:, u % 4, :], work[:, t % 4, :].rearrange("p (c k) -> p c k", c=2),
                                             AX_X, ALU.max))
                step.settle()
                nc.vector.tensor_scalar(low[:, u % 4, :], peak[:, u % 4, :], -DA_DK ** -0.5, None,
                                        ALU.mult).then_inc(low_ready, 1)

            def da_weigh(u):
                s = share[:, u % 4, :]
                step(nc.vector.reciprocal(s, mass[:, u % 4, :]))
                step.settle()
                step(nc.vector.tensor_tensor(s[:, 1:2], s[:, 1:2], lam[:, 0:1], ALU.mult))
                first, second = probs[:, u % 2, 0:S], probs[:, u % 2, S:2 * S]
                step(nc.vector.tensor_scalar(first, first, s[:, 0:1], None, ALU.mult))
                step.settle()
                nc.vector.scalar_tensor_tensor(out=first, in0=second, scalar=s[:, 1:2], in1=first, op0=ALU.mult,
                                               op1=ALU.add).then_inc(share_ready, 1)

            def xa_begin(u, t, j, h):
                filled(dve, t)
                step(nc.vector.tensor_reduce(peak[:, u % 4, 0:1], work[:, t % 4, 0:S], AX_X, ALU.max))
                step.settle()
                nc.vector.tensor_scalar(low[:, u % 4, 0:1], peak[:, u % 4, 0:1], -XA_DK ** -0.5, None,
                                        ALU.mult).then_inc(low_ready, 1)

            def xa_weigh(u):
                step(nc.vector.reciprocal(share[:, u % 4, 0:1], mass[:, u % 4, 0:1]))

            def cross_attention(i):
                attention(f"xa_att{i}", XA_H, xa_begin, xa_weigh, XA_DK)
                if i == 1:
                    dve.wait_ge(ctx_landed, 16)
                    mod_norm("ctx_norm", [1])
                split_first(2 * i + 1, 2)
                layer_norm(f"xa_norm{i}", f"xa_out{i}", ALPHA, LN_EPS)

            def wrapped_angle(a, turns):
                step(nc.vector.tensor_scalar(turns, turns, MAGIC, MAGIC, ALU.add, ALU.subtract))
                step.settle()
                for part in two_pi_parts():
                    step(nc.vector.scalar_tensor_tensor(out=a, in0=turns, scalar=-part, in1=a, op0=ALU.mult, op1=ALU.add))
                    step.settle()

            def mlp_layer(n):
                t = plan[f"hy_mlp{n + 1}"].tiles
                filled(dve, t)
                a = hy_h[:, n, :]
                c = 2 * HY_FFN
                nc.vector.tensor_scalar(a, work[0:HY_FFN, t % 4, 0:S], hy_small[:, c + n:c + n + 1],
                                        hy_small[:, c + 2 + n:c + 3 + n], ALU.add, ALU.mult).then_inc(tile_read[t % 4], 1)
                read_out(dve, t)
                turns = mlp_turns[:, :]
                step(nc.vector.tensor_scalar(turns, a, 1.0 / TWO_PI, None, ALU.mult))
                step.settle()
                wrapped_angle(a, turns)
                nc.vector.tensor_scalar(a, a, PI_BELOW, -PI_BELOW, ALU.min, ALU.max).then_inc(mlp_angles, 1)

            def lags(c, o):
                at = plan[f"hy_f{c}{o}"]
                t = at.tiles
                tmp = hy_lags_tmp[o]
                for j in range(NT):
                    filled(dve, t)
                    src = work[:, t % 4, :].rearrange("p (a c) -> p a c", a=2)
                    step(nc.vector.tensor_tensor(tmp[:, 0, :], src[:, 0, :], hy_window[:, j, :], ALU.mult))
                    nc.vector.scalar_tensor_tensor(out=tmp[:, 1, :], in0=src[:, 1, :], scalar=const("not_first")[:, j:j + 1],
                                                   in1=hy_window[:, j, :], op0=ALU.mult,
                                                   op1=ALU.mult).then_inc(tile_read[t % 4], 1)
                    read_out(dve, t)
                    step.settle()
                    step(nc.vector.tensor_tensor(hy_lags[o][:, j, 0:HC], tmp[:, 0, :], tmp[:, 1, :], ALU.add))
                    nc.vector.tensor_tensor(hy_lags[o][:, j, HC:2 * HC], tmp[:, 0, :], tmp[:, 1, :],
                                            ALU.subtract).then_inc(lags_ready, 1)
                    dve.wait_ge(lags_ready, at.lags + j + 1)
                    step.settle()
                    t += 1

            def hyena_step(c, biases):
                t = plan[f"hy_u{c}"].tiles
                dve.wait_ge(window_landed, 16 * (c + 1))
                for section in range(3):
                    if section == 2:
                        lags(c, 0)
                        t = plan[f"hy_w{c}"].tiles
                    for a in range(2):
                        m = 2 * section + a
                        b = section * KB + 2 * c + a
                        read_out(dve, t)
                        x = hy_biased[:, a, :].rearrange("p (s t) -> p s t", s=2)
                        y = (hy_y[:, m, :] if section < 2 else hy_x2[:, a, :]).rearrange("p (s t) -> p s t", s=2)
                        step(nc.vector.tensor_scalar(y, x, hy_cols[:, b, 3:4], hy_cols[:, b, 1:2], ALU.mult, ALU.add))
                        step.settle()
                        step(nc.vector.scalar_tensor_tensor(out=y[:, :, 1:S], in0=x[:, :, 0:S - 1], scalar=hy_cols[:, b, 2:3],
                                                            in1=y[:, :, 1:S], op0=ALU.mult, op1=ALU.add))
                        step.settle()
                        nc.vector.scalar_tensor_tensor(out=y[:, :, 0:S - 1], in0=x[:, :, 1:S], scalar=hy_cols[:, b, 4:5],
                                                       in1=y[:, :, 0:S - 1], op0=ALU.mult, op1=ALU.add).then_inc(conv_ready, 1)
                        t += 1
                dve.wait_ge(conv_ready, plan[f"hy_u{c}"].convs + 6)
                for o in range(2):
                    t = plan[f"hy_k{c}{o}"].tiles
                    for f in range(NT):
                        filled(dve, t)
                        src = work[:, t % 4, :].rearrange("p (a c) -> p a c", a=2)
                        step(nc.vector.tensor_tensor(hy_k[:, f, 0, :], src[:, 0, :], biases[o][:, c * HC:(c + 1) * HC], ALU.add))
                        nc.vector.tensor_copy(hy_k[:, f, 1, :], src[:, 1, :]).then_inc(tile_read[t % 4], 1)
                        read_out(dve, t)
                        t += 1
                    step.settle()
                    at = plan[f"hy_v{c}{o}"]
                    t = at.tiles
                    both = hy_tmp.rearrange("p (s c) -> p s c", s=2)
                    for f in range(NT):
                        vr = work[:, t % 4, :].rearrange("p (s c) -> p s c", s=2)
                        vi = work[:, (t + 1) % 4, :].rearrange("p (s c) -> p s c", s=2)
                        kr = hy_k[:, f, 0:1, :].broadcast_to([P, 2, HC])
                        ki = hy_k[:, f, 1:2, :].broadcast_to([P, 2, HC])
                        yr = hy_spec[:, f, 0, :].rearrange("p (s c) -> p s c", s=2)
                        yi = hy_spec[:, f, 1, :].rearrange("p (s c) -> p s c", s=2)
                        filled(dve, t)
                        step(nc.vector.tensor_tensor(yr, vr, kr, ALU.mult))
                        nc.vector.tensor_tensor(yi, vr, ki, ALU.mult).then_inc(tile_read[t % 4], 1)
                        filled(dve, t + 1)
                        step(nc.vector.tensor_tensor(both, vi, ki, ALU.mult))
                        step.settle()
                        step(nc.vector.tensor_tensor(yr, yr, both, ALU.subtract))
                        step.settle()
                        nc.vector.tensor_tensor(both, vi, kr, ALU.mult).then_inc(tile_read[(t + 1) % 4], 1)
                        read_out(dve, t)
                        read_out(dve, t + 1)
                        nc.vector.tensor_tensor(yi, yi, both, ALU.add).then_inc(spectra_ready, 1)
                        dve.wait_ge(spectra_ready, at.spectra + f + 1)
                        t += 2
                    if o == 0:
                        lags(c, 1)
                    t = plan[f"hy_y{c}{o}"].tiles
                    for b in range(2):
                        filled(dve, t)
                        if o == 0:
                            if b == 0:
                                for q in (2, 3):
                                    read_out(dve, plan[f"hy_w{c}"].tiles + q)
                            nc.vector.tensor_tensor(hy_v[:, b, :], work[:, t % 4, :], hy_x1[:, b, :],
                                                    ALU.mult).then_inc(tile_read[t % 4], 1)
                        else:
                            nc.vector.tensor_tensor(hy_z[:, 2 * c + b, :], work[:, t % 4, :], hy_x2[:, b, :],
                                                    ALU.mult).then_inc(tile_read[t % 4], 1)
                        t += 1
                nc.vector.tensor_copy(newton[:, 0:1], hy_window[:, 0, 0:1]).then_inc(filters_done, 1)

            def add_product(name):
                def mix(i, scale):
                    at, j = plan[name(i // NT)], i % NT
                    dve.wait_ge(acc_full, NT * at.acc + j + 1)
                    step.settle()
                    nc.vector.tensor_tensor(mix_tmp, acc[:, 2 * j:2 * j + 2, :].rearrange("p a c -> p (a c)"), scale,
                                            ALU.mult).then_inc(acc_read, 1)
                    dve.wait_ge(acc_read, NT * at.acc + j + 1)
                    step(nc.vector.tensor_tensor(rows_x[:, i, :], rows_x[:, i, :], mix_tmp, ALU.add))
                    step.settle()

                return mix

            def add_rows(i, scale):
                step.settle()
                step(nc.vector.tensor_tensor(rows_h[:, i, :], rows_h[:, i, :], scale, ALU.mult))
                step.settle()
                step(nc.vector.tensor_tensor(rows_x[:, i, :], rows_x[:, i, :], rows_h[:, i, :], ALU.add))
                step.settle()

            def experts(layer):
                streams = 2 - layer
                m = CAP * streams
                groups = P // m
                tiles = NT * streams
                t = plan[f"router{layer}"].tiles
                filled(dve, t)
                src = work[:, t % 4, 0:tiles * E_N].rearrange("p (i e) -> p i e", i=tiles)
                lg = logit[:, 0:tiles, :]
                pk = logit_peak[:, 0:tiles]
                step(nc.vector.tensor_reduce(pk, src, AX_X, ALU.max))
                step.settle()
                nc.vector.tensor_tensor(lg, src, pk.unsqueeze(2).broadcast_to([P, tiles, E_N]), ALU.subtract)                    .then_inc(tile_read[t % 4], 1)
                read_out(dve, t)
                nc.vector.tensor_copy(newton[:, 0:1], pk[:, 0:1]).then_inc(logits_low, 1)
                dve.wait_ge(logits_exp, layer + 1)
                step(nc.vector.tensor_reduce(pk, lg, AX_X, ALU.add))
                step.settle()
                step(nc.vector.reciprocal(pk, pk))
                step.settle()
                nc.vector.tensor_tensor(gate[:, 0:tiles, :], lg, pk.unsqueeze(2).broadcast_to([P, tiles, E_N]), ALU.mult)                    .then_inc(gates_ready, 1)
                step(nc.vector.memset(zeros16, 0.0))
                read_out(dve, t + 1)
                step(nc.vector.tensor_copy(left[:, 0:tiles * P], aff[:, 0:tiles * P]))
                step.settle()
                for s in range(streams):
                    mine = left[:, s * S:(s + 1) * S]
                    for _ in range(CAP // 8):
                        step(nc.vector.max(top8[:, :], mine))
                        step.settle()
                        step(nc.vector.match_replace(mine, top8[:, :], mine, -1.0))
                        step.settle()
                step(nc.vector.tensor_scalar(picked[:, 0:tiles * P], left[:, 0:tiles * P], 0.0, None, ALU.is_lt))
                step.settle()
                for s in range(streams):
                    step(nc.vector.tensor_tensor_scan(count[:, s * S:(s + 1) * S], picked[:, s * S:(s + 1) * S],
                                                      zeros16[:, 0:S], 0.0, ALU.add, ALU.add))
                step.settle()
                nc.vector.tensor_tensor(picked[:, 0:tiles * P], picked[:, 0:tiles * P], count[:, 0:tiles * P], ALU.mult)                    .then_inc(codes_ready, 1)
                filled(dve, t + 2)
                nc.vector.tensor_copy(codes[:, 0:tiles, :], work[:, (t + 2) % 4, 0:tiles * E_N].rearrange("p (i e) -> p i e", i=tiles))                    .then_inc(tile_read[(t + 2) % 4], 1)
                read_out(dve, t + 2)
                for i in range(tiles):
                    ins = nc.vector.tensor_tensor(chosen[:, i, :].rearrange("p (e c) -> p e c", e=E_N),
                                                  codes[:, i, :].unsqueeze(2).broadcast_to([P, E_N, CAP]),
                                                  const("iota").unsqueeze(1).broadcast_to([P, E_N, CAP]), ALU.is_equal)
                    if i < tiles - 1:
                        step(ins)
                ins.then_inc(choice_ready, 1)
                dve.wait_ge(choice_ready, layer + 1)
                per = moe_body_tiles(streams)
                base = plan[f"experts{layer}"]
                read_out(dve, base.tiles - 1)
                step(nc.vector.memset(rows_h[:, 0:tiles, :], 0.0))
                step(nc.vector.memset(spread_e[:, :, :], 0.0))
                step.settle()
                with dve.Fori(0, E_N) as e:
                    t = base.tiles
                    more = e * (per // 4)
                    for i in range(tiles):
                        s = i // NT
                        dst = spread_e[:, i, :].rearrange("p (g s c) -> p g s c", g=groups, s=streams)[:, :, s, :]
                        ins = nc.vector.tensor_scalar(dst, const("iota").unsqueeze(1).broadcast_to([P, groups, CAP]),
                                                      codes[:, i, bass.ds(e, 1)], gate[:, i, bass.ds(e, 1)],
                                                      ALU.is_equal, ALU.mult)
                    ins.then_inc(spread_ready, 1)
                    for q in range(2):
                        b = t + 2 + q
                        filled(dve, b, more)
                        nc.vector.tensor_copy(up_part[:, q * 512:q * 512 + 512], work[:, b % 4, :]).then_inc(tile_read[b % 4], 1)
                    gv = gated_e[:, 0:KB * m].rearrange("p (k c) -> p k c", k=KB)
                    sv = silu_e[:, 0:KB * m].rearrange("p (k c) -> p k c", k=KB)
                    for q in range(2):
                        b = t + 8 + q
                        filled(dve, b, more)
                        read_out(dve, t + 6 + q, more)
                        nc.vector.tensor_tensor(gv[:, 4 * q:4 * q + 4, :], sv[:, 4 * q:4 * q + 4, :],
                                                work[:, b % 4, :].rearrange("p (k c) -> p k c", k=4)[:, :, 0:m],
                                                ALU.mult).then_inc(tile_read[b % 4], 1)
                    b = t + 11
                    filled(dve, b, more)
                    nc.vector.tensor_copy(down_part[:, 512:1024], work[:, b % 4, :]).then_inc(tile_read[b % 4], 1)
                    for cb in range(2):
                        for i in range(tiles):
                            b = t + 12 + tiles * cb + i
                            filled(dve, b, more)
                            there = rows_h[:, i, cb * 512:cb * 512 + 512]
                            nc.vector.tensor_tensor(there, there, work[:, b % 4, :], ALU.add).then_inc(tile_read[b % 4], 1)
                for q in range(4):
                    read_out(dve, base.tiles + E_N * per - 1 - q)

            step(nc.vector.memset(act_col[:, :, :], 0.0))
            step.settle()
            nc.vector.memset(newton[:, :], 0.0).then_inc(cond_zeroed, 1)

            def small_tables():
                dve.wait_ge(consts_landed, 16)
                dve.wait_ge(small_landed, 16 * 4)
                step(nc.vector.tensor_copy(pos_f[:, :], pos_i[:, :]))
                step.settle()
                for c in range(2):
                    for j in range(NT):
                        step(nc.vector.tensor_scalar(angle[:, c, j, :], const("da_inv"), pos_f[:, j:j + 1], None, ALU.mult))
                step.settle()
                for c in range(2):
                    step(nc.vector.tensor_scalar(turns[:, c, :, :], angle[:, c, :, :], 1.0 / TWO_PI, 0.25 * (1 - c), ALU.mult, ALU.add))
                step.settle()
                step(nc.vector.tensor_scalar(turns[:, :, :, :], turns[:, :, :, :], MAGIC, MAGIC, ALU.add, ALU.subtract))
                step.settle()
                for part in two_pi_parts():
                    step(nc.vector.scalar_tensor_tensor(out=angle[:, :, :, :], in0=turns[:, :, :, :], scalar=-part,
                                                        in1=angle[:, :, :, :], op0=ALU.mult, op1=ALU.add))
                    step.settle()
                step(nc.vector.tensor_scalar(angle[:, 0, :, :], angle[:, 0, :, :], math.pi / 2, None, ALU.add))
                step.settle()
                nc.vector.tensor_scalar(angle[:, :, :, :], angle[:, :, :, :], PI_BELOW, -PI_BELOW, ALU.min, ALU.max)\
                    .then_inc(angles_ready, 1)
                step(nc.vector.tensor_tensor(lam_in[:, 0, :], lam_in[:, 0, :], lam_in[:, 1, :], ALU.mult))
                dve.wait_ge(router_landed, 32)
                step(nc.vector.tensor_scalar(neg_sink[:, :], neg_sink[:, :], -1.0, None, ALU.mult))
                step(nc.vector.tensor_scalar(subln[:, :], subln[:, :], 1.0 - LAM_INIT, None, ALU.mult))
                step.settle()
                nc.vector.tensor_reduce(lam[:, 0:2], lam_in[:, 0, :].rearrange("p (c d) -> p c d", c=2), AX_X, ALU.add)\
                    .then_inc(lam_sums, 1)

            def first_layer():
                dve.wait_ge(hy_landed, 16 * 3)
                mlp_layer(0)

            split_first(0, 1)
            ffn(0, first=first_layer, between=small_tables)
            dve.wait_ge(lam_exp, 1)
            step(nc.vector.tensor_tensor(lam[:, 0:1], lam[:, 3:4], lam[:, 2:3], ALU.subtract))
            step.settle()
            step(nc.vector.tensor_scalar(lam[:, 0:1], lam[:, 0:1], -LAM_INIT, None, ALU.add))
            layer_norm("ffn_norm0", "ffn0", 2.0 * ALPHA, 4.0 * LN_EPS)

            mlp_layer(1)

            dve.wait_ge(sines_ready, 1)
            dve.wait_ge(mods_stored, 16)
            step(nc.vector.memset(q_lo[64:128, :, :], 0.0))
            nc.vector.memset(q_hi[0:64, :, :], 0.0).then_inc(padded, 1)
            at = plan["da_qkv"]
            for cb in range(6):
                for j in range(NT):
                    t = at.tiles + NT * cb + j
                    filled(dve, t)
                    c0 = (cb % 2) * 512
                    if cb < 4:
                        dst = (q_rows if cb < 2 else k_rows)[:, j, c0:c0 + 512].rearrange("p (h c d) -> p h c d", c=2, d=32)
                        src = work[:, t % 4, :].rearrange("p (h c d) -> p h c d", c=2, d=32)
                        tmp = rope_tmp.rearrange("p (h c d) -> p h c d", c=2, d=32)
                        sin = da_cs[:, 1, j:j + 1, :].broadcast_to([P, 8, 32])
                        cos = da_cs[:, 0, j:j + 1, :].broadcast_to([P, 8, 32])
                        if t > at.tiles:
                            step.settle()
                            read_out(dve, t - 1)
                        for c in range(2):
                            step(nc.vector.tensor_tensor(dst[:, :, c, :], src[:, :, c, :], cos, ALU.mult))
                            step(nc.vector.tensor_tensor(tmp[:, :, c, :], src[:, :, 1 - c, :], sin, ALU.mult))
                        step.settle()
                        step(nc.vector.tensor_tensor(dst[:, :, 0, :], dst[:, :, 0, :], tmp[:, :, 0, :], ALU.subtract))
                        nc.vector.tensor_tensor(dst[:, :, 1, :], dst[:, :, 1, :], tmp[:, :, 1, :], ALU.add)\
                            .then_inc(tile_read[t % 4], 1)
                    else:
                        nc.vector.tensor_copy(v_rows[:, j, c0:c0 + 512], work[:, t % 4, :]).then_inc(tile_read[t % 4], 1)
            attention("da_att", DA_H, da_begin, da_weigh, 2 * DA_DK, weighed=True)
            read_last = plan["da_att"].tiles + attention_order(NT * DA_H)["o", NT * DA_H - 1]
            read_out(dve, read_last)
            for j in range(NT):
                step(nc.vector.tensor_tensor(k_rows[:, j, :], q_rows[:, j, :], q_rows[:, j, :], ALU.mult))
            step.settle()
            step(nc.vector.tensor_reduce(head_sq[:, 0, :], k_rows.rearrange("p j (h d) -> p (j h) d", h=DA_H), AX_X, ALU.add))
            step.settle()
            nc.vector.tensor_scalar(head_sq[:, 0, :], head_sq[:, 0, :], 1.0 / (2 * DA_DK), LN_EPS, ALU.mult, ALU.add)\
                .then_inc(var_ready, 1)
            dve.wait_ge(root_ready, plan["da_cols"].norms + 1)
            newton_root(head_sq[:, 0, :], head_sq[:, 1, :], head_sq[:, 2, :], head_tmp[:, :])
            heads = q_rows.rearrange("p j (h d) -> p (j h) d", h=DA_H)
            step(nc.vector.tensor_tensor(heads, heads, head_sq[:, 2, :].unsqueeze(2).broadcast_to([P, NT * DA_H, 2 * DA_DK]), ALU.mult))
            step.settle()
            nc.vector.tensor_tensor(heads, heads, subln[:, :].unsqueeze(1).broadcast_to([P, NT * DA_H, 2 * DA_DK]), ALU.mult)\
                .then_inc(heads_normed, 1)
            layer_norm("mix_norm0", "da_out", ALPHA, LN_EPS)
            cross_attention(0)
            ffn(1)
            dve.wait_ge(mods_stored, 32)
            split_first(2, 1)
            layer_norm("ffn_norm1", "ffn1", 2.0 * ALPHA, 4.0 * LN_EPS)
            ffn(2)
            layer_norm("ffn_norm2", "ffn2", 2.0 * ALPHA, 4.0 * LN_EPS)

            pool_bias, pool_scale = param_row(), param_row()

            def pool_residual(j):
                use = plan["pool_out"].acc
                nc.vector.tensor_tensor(pool_y, acc[:, 2 * j:2 * j + 2, :].rearrange("p a c -> p (a c)"), pool_bias,
                                        ALU.add).then_inc(acc_read, 1)
                dve.wait_ge(acc_read, NT * use + j + 1)
                ins = nc.vector.tensor_tensor(pool_y, pool_y, pool_scale, ALU.mult)
                step(ins)
                step.settle()
                x = rows_x[:, j, :]
                ins = nc.vector.scalar_tensor_tensor(out=x, in0=x, scalar=ALPHA, in1=pool_y, op0=ALU.mult, op1=ALU.add)
                if j == NT - 1:
                    ins.then_inc(rows_used, 2)
                    returned[0] += 2
                    dve.wait_ge(rows_used, returned[0])
                else:
                    step(ins)
                    step.settle()

            layer_norm("mix_norm1", "pool_out", ALPHA, LN_EPS, prepare=pool_residual)
            cross_attention(1)
            ffn(3)
            layer_norm("ffn_norm3", "ffn3", 2.0 * ALPHA, 4.0 * LN_EPS)

            mod_norm("mod_norm0", [0])
            biases = [param_row(), param_row()]
            for c in range(D // HC):
                hyena_step(c, biases)
            dve.wait_ge(filters_done, D // HC)
            give_back(2)
            mod_norm("moe_norm0", [0, 1], mix=add_product(lambda s: f"hy_out{s}"), out_bias=True,
                     dst=lambda i: h_main[:, i, :] if i < NT else rows_h[:, i, :])
            experts(0)

            mod_norm("mod_norm1", [0, 1], mix=add_rows)
            step(nc.vector.memset(q_lo[64:128, :, :], 0.0))
            nc.vector.memset(q_hi[0:64, :, :], 0.0).then_inc(padded, 1)
            at = plan["sw_q"]
            tmp = sw_tmp

            def rotate(dst, src, tmp, j, shape):
                cos = const("sw_cos")[:, j * 32:(j + 1) * 32]
                sin = const("sw_sin")[:, j * 32:(j + 1) * 32]
                for _ in shape:
                    cos, sin = cos.unsqueeze(1), sin.unsqueeze(1)
                cos, sin = cos.broadcast_to([P, *shape, 32]), sin.broadcast_to([P, *shape, 32])
                for c in range(2):
                    step(nc.vector.tensor_tensor(dst(c), src(c), cos, ALU.mult))
                    step(nc.vector.tensor_tensor(tmp(c), src(1 - c), sin, ALU.mult))
                step.settle()
                step(nc.vector.tensor_tensor(dst(0), dst(0), tmp(0), ALU.subtract))
                return nc.vector.tensor_tensor(dst(1), dst(1), tmp(1), ALU.add)

            for cb in range(2):
                for j in range(NT):
                    t = at.tiles + NT * cb + j
                    filled(dve, t)
                    s4 = work[:, t % 4, :].rearrange("p (g r c d) -> p g r c d", g=2, r=4, c=2)
                    d4 = q_rows[:, j, cb * 512:cb * 512 + 512].rearrange("p (r g c d) -> p g r c d", g=2, r=4, c=2)
                    t4 = tmp.rearrange("p (g r c d) -> p g r c d", g=2, r=4, c=2)
                    rotate(lambda c: d4[:, :, :, c, :], lambda c: s4[:, :, :, c, :], lambda c: t4[:, :, :, c, :], j, (2, 4))                        .then_inc(tile_read[t % 4], 1)
                    read_out(dve, t)
                    step.settle()
            for q in range(2 * NT):
                t = plan["sw_kv"].tiles + q
                kt = (q + NT) % (2 * NT)
                filled(dve, t)
                step(nc.vector.tensor_copy(sw_v[:, kt, :], work[:, t % 4, 256:512]))
                if q < NT:
                    s3 = work[:, t % 4, 0:256].rearrange("p (g c d) -> p g c d", g=4, c=2)
                    d3 = sw_k_rows[:, kt, :].rearrange("p (g c d) -> p g c d", g=4, c=2)
                    t3 = tmp[:, 0:256].rearrange("p (g c d) -> p g c d", g=4, c=2)
                    ins = rotate(lambda c: d3[:, :, c, :], lambda c: s3[:, :, c, :], lambda c: t3[:, :, c, :], q, (4,))
                else:
                    ins = nc.vector.tensor_copy(sw_k_rows[:, kt, :], work[:, t % 4, 0:256])
                ins.then_inc(tile_read[t % 4], 1)
                read_out(dve, t)
                step.settle()

            def sw_begin(u, t, j, h):
                filled(dve, t)
                pk = peak[:, u % 4, 0:1]
                step(nc.vector.tensor_reduce(pk, work[:, t % 4, :], AX_X, ALU.max))
                step.settle()
                nc.vector.tensor_scalar(low[:, u % 4, 0:1], pk, -SW_HD ** -0.5, neg_sink[:, h:h + 1], ALU.mult,
                                        ALU.min).then_inc(low_ready, 1)

            def sw_weigh(u):
                sh = share[:, u % 4, 0:1]
                step(nc.vector.tensor_tensor(sh, mass[:, u % 4, 0:1], sink_exp[:, u % 4:u % 4 + 1], ALU.add))
                step.settle()
                step(nc.vector.reciprocal(sh, sh))

            attention("sw_att", SW_HQ, sw_begin, sw_weigh, SW_HD)
            mod_norm("moe_norm1", [0], mix=add_product(lambda s: "sw_out"))
            experts(1)
            mod_norm("last_norm", [0], mix=add_rows, last=True)

        @block.gpsimd
        def _(pool):
            rows = param_rows(io, mod_rows)
            r = 0

            def load_row():
                nonlocal r
                if r >= PR_RING:
                    pool.wait_ge(rows_used, r - PR_RING + 1)
                pool.dma_start(prow[:, r % PR_RING, :], rows[r].partition_broadcast(P)).then_inc(row_landed[r % PR_RING], 16)
                r += 1

            def load_ada_bias(i):
                pool.dma_start(mods[0:2, :], io["ada_b"][i].partition_broadcast(2)).then_inc(ada_bias_landed, 16)

            def store_mods(i):
                at = plan[f"ffn{i}"]
                _, t0, _ = ffn_events(range(FFN_HEAD), False)
                body, t1, _ = ffn_events(range(FFN_HEAD, FFN_HEAD + FFN_BODY), True)
                last = max(t for kind, _, t, _ in body if kind == "sum")
                read_out(pool, at.tiles + t0 + last, (FFN_LOOPS - 1) * (t1 // 4))
                pool.dma_start(mod_rows[i], mods[0:2, :]).then_inc(mods_stored, 16)

            pool.dma_start(hy_cols[:, :, :], io["hy_cols"].rearrange("p (k n) -> p k n", n=5)).then_inc(hy_landed, 16)
            pool.dma_start(hy_small[:, :], io["hy_small"]).then_inc(hy_landed, 16)
            pool.dma_start(hy_z_in, io["hy_z"]).then_inc(hy_landed, 16)
            pool.dma_start(router_w[:, :, :, :], io["router_cols"].rearrange("p (l k e) -> p l k e", l=DEPTH, k=KB)).then_inc(router_landed, 16)
            pool.dma_start(neg_sink[:, :], io["sw_sink"].partition_broadcast(P)).then_inc(router_landed, 16)
            pool.dma_start(pos_i[:, :], io["pos_cols"]).then_inc(small_landed, 16)
            for c, name in enumerate(("da_lam_q", "da_lam_k")):
                pool.dma_start(lam_in[:, c, :], io[name][0].rearrange("a d -> (a d)").partition_broadcast(P)).then_inc(small_landed, 16)
            pool.dma_start(subln[:, :], io["da_subln_g"][0].partition_broadcast(P)).then_inc(small_landed, 16)
            load_ada_bias(0)
            pool.dma_start(mask[:, :, :], io["masks"][0].rearrange("p (j k) -> p j k", j=NT)).then_inc(mask_landed, 16)
            def rows_until(n):
                while r < n:
                    load_row()

            def load_window(c):
                if c:
                    pool.wait_ge(filters_done, c)
                pool.dma_start(hy_window[:, :, :], io["hy_window"][:, :, c * HC:(c + 1) * HC]).then_inc(window_landed, 16)

            rows_until(PR_RING)
            store_mods(0)
            rows_until(8)
            pool.wait_ge(mods_stored, 16)
            pool.wait_ge(rows_ready, plan["xa_norm0"].rows + NT)
            load_ada_bias(1)
            pool.dma_start(mask[:, :, :], io["masks"][1].rearrange("p (j k) -> p j k", j=NT)).then_inc(mask_landed, 16)
            store_mods(1)
            pool.wait_ge(mods_stored, 32)
            before_ctx = 8 * DEPTH - 2
            rows_until(before_ctx + 3)
            at = plan["xa_att1"]
            read_out(pool, at.tiles + attention_order(NT * XA_H)["o", NT * XA_H - 1])
            pool.dma_start(rows_x[:, NT:2 * NT, :], io["ctx"][0].rearrange("(j p) d -> p j d", p=P)).then_inc(ctx_landed, 16)
            hyena_rows = before_ctx + 12
            rows_until(hyena_rows)
            pool.wait_ge(rows_ready, plan["mod_norm0"].rows + NT)
            for c in range(D // HC):
                load_window(c)
            rows_until(len(rows))


IN_NAMES = ["x", "mem", "ffn_w_in", "ffn_w_out", "ln_g", "ln_b", "da_w_qkv", "da_w_o", "da_lam_q", "da_lam_k",
            "da_subln_g", "pool_w", "pool_b", "pool_scale", "xa_wq", "xa_wkv", "xa_wo"]


def lay_out(inputs):
    a = {n: np.ascontiguousarray(inputs[n]) for n in IN_NAMES}
    a["ada_w"] = np.ascontiguousarray(inputs["ada_w_2"])
    a["ada_b"] = np.ascontiguousarray(inputs["ada_b_2"])
    cond = np.stack([np.asarray(inputs["c_2"])[0], np.asarray(inputs["c_ctx_2"])])
    a["cond_cols"] = np.ascontiguousarray(cond.reshape(2, KB, P).transpose(2, 1, 0).reshape(P, 2 * KB))
    a["pos_cols"] = np.ascontiguousarray(np.asarray(inputs["positions"]).reshape(NT, P).T)
    a["ctx"] = np.ascontiguousarray(inputs["ctx_2"])
    for name in ("norm1_w", "norm2_w"):
        a[name] = np.ascontiguousarray(inputs[name + "_2"])
    a["final_w"] = np.ascontiguousarray(inputs["final_norm_w_2"])
    a["hy_bias"] = np.ascontiguousarray(inputs["hy_filter_bias_2"])
    a["hy_b_out"] = np.ascontiguousarray(inputs["hy_b_out_2"])
    a["hy_w_in"] = np.ascontiguousarray(inputs["hy_w_in_2"])
    a["hy_w3"] = np.ascontiguousarray(inputs["hy_ffn_w3_2"])
    a["hy_w_out"] = np.ascontiguousarray(inputs["hy_w_out_2"])
    a["sw_w_in"] = np.ascontiguousarray(inputs["sw_w_in_2"])
    a["sw_w_out"] = np.ascontiguousarray(inputs["sw_w_out_2"])
    a["sw_sink"] = np.ascontiguousarray(inputs["sw_sink_2"])
    a["moe_gate"] = np.ascontiguousarray(inputs["moe_w_gate_2"])
    a["moe_up"] = np.ascontiguousarray(inputs["moe_w_up_2"])
    a["moe_down"] = np.ascontiguousarray(inputs["moe_w_down_2"])
    taps = np.asarray(inputs["hy_short_w_2"])
    cols = np.stack([np.asarray(inputs["hy_b_in_2"]), np.asarray(inputs["hy_short_b_2"]), *taps])
    a["hy_cols"] = np.ascontiguousarray(cols.reshape(5, 3 * KB, P).transpose(2, 1, 0).reshape(P, -1))
    small = np.zeros((HY_FFN, 2 * HY_FFN + 4), np.float32)
    small[:HY_EMB, :HY_FFN] = inputs["hy_ffn_w1_2"]
    small[:, HY_FFN:2 * HY_FFN] = inputs["hy_ffn_w2_2"]
    for n, col in enumerate((inputs["hy_ffn_b1_2"], inputs["hy_ffn_b2_2"], *np.asarray(inputs["hy_sin_freq_2"]))):
        small[:, 2 * HY_FFN + n] = col
    a["hy_small"] = small
    router = np.asarray(inputs["moe_router_2"])
    a["router_cols"] = np.ascontiguousarray(router.reshape(DEPTH, KB, P, E_N).transpose(2, 0, 1, 3).reshape(P, -1))
    a["hy_z"] = position_features()
    a["dft"] = dft_tables()
    a["hy_window"] = window_table()
    a["consts"] = CONSTS
    a["masks"] = mask_tables()
    a["pool_tables"] = pool_tables()
    return a


def kernel(**inputs):
    import concourse.bacc as bacc
    from concourse.bass_utils import run_bass_kernel_spmd

    nc = bacc.Bacc("TRN2", target_bir_lowering=False, num_devices=1)
    arrays, io = {}, {}
    for name, a in lay_out(inputs).items():
        arrays[f"in_{name}"] = a
        io[name] = nc.dram_tensor(f"in_{name}", a.shape, mybir.dt.from_np(a.dtype), kind="ExternalInput").ap()
    out = nc.dram_tensor("out", (1, S, D), F32, kind="ExternalOutput").ap()
    mod_rows = nc.dram_tensor("mod_rows", (DEPTH, 2, NMOD * D), F32, kind="Internal").ap()
    build_program(nc, io, out[0], mod_rows)
    r = run_bass_kernel_spmd(nc, [arrays], core_ids=[0])
    return r.results[0]["out"]
```
